# Optimizing a Trainium2 kernel written in Bass

```python
import jax, jax.numpy as jnp
from jax import lax
import numpy as np

D_MODEL = 1024
BATCH = 1
SEQ = 512
DEPTH = 1

HEAD_DIM = 64
ATT_Q_HEADS = 8
ATT_KV_HEADS = 2
ATT_GROUP = ATT_Q_HEADS // ATT_KV_HEADS
WINDOW = 128
ROPE_THETA = 10000.0
SGU_HEADS = 8
SGU_CHUNK = 128
ATT_WIDTH = ATT_Q_HEADS * HEAD_DIM
KV_WIDTH = ATT_KV_HEADS * HEAD_DIM
SGU_WIDTH = SGU_HEADS * HEAD_DIM
MIX_WIDTH = ATT_WIDTH + SGU_WIDTH
IN_COLS = ATT_WIDTH + 2 * KV_WIDTH + 2 * SGU_WIDTH
SPLITS = (ATT_WIDTH, ATT_WIDTH + KV_WIDTH, ATT_WIDTH + 2 * KV_WIDTH,
          ATT_WIDTH + 2 * KV_WIDTH + SGU_WIDTH)
PEER_HEADS = 8
PEER_N_KEYS = 128
PEER_N_EXPERTS = PEER_N_KEYS * PEER_N_KEYS
PEER_TOPK = 16
PEER_QDIM = 256
PEER_TOKEN_BLOCK = 128
EPS = 1e-6

kernel_name = "hybrid_sgu_swa_sink_peer_block"

def rms_norm(x, g):
    xf = x.astype(jnp.float32)
    y = xf * lax.rsqrt(jnp.mean(xf * xf, axis=-1, keepdims=True) + EPS)
    return (y * g.astype(jnp.float32)).astype(x.dtype)

def layer_norm(x, g, b):
    xf = x.astype(jnp.float32)
    mu = jnp.mean(xf, axis=-1, keepdims=True)
    var = jnp.mean(jnp.square(xf - mu), axis=-1, keepdims=True)
    y = (xf - mu) * lax.rsqrt(var + EPS) * g.astype(jnp.float32) + b.astype(jnp.float32)
    return y.astype(x.dtype)

def rope(x, pos):
    half = HEAD_DIM // 2
    inv = ROPE_THETA ** (-jnp.arange(half, dtype=jnp.float32) / half)
    ang = pos.astype(jnp.float32)[:, None] * inv[None, :]
    cos = jnp.cos(ang)[None, :, None, :]
    sin = jnp.sin(ang)[None, :, None, :]
    xf = x.astype(jnp.float32)
    x1, x2 = xf[..., :half], xf[..., half:]
    out = jnp.concatenate([x1 * cos - x2 * sin, x2 * cos + x1 * sin], axis=-1)
    return out.astype(x.dtype)

def sliding_window_attention(q, k, v, sinks):
    B, S = q.shape[0], q.shape[1]
    nb = S // WINDOW
    qb = q.reshape(B, nb, WINDOW, ATT_KV_HEADS, ATT_GROUP, HEAD_DIM)
    kb = k.reshape(B, nb, WINDOW, ATT_KV_HEADS, HEAD_DIM)
    vb = v.reshape(B, nb, WINDOW, ATT_KV_HEADS, HEAD_DIM)
    pad = ((0, 0), (1, 0), (0, 0), (0, 0), (0, 0))
    kcat = jnp.concatenate([jnp.pad(kb[:, :-1], pad), kb], axis=2)
    vcat = jnp.concatenate([jnp.pad(vb[:, :-1], pad), vb], axis=2)
    s = jnp.einsum('bnqhgd,bnkhd->bnhgqk', qb, kcat,
                   preferred_element_type=jnp.float32) * (HEAD_DIM ** -0.5)
    blk = jnp.arange(nb)[:, None, None] * WINDOW
    qpos = blk + jnp.arange(WINDOW)[None, :, None]
    kpos = blk - WINDOW + jnp.arange(2 * WINDOW)[None, None, :]
    diff = qpos - kpos
    valid = (diff >= 0) & (diff < WINDOW) & (kpos >= 0)
    s = jnp.where(valid[None, :, None, None, :, :], s, -jnp.inf)
    sink = sinks.astype(jnp.float32).reshape(ATT_KV_HEADS, ATT_GROUP)[None, None, :, :, None, None]
    m = jnp.maximum(jnp.max(s, axis=-1, keepdims=True), sink)
    p = jnp.exp(s - m)
    p = p / (jnp.sum(p, axis=-1, keepdims=True) + jnp.exp(sink - m))
    o = jnp.einsum('bnhgqk,bnkhd->bnqhgd', p.astype(v.dtype), vcat)
    return o.reshape(B, S, ATT_WIDTH).astype(q.dtype)

def chunked_spatial_gating(u, v, w_s, b_s, ln_g, ln_b):
    B, S = u.shape[0], u.shape[1]
    nc = S // SGU_CHUNK
    vn = layer_norm(v, ln_g, ln_b)
    vc = vn.reshape(B, nc, SGU_CHUNK, SGU_HEADS, HEAD_DIM)
    causal = jnp.tril(jnp.ones((SGU_CHUNK, SGU_CHUNK), dtype=bool))
    w = jnp.where(causal[None], w_s, 0).astype(v.dtype)
    mixed = jnp.einsum('hts,bcshd->bcthd', w, vc) + b_s.T.astype(v.dtype)[None, None, :, :, None]
    return (u * mixed.reshape(u.shape)).reshape(B, S, SGU_WIDTH)

def hybrid_mixer(h, w_in, w_s, b_s, sgu_ln_g, sgu_ln_b, sinks, g_att_out, g_sgu_out, w_out):
    B, S, _ = h.shape
    proj = h @ w_in
    q, k, v, u_s, v_s = jnp.split(proj, SPLITS, axis=-1)
    pos = jnp.arange(S)
    q = rope(q.reshape(B, S, ATT_Q_HEADS, HEAD_DIM), pos)
    k = rope(k.reshape(B, S, ATT_KV_HEADS, HEAD_DIM), pos)
    v = v.reshape(B, S, ATT_KV_HEADS, HEAD_DIM)
    att = sliding_window_attention(q, k, v, sinks)
    u_s = jax.nn.gelu(u_s, approximate=False).reshape(B, S, SGU_HEADS, HEAD_DIM)
    v_s = jax.nn.gelu(v_s, approximate=False).reshape(B, S, SGU_HEADS, HEAD_DIM)
    sgu = chunked_spatial_gating(u_s, v_s, w_s, b_s, sgu_ln_g, sgu_ln_b)
    y = jnp.concatenate([rms_norm(att, g_att_out), rms_norm(sgu, g_sgu_out)], axis=-1)
    return y @ w_out

def peer_ffn(h, w_query, sub_keys, expert_down, expert_up):
    B, S, D = h.shape
    T = B * S
    ht = h.reshape(T, D)
    q = (ht @ w_query).reshape(T, PEER_HEADS, 2, PEER_QDIM // 2)
    sc = jnp.einsum('thpd,hpnd->thpn', q, sub_keys, preferred_element_type=jnp.float32)
    sub_s, sub_i = lax.top_k(sc, PEER_TOPK)
    cand_s = sub_s[:, :, 0, :, None] + sub_s[:, :, 1, None, :]
    cand_i = sub_i[:, :, 0, :, None] * PEER_N_KEYS + sub_i[:, :, 1, None, :]
    top_s, top_j = lax.top_k(cand_s.reshape(T, PEER_HEADS, PEER_TOPK * PEER_TOPK), PEER_TOPK)
    experts = jnp.take_along_axis(cand_i.reshape(T, PEER_HEADS, PEER_TOPK * PEER_TOPK), top_j, axis=-1)
    gates = jax.nn.softmax(top_s, axis=-1)
    nblk = T // PEER_TOKEN_BLOCK
    HK = PEER_HEADS * PEER_TOPK

    def block(args):
        xb, eb, gb = args
        u = jnp.take(expert_down, eb, axis=0)
        a = jax.nn.gelu(jnp.einsum('tkd,td->tk', u, xb), approximate=False)
        w = jnp.take(expert_up, eb, axis=0)
        return jnp.einsum('tk,tkd->td', gb * a, w)

    out = lax.map(block, (ht.reshape(nblk, PEER_TOKEN_BLOCK, D),
                          experts.reshape(nblk, PEER_TOKEN_BLOCK, HK),
                          gates.reshape(nblk, PEER_TOKEN_BLOCK, HK).astype(h.dtype)))
    return out.reshape(B, S, D)

def setup_inputs(seed: int = 0) -> dict:
    key = jax.random.key(seed)
    ks = jax.random.split(key, 24)
    f32 = jnp.float32
    L, D = DEPTH, D_MODEL
    nrm = lambda k, shape, s: jax.random.normal(k, shape, f32) * s
    gain = lambda k, shape: 1.0 + 0.05 * jax.random.normal(k, shape, f32)
    return {
        "x": jax.random.normal(ks[0], (BATCH, SEQ, D), f32),
        "c": jax.random.normal(ks[1], (BATCH, D), f32),
        "w_ada": nrm(ks[2], (L, D, 6 * D), 0.5 * D ** -0.5),
        "b_ada": nrm(ks[3], (L, 6 * D), 0.02),
        "g_pre_mix": gain(ks[4], (L, D)),
        "g_post_mix": gain(ks[5], (L, D)),
        "g_pre_ffn": gain(ks[6], (L, D)),
        "g_post_ffn": gain(ks[7], (L, D)),
        "w_in": nrm(ks[8], (L, D, IN_COLS), D ** -0.5),
        "w_s": nrm(ks[9], (L, SGU_HEADS, SGU_CHUNK, SGU_CHUNK), SGU_CHUNK ** -0.5),
        "b_s": 1.0 + nrm(ks[10], (L, SGU_HEADS, SGU_CHUNK), 0.02),
        "sgu_ln_g": gain(ks[11], (L, SGU_HEADS, HEAD_DIM)),
        "sgu_ln_b": nrm(ks[12], (L, SGU_HEADS, HEAD_DIM), 0.02),
        "sinks": nrm(ks[13], (L, ATT_Q_HEADS), 0.5),
        "g_att_out": gain(ks[14], (L, ATT_WIDTH)),
        "g_sgu_out": gain(ks[15], (L, SGU_WIDTH)),
        "w_out": nrm(ks[16], (L, MIX_WIDTH, D), MIX_WIDTH ** -0.5),
        "w_query": nrm(ks[17], (L, D, PEER_HEADS * PEER_QDIM), D ** -0.5),
        "sub_keys": nrm(ks[18], (L, PEER_HEADS, 2, PEER_N_KEYS, PEER_QDIM // 2), (PEER_QDIM // 2) ** -0.5),
        "expert_down": nrm(ks[19], (L, PEER_N_EXPERTS, D), D ** -0.5),
        "expert_up": nrm(ks[20], (L, PEER_N_EXPERTS, D), PEER_HEADS ** -0.5),
    }

def reference(x, c, w_ada, b_ada, g_pre_mix, g_post_mix, g_pre_ffn, g_post_ffn,
              w_in, w_s, b_s, sgu_ln_g, sgu_ln_b, sinks, g_att_out, g_sgu_out, w_out,
              w_query, sub_keys, expert_down, expert_up):
    c_act = jax.nn.silu(c)
    for l in range(DEPTH):
        mod = c_act @ w_ada[l] + b_ada[l]
        sh1, sc1, gt1, sh2, sc2, gt2 = [m[:, None, :] for m in jnp.split(mod, 6, axis=-1)]
        h = rms_norm(x, g_pre_mix[l]) * (1.0 + sc1) + sh1
        y = hybrid_mixer(h, w_in[l], w_s[l], b_s[l], sgu_ln_g[l], sgu_ln_b[l], sinks[l],
                         g_att_out[l], g_sgu_out[l], w_out[l])
        x = x + gt1 * rms_norm(y, g_post_mix[l])
        h = rms_norm(x, g_pre_ffn[l]) * (1.0 + sc2) + sh2
        y = peer_ffn(h, w_query[l], sub_keys[l], expert_down[l], expert_up[l])
        x = x + gt2 * rms_norm(y, g_post_ffn[l])
    return x


_drawn_inputs = setup_inputs


def setup_inputs(seed=0):
    import zlib

    import numpy as np

    out = dict(_drawn_inputs(seed))
    spreads = {}
    factors = {'g_post_ffn': 4.131, 'b_s': 3.058, 'sgu_ln_b': 3.895, 'sinks': 7.413}
    for name, (base, spread) in spreads.items():
        noise = np.random.default_rng([zlib.crc32(name.encode()), seed]).standard_normal(out[name].shape)
        drawn = base * np.exp(spread * noise) if base else spread * noise
        out[name] = __import__('jax').numpy.asarray(drawn.astype(out[name].dtype))
    for name, factor in factors.items():
        out[name] = (out[name] * factor).astype(out[name].dtype)
    return out
```

```python
from contextlib import ExitStack

import numpy as np

import concourse.bass as bass
from concourse import mybir
from concourse.alu_op_type import AluOpType as ALU

F32 = mybir.dt.float32
BF16 = mybir.dt.bfloat16
U32 = mybir.dt.uint32
ACT = mybir.ActivationFunctionType
AX_X = mybir.AxisListType.X

P = 128
D, SEQ = 1024, 512
NB = SEQ // P
KD = D // P
HD = 64
QH, KVH = 8, 2
GROUP = QH // KVH
SGU_H = 8
ATT_W, KV_W, SGU_W = QH * HD, KVH * HD, SGU_H * HD
IN_COLS = ATT_W + 2 * KV_W + 2 * SGU_W
PROJ = [(0, ATT_W), (ATT_W, 2 * KV_W), (ATT_W + 2 * KV_W, SGU_W), (ATT_W + 2 * KV_W + SGU_W, SGU_W)]
PH, TOPK, NKEY = 8, 16, 128
HP = PH * 2
UNITS = NB * PH
EPS = 1e-6
MASKED = -1e30
REMOVED = -3e38
RING = 8
WRING = 5
ADA_CHUNKS = 6 * KD
SH1, SC1, GT1, SH2, SC2, GT2 = range(6)
COL_C, COL_BADA, COL_G1, COL_G2, COL_GOUT, N_COLS = 0, 8, 56, 64, 72, 80


def steps():
    out = [("N", 0), ("ADA_COL", SH1), ("ADA_COL", SC1)]
    for s in range(NB + 2):
        if s < NB:
            out.append(("T", s))
        if 1 <= s <= NB:
            out.append(("S1", s - 1))
        if s + 1 < NB:
            out.append(("N", s + 1))
        if 1 <= s <= NB:
            out.append(("LN", s - 1))
        if s < NB:
            out.append(("P", s))
        if s == 0:
            out.append(("ADA_ROW", GT1))
        if s == 1:
            out += [("ADA_COL", SH2), ("ADA_COL", SC2)]
        if 1 <= s <= NB:
            out += [("S2", s - 1), ("G", s - 1)]
        if s >= 2:
            out.append(("W", s - 2))
        if 1 <= s <= NB:
            out.append(("O", s - 1))
        if s >= 2:
            out.append(("F", s - 2))
    out.append(("ADA_ROW", GT2))
    return out


def bank_turns(names):
    return {name: (n % 2, n // 2) for n, name in enumerate(names)}


def matmul_uses():
    out = []
    for stage, b in steps():
        if stage == "ADA_COL":
            out.append(("ada", b))
        elif stage == "ADA_ROW":
            out += [("ada", b, half) for half in range(2)]
        elif stage == "P":
            out += [("proj", b, c) for c in range(len(PROJ))]
        elif stage == "W":
            out += [("y", b, half) for half in range(2)]
    for half in range(2):
        out += [("query", half, hp) for hp in range(HP)]
    return bank_turns(out)


def transpose_uses():
    out = []
    for stage, b in steps():
        if stage == "T":
            out += [("x", b, half) for half in range(2)]
        elif stage == "S1":
            out += [("q", b), ("k", b)]
        elif stage == "O":
            out += [("prob", b, g, j) for g in range(KVH) for j in range(2)]
        elif stage == "W":
            out += [("mix", b, half) for half in range(2)]
        elif stage == "F":
            out += [("ffn", b, half) for half in range(2)]
    out += [("h2", b, half) for b in range(NB) for half in range(2)]
    return bank_turns(out)


def hybrid_block(nc, x, cols, rows, w_ada, w_in, w_s, b_s, sinks, w_out, w_query, keys, down, up,
                 cos_tab, sin_tab, masks, ident_in, iota_in, out):
    MM, TR = matmul_uses(), transpose_uses()
    with ExitStack() as ctx:
        def sb(name, shape, dt=F32):
            return ctx.enter_context(nc.sbuf_tensor(name, shape, dt))

        def psum(name, shape):
            return ctx.enter_context(nc.psum_tensor(name, shape, F32))

        def sem(name):
            return ctx.enter_context(nc.semaphore(name))

        W = sb("W", [P, KD * IN_COLS + KD * D])
        win_sb = W[:, 0:KD * IN_COLS].rearrange("p (k n) -> p k n", k=KD)
        wout_sb = W[:, KD * IN_COLS:KD * (IN_COLS + D)].rearrange("p (k n) -> p k n", k=KD)
        down_ring = W[:, 0:RING * D].rearrange("p (r n) -> p r n", r=RING)
        up_ring = W[:, RING * D:2 * RING * D].rearrange("p (r n) -> p r n", r=RING)
        h2 = W[:, 16 * D:18 * D].rearrange("p (r n) -> p r n", r=2)
        acc = W[:, 18 * D:20 * D].rearrange("p (r n) -> p r n", r=2)
        gain2 = W[:, 20 * D:21 * D]
        dot_junk = W[:, 21 * D:22 * D].bitcast(BF16).rearrange("p (r n) -> p r n", r=2)

        wring = sb("wring", [P, WRING, KD, P])
        x_sb = sb("x_sb", [P, NB, D])
        h2T = sb("h2T", [P, KD, SEQ])
        c_rows = h2T[:, :, 0:P]
        c_rows2 = W[:, 21 * D:22 * D].rearrange("p (k n) -> p k n", k=KD)

        WORK = 15488
        work = sb("work", [P, WORK])
        at = [0]

        def take(n):
            at[0] += n
            assert at[0] <= WORK, at[0]
            return work[:, at[0] - n:at[0]]

        xn = take(D)
        actT = take(D).rearrange("p (k n) -> p k n", k=KD)
        yn = take(D)
        rope_tmp = take(2 * ATT_W).rearrange("p (a n) -> p a n", a=2)
        probs = [take(GROUP * 2 * P), rope_tmp.rearrange("p a n -> p (a n)")]
        q_rot = take(ATT_W)
        k_dup = take(2 * KV_W).rearrange("p (g r d) -> p g r d", g=KVH, r=2)
        v_all = take(NB * KV_W).rearrange("p (b n) -> p b n", b=NB)
        kT = take(KVH * NB * P).rearrange("p (g n) -> p g n", g=KVH)
        u_sb = take(2 * SGU_W).rearrange("p (r n) -> p r n", r=2)
        vg = take(SGU_W)
        ln_both = take(2 * SGU_W)
        ln_d, vn = ln_both[:, 0:SGU_W], ln_both[:, SGU_W:2 * SGU_W]
        xn2 = ln_both
        qT = take(ATT_W).rearrange("p (a n) -> p a n", a=GROUP)
        pT = take(2 * GROUP * P).rearrange("p (j h n) -> p j h n", j=2, h=GROUP)
        wsT = take(SGU_H * P).rearrange("p (h n) -> p h n", h=SGU_H)
        gain1 = take(D)
        ln_rows = take(2 * SGU_W).rearrange("p (a n) -> p a n", a=2)
        causal = take(P)
        mask_sb = take(2 * P)
        junk = take(D // 2).bitcast(BF16)

        at[0] = 0
        scores = take(UNITS * 2 * P)
        qhT = take(2 * 4 * 2 * P).rearrange("p (r h n) -> p r h n", r=2, h=4)
        keys_sb = take(HP * P).rearrange("p (h n) -> p h n", h=HP)
        key_s = take(2 * P).rearrange("p (a n) -> p a n", a=2)
        key_s2 = take(2 * P).rearrange("p (a n) -> p a n", a=2)
        cand = take(TOPK * TOPK)
        cand2 = take(TOPK * TOPK)
        onehot = take(2 * TOPK * TOPK).rearrange("p (a j) -> p a j", j=TOPK)
        index = take(UNITS * TOPK).bitcast(U32)
        gates = take(UNITS * TOPK)

        ident = sb("ident", [P, P])
        rope_cs = sb("rope_cs", [P, 2, NB, HD])
        col = sb("col", [P, N_COLS])
        mod = sb("mod", [P, 4 * KD])
        bs_sb = sb("bs_sb", [P, SGU_H])
        sink_sb = sb("sink_sb", [P, QH])
        c_act = sb("c_act", [P, KD])
        halves = sb("halves", [P, 4])
        eps_sb = sb("eps_sb", [P, 1])
        st = sb("st", [P, 16])
        stat = sb("stat", [P, 4, SGU_H])
        soft = sb("soft", [P, KVH, 6, GROUP])
        iota = sb("iota", [P, TOPK])
        top_v = sb("top_v", [P, 2, TOPK])
        top_i = sb("top_i", [P, 2, TOPK], U32)
        top_f = sb("top_f", [P, 2, TOPK])
        best_v = sb("best_v", [P, TOPK])
        best_j = sb("best_j", [P, TOPK], U32)
        pos_u = sb("pos_u", [P, 2, TOPK], U32)
        pos_f = sb("pos_f", [P, 2, TOPK])
        sel = sb("sel", [P, 2, TOPK])
        expert_f = sb("expert_f", [P, TOPK])
        gate_e = sb("gate_e", [P, TOPK])
        gate_s = sb("gate_s", [P, 4])
        staged = sb("staged", [P, 2, TOPK], U32)
        dots = sb("dots", [P, 2, RING])
        gelus = sb("gelus", [P, 2, RING])
        coef = sb("coef", [P, 2, RING])
        fin = sb("fin", [P, 4])

        mm = psum("mm", [P, 2, 512])
        tr = psum("tr", [P, 2, 512])
        sc = psum("sc", [P, 2, 512])
        att_ps = psum("att_ps", [P, 512])
        sgu_ps = psum("sgu_ps", [P, 512])

        consts_in = sem("consts_in")
        x_in = sem("x_in")
        win_in = [sem(f"win_in{c}") for c in range(len(PROJ))]
        wout_in = sem("wout_in")
        chunk_in = [sem(f"chunk_in{r}") for r in range(WRING)]
        chunk_used = sem("chunk_used")
        gain2_in = sem("gain2_in")
        keys_in = sem("keys_in")
        mm_full = [sem(f"mm_full{i}") for i in range(2)]
        mm_free = [sem(f"mm_free{i}") for i in range(2)]
        tr_full = [sem(f"tr_full{i}") for i in range(2)]
        tr_free = [sem(f"tr_free{i}") for i in range(2)]
        c_rows_ready = sem("c_rows_ready")
        c_ready = sem("c_ready")
        mod_ready = sem("mod_ready")
        x_squared = sem("x_squared")
        x_ms = sem("x_ms")
        x_rs = sem("x_rs")
        xn_ready = sem("xn_ready")
        actT_dve = sem("actT_dve")
        actT_act = sem("actT_act")
        rope_ready = sem("rope_ready")
        vg_ready = sem("vg_ready")
        vg_used = sem("vg_used")
        var_ready = sem("var_ready")
        var_rs = sem("var_rs")
        vn_ready = sem("vn_ready")
        wsT_ready = sem("wsT_ready")
        qT_ready = sem("qT_ready")
        kT_ready = sem("kT_ready")
        sc_full = sem("sc_full")
        sc_free = sem("sc_free")
        bias_ready = sem("bias_ready")
        exp_ready = sem("exp_ready")
        pT_act = sem("pT_act")
        pT_dve = sem("pT_dve")
        att_full = sem("att_full")
        sgu_full = sem("sgu_full")
        att_free = sem("att_free")
        sgu_free = sem("sgu_free")
        att_ready = sem("att_ready")
        u_ready = sem("u_ready")
        sgu_ready = sem("sgu_ready")
        mix_squared = sem("mix_squared")
        mix_ms = sem("mix_ms")
        mix_rs = sem("mix_rs")
        mix_ready = sem("mix_ready")
        y_squared = sem("y_squared")
        y_ms = sem("y_ms")
        y_rs = sem("y_rs")
        x1_ready = sem("x1_ready")
        x1_squared = sem("x1_squared")
        x1_ms = sem("x1_ms")
        x1_rs = sem("x1_rs")
        xn2_ready = sem("xn2_ready")
        h2T_dve = sem("h2T_dve")
        h2T_act = sem("h2T_act")
        mixer_pe = sem("mixer_pe")
        mixer_dve = sem("mixer_dve")
        mixer_act = sem("mixer_act")
        qhT_ready = sem("qhT_ready")
        qs_full = sem("qs_full")
        qs_free = sem("qs_free")
        scores_ready = sem("scores_ready")
        h2_ready = sem("h2_ready")
        h2_used = sem("h2_used")
        down_in = [sem(f"down_in{r}") for r in range(RING)]
        up_in = [sem(f"up_in{r}") for r in range(RING)]
        down_free = sem("down_free")
        up_free = sem("up_free")
        index_ready = sem("index_ready")
        staged_ready = sem("staged_ready")
        issue_ok = sem("issue_ok")
        best_ready = sem("best_ready")
        gate_exp = sem("gate_exp")
        gelu_ready = sem("gelu_ready")
        y2_ready = sem("y2_ready")
        y2_rms = sem("y2_rms")
        out_ready = sem("out_ready")
        out_done = sem("out_done")
        dve_chain = sem("dve_chain")
        act_chain = sem("act_chain")
        pool_chain = sem("pool_chain")

        def linker(eng, chain):
            n = [0]

            def link(ins):
                n[0] += 1
                ins.then_inc(chain, 1)
                eng.wait_ge(chain, n[0])

            return link

        N_CONSTS = 13
        block = ctx.enter_context(nc.Block())

        @block.sync
        def _(sp):
            def chunk(n, source):
                if n >= WRING:
                    sp.wait_ge(chunk_used, n - WRING + 1)
                sp.dma_start(wring[:, n % WRING], source).then_inc(chunk_in[n % WRING], 16)

            sp.dma_start(col[:], cols).then_inc(consts_in, 16)
            sp.dma_start(x_sb[:, 0], x[0:P, :]).then_inc(x_in, 16)
            sp.dma_start(ident[:], ident_in).then_inc(consts_in, 16)
            sp.dma_start(rope_cs[:, 0], cos_tab).then_inc(consts_in, 16)
            sp.dma_start(rope_cs[:, 1], sin_tab).then_inc(consts_in, 16)
            sp.dma_start(causal, masks[:, 0:P]).then_inc(consts_in, 16)
            sp.dma_start(mask_sb, masks[:, P:3 * P]).then_inc(consts_in, 16)
            sp.dma_start(iota[:], iota_in).then_inc(consts_in, 16)
            sp.dma_start(bs_sb[:], b_s).then_inc(consts_in, 16)
            sp.dma_start(sink_sb[:], sinks.partition_broadcast(P)).then_inc(consts_in, 16)
            sp.dma_start(wsT, w_s).then_inc(consts_in, 16)
            sp.dma_start(ln_rows, rows[4 * D:4 * D + 2 * SGU_W].partition_broadcast(P)
                         .rearrange("p (a n) -> p a n", a=2)).then_inc(consts_in, 16)
            sp.dma_start(gain1, rows[0:D].partition_broadcast(P)).then_inc(consts_in, 16)
            sp.dma_start(yn, rows[D:2 * D].partition_broadcast(P)).then_inc(consts_in, 16)
            for n in range(2 * KD):
                chunk(n, w_ada[n])
            for c, (first, n) in enumerate(PROJ):
                sp.dma_start(win_sb[:, :, first:first + n],
                             w_in.rearrange("(k p) n -> p k n", p=P)[:, :, first:first + n]
                             ).then_inc(win_in[c], 16)
            sp.wait_ge(x_in, 16)
            for b in range(1, NB):
                sp.dma_start(x_sb[:, b], x[b * P:(b + 1) * P, :]).then_inc(x_in, 16)
                sp.wait_ge(x_in, 16 * (b + 1))
            sp.dma_start(wout_sb, w_out.rearrange("(k p) n -> p k n", p=P)).then_inc(wout_in, 16)
            for n in range(2 * KD, ADA_CHUNKS):
                chunk(n, w_ada[n])
            sp.wait_ge(mixer_pe, 1)
            sp.wait_ge(mixer_dve, 1)
            sp.wait_ge(mixer_act, 1)
            sp.dma_start(gain2, rows[2 * D:3 * D].partition_broadcast(P)).then_inc(gain2_in, 16)
            sp.dma_start(acc[:, 0], rows[3 * D:4 * D].partition_broadcast(P)).then_inc(gain2_in, 16)
            sp.dma_start(keys_sb, keys).then_inc(keys_in, 16)
            for half in range(2):
                for hp in range(HP):
                    chunk(ADA_CHUNKS + half * HP + hp, w_query[hp])
            for b in range(NB):
                sp.wait_ge(out_ready, b + 1)
                sp.dma_start(out[b * P:(b + 1) * P, :], x_sb[:, b]).then_inc(out_done, 16)
            sp.wait_ge(out_done, 16 * NB)

        @block.gpsimd
        def _(pool):
            link = linker(pool, pool_chain)
            link(nc.gpsimd.memset(halves[:], -0.5))

            def rsqrt(ready, done, n, at_, width=1):
                pool.wait_ge(ready, n)
                nc.gpsimd.tensor_tensor(at_, at_, halves[:, 0:1].to_broadcast([P, width]),
                                        ALU.pow).then_inc(done, 1)

            for stage, b in steps():
                if stage == "N":
                    rsqrt(x_ms, x_rs, b + 1, st[:, 0:1])
                elif stage == "LN":
                    rsqrt(var_ready, var_rs, b + 1, stat[:, 3], SGU_H)
                elif stage == "O":
                    rsqrt(mix_ms, mix_rs, b + 1, st[:, 2:4], 2)
                elif stage == "W":
                    rsqrt(y_ms, y_rs, b + 1, st[:, 6:7])
                elif stage == "F":
                    rsqrt(x1_ms, x1_rs, b + 1, st[:, 8:9])
            pool.wait_ge(mixer_pe, 1)

            def gather(table, ring, free, arrived, r, side, first):
                pool.wait_ge(free, first + r + 1)
                pool.sem_inc(issue_ok, 1)
                nc.gpsimd.indirect_dma_start(
                    ring[:, r % RING], None, table,
                    bass.IndirectOffsetOnAxis(ap=staged[:, side, r:r + 1], axis=0),
                ).then_inc(arrived[r % RING], 16)

            with pool.Fori(0, UNITS // 2, 1) as i:
                for side in range(2):
                    unit = i * 2 + side
                    pool.wait_ge(index_ready, unit + 1)
                    pool.wait_ge(up_free, unit * TOPK + 1)
                    nc.gpsimd.tensor_copy(staged[:, side], index[:, bass.ds(unit * TOPK, TOPK)]
                                          ).then_inc(staged_ready, 1)
                    pool.wait_ge(staged_ready, unit + 1)
                    pool.sem_inc(issue_ok, 1)
                    for part in range(TOPK // RING):
                        for r in range(part * RING, (part + 1) * RING):
                            gather(down, down_ring, down_free, down_in, r, side, unit * TOPK)
                        for r in range(part * RING, (part + 1) * RING):
                            gather(up, up_ring, up_free, up_in, r, side, unit * TOPK)

        @block.scalar
        def _(act):
            link = linker(act, act_chain)
            act.wait_ge(consts_in, 16 * N_CONSTS)
            nc.scalar.activation(c_act[:], col[:, COL_C:COL_C + KD], ACT.Silu).then_inc(c_ready, 1)

            def scale_shift(key, out_of, gain_of, shift_of, done):
                bank, turn = TR[key]
                act.wait_ge(tr_full[bank], turn + 1)
                for j in range(4):
                    k = 4 * key[-1] + j
                    shift = shift_of(k) if shift_of else 0.0
                    last = nc.scalar.activation(out_of(k), tr[:, bank, j * P:(j + 1) * P],
                                                ACT.Identity if shift_of else ACT.Copy,
                                                bias=shift, scale=gain_of(k))
                link(last)
                act.sem_inc(tr_free[bank], 1)
                act.sem_inc(done, 1)

            for stage, b in steps():
                if stage == "N":
                    act.wait_ge(x_in, 16 * (b + 1))
                    if b:
                        bank, turn = TR["x", b - 1, 1]
                        act.wait_ge(tr_full[bank], turn + 1)
                        act.wait_ge(x_ms, b)
                    nc.scalar.activation(junk, x_sb[:, b], ACT.Square, accum_out=st[:, 1:2]).then_inc(x_squared, 1)
                    act.wait_ge(x_rs, b + 1)
                    nc.scalar.activation(xn, x_sb[:, b], ACT.Copy, scale=st[:, 0:1]).then_inc(xn_ready, 1)
                elif stage == "T":
                    act.wait_ge(mod_ready, 2)
                    scale_shift(("x", b, 1), lambda k: actT[:, k],
                                lambda k: mod[:, KD + k:KD + k + 1], lambda k: mod[:, k:k + 1], actT_act)
                elif stage == "S1":
                    bank, turn = TR["k", b]
                    act.wait_ge(tr_full[bank], turn + 1)
                    link(nc.scalar.activation(kT[:, :, b * P:(b + 1) * P],
                                              tr[:, bank, 0:2 * P].rearrange("p (g n) -> p g n", g=2), ACT.Copy))
                    act.sem_inc(tr_free[bank], 1)
                    act.sem_inc(kT_ready, 1)
                elif stage == "P":
                    bank, turn = MM["proj", b, 2]
                    act.wait_ge(mm_full[bank], turn + 1)
                    if b >= 2:
                        act.wait_ge(mix_ready, b - 1)
                    link(nc.scalar.activation(u_sb[:, b % 2], mm[:, bank, :], ACT.Gelu))
                    act.sem_inc(mm_free[bank], 1)
                    act.sem_inc(u_ready, 1)
                    bank, turn = MM["proj", b, 3]
                    act.wait_ge(mm_full[bank], turn + 1)
                    if b:
                        act.wait_ge(vg_used, b)
                    link(nc.scalar.activation(vg, mm[:, bank, :], ACT.Gelu))
                    act.sem_inc(mm_free[bank], 1)
                    act.sem_inc(vg_ready, 1)
                elif stage == "S2":
                    for g in range(KVH):
                        act.wait_ge(bias_ready, 2 * b + g + 1)
                        for h in range(GROUP):
                            s = probs[g][:, h * 2 * P:(h + 1) * 2 * P]
                            nc.scalar.activation(s, s, ACT.Exp, bias=soft[:, g, 1, h:h + 1],
                                                 accum_out=soft[:, g, 2, h:h + 1])
                        nc.scalar.activation(soft[:, g, 4], soft[:, g, 3], ACT.Exp).then_inc(exp_ready, 1)
                elif stage == "W":
                    scale_shift(("mix", b, 1), lambda k: actT[:, k],
                                lambda k: col[:, COL_GOUT + k:COL_GOUT + k + 1], None, actT_act)
                    for half in range(2):
                        bank, turn = MM["y", b, half]
                        act.wait_ge(mm_full[bank], turn + 1)
                        last = nc.scalar.activation(junk[:, half * 512:(half + 1) * 512], mm[:, bank, :],
                                                    ACT.Square, accum_out=st[:, 4 + half:5 + half])
                    last.then_inc(y_squared, 1)
                elif stage == "O":
                    for g in range(KVH):
                        bank, turn = TR["prob", b, g, 0]
                        act.wait_ge(tr_full[bank], turn + 1)
                        link(nc.scalar.activation(pT[:, 0], tr[:, bank, :].rearrange("p (h n) -> p h n", h=GROUP),
                                                  ACT.Copy))
                        act.sem_inc(tr_free[bank], 1)
                        act.sem_inc(pT_act, 1)
                    act.wait_ge(sgu_ready, b + 1)
                    link(nc.scalar.activation(junk[:, 512:1024], u_sb[:, b % 2], ACT.Square, accum_out=st[:, 11:12]))
                    act.wait_ge(att_ready, b + 1)
                    link(nc.scalar.activation(junk[:, 0:512], yn[:, 0:512], ACT.Square, accum_out=st[:, 10:11]))
                    act.sem_inc(mix_squared, 1)
                    act.wait_ge(mix_rs, b + 1)
                    nc.scalar.activation(yn[:, 0:512], yn[:, 0:512], ACT.Copy, scale=st[:, 2:3])
                    nc.scalar.activation(yn[:, 512:1024], u_sb[:, b % 2], ACT.Copy,
                                         scale=st[:, 3:4]).then_inc(mix_ready, 1)
                elif stage == "F":
                    act.wait_ge(x1_ready, b + 1)
                    nc.scalar.activation(junk, x_sb[:, b], ACT.Square, accum_out=st[:, 9:10]).then_inc(x1_squared, 1)
                    act.wait_ge(x1_rs, b + 1)
                    nc.scalar.activation(xn2, x_sb[:, b], ACT.Copy, scale=st[:, 8:9]).then_inc(xn2_ready, 1)
                    act.wait_ge(mod_ready, 4)
                    scale_shift(("ffn", b, 1), lambda k: h2T[:, k, b * P:(b + 1) * P],
                                lambda k: mod[:, 3 * KD + k:3 * KD + k + 1],
                                lambda k: mod[:, 2 * KD + k:2 * KD + k + 1], h2T_act)
            act.sem_inc(mixer_act, 1)

            def query(half):
                for group in range(4):
                    side = group % 2
                    for j in range(4):
                        bank, turn = MM["query", half, 4 * group + j]
                        act.wait_ge(mm_full[bank], turn + 1)
                        link(nc.scalar.activation(qhT[:, side, j], mm[:, bank, 0:2 * P], ACT.Copy))
                        act.sem_inc(mm_free[bank], 1)
                    act.sem_inc(qhT_ready, 1)
                    for tb in range(2):
                        n = (half * 4 + group) * 2 + tb
                        act.wait_ge(qs_full, n + 1)
                        first = ((2 * half + tb) * HP + 4 * group) * P
                        link(nc.scalar.activation(scores[:, first:first + 4 * P], sc[:, tb, :], ACT.Copy))
                        act.sem_inc(qs_free, 1)
                act.sem_inc(scores_ready, 1)

            def h2_rows(b):
                if b >= 2:
                    act.wait_ge(h2_used, b - 1)
                for part in range(2):
                    bank, turn = TR["h2", b, part]
                    act.wait_ge(tr_full[bank], turn + 1)
                    link(nc.scalar.activation(h2[:, b % 2, part * 512:(part + 1) * 512], tr[:, bank, :], ACT.Copy))
                    act.sem_inc(tr_free[bank], 1)
                act.sem_inc(h2_ready, 1)

            act.wait_ge(mixer_pe, 1)
            act.wait_ge(mixer_dve, 1)
            query(0)
            h2_rows(0)
            h2_rows(1)

            def gate_softmax(unit):
                act.wait_ge(best_ready, unit + 1)
                nc.scalar.activation(gate_e[:], best_v[:], ACT.Exp, bias=gate_s[:, 0:1],
                                     accum_out=gate_s[:, 1:2]).then_inc(gate_exp, 1)

            def experts(unit, more):
                for part in range(2):
                    act.wait_ge(down_free, unit * TOPK + (part + 2) * RING)
                    nc.scalar.activation(gelus[:, part], dots[:, part], ACT.Gelu).then_inc(gelu_ready, 1)
                if more:
                    gate_softmax(unit + 1)

            gate_softmax(0)
            for b in range(NB):
                if b == 1:
                    h2_rows(2)
                if b == 2:
                    h2_rows(3)
                with act.Fori(0, PH - 1, 1) as h:
                    experts(h + b * PH, True)
                if b == 0:
                    query(1)
                experts(b * PH + PH - 1, b < NB - 1)
                act.wait_ge(y2_ready, b + 1)
                link(nc.scalar.activation(acc[:, 1], acc[:, 0], ACT.Square, accum_out=fin[:, 0:1]))
                nc.scalar.activation(fin[:, 1:2], fin[:, 0:1], ACT.Sqrt, bias=eps_sb[:],
                                     scale=1.0 / D).then_inc(y2_rms, 1)

        @block.vector
        def _(dve):
            link = linker(dve, dve_chain)
            V = nc.vector
            link(V.memset(eps_sb[:], EPS))
            dve.wait_ge(consts_in, 16 * N_CONSTS)
            dve.wait_ge(c_ready, 1)
            V.tensor_copy(c_rows, c_act[:].unsqueeze(2).broadcast_to([P, KD, P])).then_inc(c_rows_ready, 1)
            link(V.tensor_tensor(wsT, wsT, causal.unsqueeze(1).broadcast_to([P, SGU_H, P]), ALU.mult))
            dve.sem_inc(wsT_ready, 1)

            def mean_square(squared, ready, n, source, target, width, count):
                dve.wait_ge(squared, n)
                V.tensor_scalar(target, source, 1.0 / count, EPS, ALU.mult, ALU.add).then_inc(ready, 1)

            def scale_shift(key, out_of, gain_of, shift_of, done):
                bank, turn = TR[key]
                dve.wait_ge(tr_full[bank], turn + 1)
                for j in range(4):
                    k = 4 * key[-1] + j
                    shift = shift_of(k) if shift_of else 0.0
                    last = V.tensor_scalar(out_of(k), tr[:, bank, j * P:(j + 1) * P], gain_of(k), shift,
                                           ALU.mult, ALU.add)
                link(last)
                dve.sem_inc(tr_free[bank], 1)
                dve.sem_inc(done, 1)

            def ada_col(v):
                bank, turn = MM["ada", v]
                dve.wait_ge(mm_full[bank], turn + 1)
                slot = {SH1: 0, SC1: 1, SH2: 2, SC2: 3}[v]
                m = mod[:, slot * KD:(slot + 1) * KD]
                link(V.tensor_tensor(m, mm[:, bank, 0:KD], col[:, COL_BADA + v * KD:COL_BADA + (v + 1) * KD], ALU.add))
                if v in (SC1, SC2):
                    g = COL_G1 if v == SC1 else COL_G2
                    link(V.scalar_tensor_tensor(m, m, 1.0, col[:, g:g + KD], ALU.add, ALU.mult))
                dve.sem_inc(mm_free[bank], 1)
                dve.sem_inc(mod_ready, 1)

            def ada_row(v, gain, factor):
                for half in range(2):
                    bank, turn = MM["ada", v, half]
                    cols_ = slice(half * 512, (half + 1) * 512)
                    dve.wait_ge(mm_full[bank], turn + 1)
                    link(V.tensor_tensor(gain[:, cols_], mm[:, bank, :], gain[:, cols_], ALU.add))
                    dve.sem_inc(mm_free[bank], 1)
                    link(V.tensor_tensor(gain[:, cols_], gain[:, cols_], factor[:, cols_], ALU.mult))

            def rope(src, out_lo_hi, heads, b):
                cos = rope_cs[:, 0, b].unsqueeze(1).broadcast_to([P, heads, HD])
                half = HD // 2
                a = rope_tmp[:, 0, 0:heads * HD].rearrange("p (h d) -> p h d", h=heads)
                c = rope_tmp[:, 1, 0:heads * HD].rearrange("p (h d) -> p h d", h=heads)
                V.tensor_tensor(a, src, cos, ALU.mult)
                for lo, hi in ((0, half), (half, 0)):
                    s = rope_cs[:, 1, b, lo:lo + half].unsqueeze(1).broadcast_to([P, heads, half])
                    last = V.tensor_tensor(c[:, :, lo:lo + half], src[:, :, hi:hi + half], s, ALU.mult)
                link(last)
                for o in out_lo_hi:
                    last = V.tensor_tensor(o, a, c, ALU.add)
                link(last)

            for stage, b in steps():
                if stage == "N":
                    mean_square(x_squared, x_ms, b + 1, st[:, 1:2], st[:, 0:1], 1, D)
                elif stage == "ADA_COL":
                    ada_col(b)
                elif stage == "ADA_ROW" and b == GT1:
                    ada_row(b, gain1, yn)
                elif stage == "ADA_ROW":
                    V.tensor_copy(c_rows2, c_act[:].unsqueeze(2).broadcast_to([P, KD, P])).then_inc(c_rows_ready, 1)
                    dve.wait_ge(gain2_in, 32)
                    ada_row(b, gain2, acc[:, 0])
                elif stage == "T":
                    scale_shift(("x", b, 0), lambda k: actT[:, k], lambda k: mod[:, KD + k:KD + k + 1],
                                lambda k: mod[:, k:k + 1], actT_dve)
                elif stage == "P":
                    bank, turn = MM["proj", b, 0]
                    dve.wait_ge(mm_full[bank], turn + 1)
                    rope(mm[:, bank, :].rearrange("p (h d) -> p h d", h=QH),
                         [q_rot.rearrange("p (h d) -> p h d", h=QH)], QH, b)
                    dve.sem_inc(mm_free[bank], 1)
                    bank, turn = MM["proj", b, 1]
                    dve.wait_ge(mm_full[bank], turn + 1)
                    V.tensor_copy(v_all[:, b], mm[:, bank, KV_W:2 * KV_W])
                    rope(mm[:, bank, 0:KV_W].rearrange("p (h d) -> p h d", h=KVH),
                         [k_dup[:, :, r] for r in range(2)], KVH, b)
                    dve.sem_inc(mm_free[bank], 1)
                    dve.sem_inc(rope_ready, 1)
                elif stage == "LN":
                    dve.wait_ge(vg_ready, b + 1)
                    v3 = vg.rearrange("p (h d) -> p h d", h=SGU_H)
                    d3 = ln_d.rearrange("p (h d) -> p h d", h=SGU_H)
                    n3 = vn.rearrange("p (h d) -> p h d", h=SGU_H)
                    link(V.tensor_reduce(stat[:, 0], v3, AX_X, ALU.add))
                    link(V.tensor_scalar(stat[:, 1], stat[:, 0], 1.0 / HD, None, ALU.mult))
                    link(V.tensor_tensor(d3, v3, stat[:, 1].unsqueeze(2).broadcast_to([P, SGU_H, HD]), ALU.subtract))
                    dve.sem_inc(vg_used, 1)
                    link(V.tensor_tensor(n3, d3, d3, ALU.mult))
                    link(V.tensor_reduce(stat[:, 2], n3, AX_X, ALU.add))
                    V.tensor_scalar(stat[:, 3], stat[:, 2], 1.0 / HD, EPS, ALU.mult, ALU.add).then_inc(var_ready, 1)
                    dve.wait_ge(var_rs, b + 1)
                    link(V.tensor_tensor(n3, d3, stat[:, 3].unsqueeze(2).broadcast_to([P, SGU_H, HD]), ALU.mult))
                    link(V.tensor_tensor(vn, vn, ln_rows[:, 0], ALU.mult))
                    V.tensor_tensor(vn, vn, ln_rows[:, 1], ALU.add).then_inc(vn_ready, 1)
                elif stage == "S1":
                    bank, turn = TR["q", b]
                    dve.wait_ge(tr_full[bank], turn + 1)
                    link(V.tensor_copy(qT.rearrange("p a n -> p (a n)"), tr[:, bank, :]))
                    dve.sem_inc(tr_free[bank], 1)
                    dve.sem_inc(qT_ready, 1)
                elif stage == "S2":
                    for g in range(KVH):
                        dve.wait_ge(sc_full, 2 * b + g + 1)
                        s3 = probs[g].rearrange("p (h n) -> p h n", h=GROUP)
                        first = 0 if b else P
                        if b == 0:
                            V.memset(s3[:, :, 0:P], MASKED)
                        link(V.scalar_tensor_tensor(
                            s3[:, :, first:], sc[:].rearrange("p a (c n) -> p (a c) n", c=2)[:, :, first:],
                            HD ** -0.5, mask_sb[:, first:].unsqueeze(1).broadcast_to([P, GROUP, 2 * P - first]),
                            ALU.mult, ALU.add))
                        dve.sem_inc(sc_free, 1)
                        t = soft[:, g]
                        sk = sink_sb[:, g * GROUP:(g + 1) * GROUP]
                        link(V.tensor_reduce(t[:, 0], s3, AX_X, ALU.max))
                        link(V.tensor_tensor(t[:, 0], t[:, 0], sk, ALU.max))
                        V.tensor_scalar(t[:, 1], t[:, 0], -1.0, None, ALU.mult)
                        link(V.tensor_tensor(t[:, 3], sk, t[:, 0], ALU.subtract))
                        dve.sem_inc(bias_ready, 1)
                elif stage == "G":
                    dve.wait_ge(sgu_full, b + 1)
                    dve.wait_ge(u_ready, b + 1)
                    o3 = ln_d.rearrange("p (h d) -> p h d", h=SGU_H)
                    link(V.tensor_tensor(o3, sgu_ps[:].rearrange("p (h d) -> p h d", h=SGU_H),
                                         bs_sb[:].unsqueeze(2).broadcast_to([P, SGU_H, HD]), ALU.add))
                    dve.sem_inc(sgu_free, 1)
                    V.tensor_tensor(u_sb[:, b % 2], ln_d, u_sb[:, b % 2], ALU.mult).then_inc(sgu_ready, 1)
                    dve.wait_ge(sgu_ready, b + 1)
                elif stage == "W":
                    scale_shift(("mix", b, 0), lambda k: actT[:, k],
                                lambda k: col[:, COL_GOUT + k:COL_GOUT + k + 1], None, actT_dve)
                    dve.wait_ge(y_squared, b + 1)
                    link(V.tensor_tensor(st[:, 7:8], st[:, 4:5], st[:, 5:6], ALU.add))
                    V.tensor_scalar(st[:, 6:7], st[:, 7:8], 1.0 / D, EPS, ALU.mult, ALU.add).then_inc(y_ms, 1)
                    dve.wait_ge(y_rs, b + 1)
                    for half in range(2):
                        bank, turn = MM["y", b, half]
                        c_ = slice(half * 512, (half + 1) * 512)
                        dve.wait_ge(mm_full[bank], turn + 1)
                        link(V.scalar_tensor_tensor(xn2[:, c_], mm[:, bank, :], st[:, 6:7], gain1[:, c_],
                                                    ALU.mult, ALU.mult))
                        dve.sem_inc(mm_free[bank], 1)
                    V.tensor_tensor(x_sb[:, b], x_sb[:, b], xn2, ALU.add).then_inc(x1_ready, 1)
                elif stage == "O":
                    for g in range(KVH):
                        bank, turn = TR["prob", b, g, 1]
                        dve.wait_ge(tr_full[bank], turn + 1)
                        link(V.tensor_copy(pT[:, 1].rearrange("p h n -> p (h n)"), tr[:, bank, :]))
                        dve.sem_inc(tr_free[bank], 1)
                        dve.sem_inc(pT_dve, 1)
                        t = soft[:, g]
                        dve.wait_ge(exp_ready, 2 * b + g + 1)
                        link(V.tensor_tensor(t[:, 5], t[:, 2], t[:, 4], ALU.add))
                        link(V.reciprocal(t[:, 5], t[:, 5]))
                    dve.wait_ge(att_full, b + 1)
                    for g in range(KVH):
                        a_ = slice(g * GROUP * HD, (g + 1) * GROUP * HD)
                        last = V.tensor_tensor(
                            yn[:, a_].rearrange("p (c o d) -> p o c d", o=2, c=2),
                            att_ps[:, a_].rearrange("p (o c d) -> p o c d", o=2, c=2),
                            soft[:, g, 5].rearrange("p (o c) -> p o c", o=2).unsqueeze(3).broadcast_to([P, 2, 2, HD]),
                            ALU.mult)
                    link(last)
                    dve.sem_inc(att_free, 1)
                    dve.sem_inc(att_ready, 1)
                    mean_square(mix_squared, mix_ms, b + 1, st[:, 10:12], st[:, 2:4], 2, SGU_W)
                elif stage == "F":
                    mean_square(x1_squared, x1_ms, b + 1, st[:, 9:10], st[:, 8:9], 1, D)
                    scale_shift(("ffn", b, 0), lambda k: h2T[:, k, b * P:(b + 1) * P],
                                lambda k: mod[:, 3 * KD + k:3 * KD + k + 1],
                                lambda k: mod[:, 2 * KD + k:2 * KD + k + 1], h2T_dve)
                if (stage, b) == ("F", NB - 1):
                    dve.sem_inc(mixer_dve, 1)
                    dve.wait_ge(mixer_pe, 1)
                    dve.wait_ge(mixer_act, 1)


            def top_keys(unit):
                V.tensor_copy(key_s.rearrange("p a n -> p (a n)"), scores[:, bass.ds(unit * (2 * P), 2 * P)])
                dve.drain()
                for p in range(2):
                    V.max(top_v[:, p, 0:8], key_s[:, p])
                dve.drain()
                for p in range(2):
                    V.max_index(top_i[:, p, 0:8], top_v[:, p, 0:8], key_s[:, p])
                    V.match_replace(key_s2[:, p], top_v[:, p, 0:8], key_s[:, p], REMOVED)
                dve.drain()
                for p in range(2):
                    V.max(top_v[:, p, 8:16], key_s2[:, p])
                dve.drain()
                for p in range(2):
                    V.max_index(top_i[:, p, 8:16], top_v[:, p, 8:16], key_s2[:, p])
                V.tensor_tensor(cand.rearrange("p (a c) -> p a c", a=TOPK),
                                top_v[:, 0].unsqueeze(2).broadcast_to([P, TOPK, TOPK]),
                                top_v[:, 1].unsqueeze(1).broadcast_to([P, TOPK, TOPK]), ALU.add)
                dve.drain()

            def top_experts(unit):
                V.tensor_copy(top_f[:], top_i[:])
                V.max(best_v[:, 0:8], cand)
                dve.drain()
                V.max_index(best_j[:, 0:8], best_v[:, 0:8], cand)
                V.match_replace(cand2, best_v[:, 0:8], cand, REMOVED)
                V.tensor_scalar(gate_s[:, 0:1], best_v[:, 0:1], -1.0, None, ALU.mult)
                dve.drain()
                V.max(best_v[:, 8:16], cand2)
                dve.drain().then_inc(best_ready, 1)
                V.max_index(best_j[:, 8:16], best_v[:, 8:16], cand2)
                dve.drain()
                V.tensor_scalar(pos_u[:, 0], best_j[:], 4, None, ALU.logical_shift_right)
                V.tensor_scalar(pos_u[:, 1], best_j[:], TOPK - 1, None, ALU.bitwise_and)
                dve.drain()
                V.tensor_copy(pos_f[:], pos_u[:])
                dve.drain()
                V.tensor_tensor(onehot, iota[:].unsqueeze(1).broadcast_to([P, 2 * TOPK, TOPK]),
                                pos_f[:].rearrange("p a k -> p (a k)").unsqueeze(2).broadcast_to([P, 2 * TOPK, TOPK]),
                                ALU.is_equal)
                dve.drain()
                hot4 = onehot.rearrange("p (a k) j -> p a k j", a=2)
                V.tensor_tensor(hot4, hot4, top_f[:].unsqueeze(2).broadcast_to([P, 2, TOPK, TOPK]), ALU.mult)
                dve.drain()
                V.tensor_reduce(sel[:].rearrange("p a k -> p (a k)"), onehot, AX_X, ALU.add)
                dve.drain()
                V.scalar_tensor_tensor(expert_f[:], sel[:, 0], float(NKEY), sel[:, 1], ALU.mult, ALU.add)
                dve.drain()
                V.tensor_copy(index[:, bass.ds(unit * TOPK, TOPK)], expert_f[:]).then_inc(index_ready, 1)

            def gate_values(unit):
                dve.wait_ge(gate_exp, unit + 1)
                V.reciprocal(gate_s[:, 2:3], gate_s[:, 1:2])
                dve.drain()
                V.tensor_scalar(gates[:, bass.ds(unit * TOPK, TOPK)], gate_e[:], gate_s[:, 2:3], None, ALU.mult)
                dve.drain()

            def dot_products(unit, b, part):
                for r in range(RING):
                    dve.wait_ge(down_in[r], unit * 32 + 16 * (part + 1))
                    dve.wait_ge(down_free, unit * TOPK + (part + 1) * RING + r - 1)
                    V.tensor_tensor_reduce(out=dot_junk[:, r % 2], in0=down_ring[:, r], in1=h2[:, b % 2],
                                           scale=1.0, scalar=0.0, op0=ALU.mult, op1=ALU.add,
                                           accum_out=dots[:, part, r:r + 1]).then_inc(down_free, 1)

            def weighted_rows(unit, part):
                dve.wait_ge(gelu_ready, unit * 2 + part + 1)
                V.tensor_tensor(coef[:, part], gelus[:, part],
                                gates[:, bass.ds(unit * TOPK + part * RING, RING)], ALU.mult)
                dve.drain()
                for r in range(RING):
                    dve.wait_ge(up_in[r], unit * 32 + 16 * (part + 1))
                    dve.wait_ge(up_free, unit * TOPK + (part + 1) * RING + r)
                    V.scalar_tensor_tensor(acc[:, 0], up_ring[:, r], coef[:, part, r:r + 1], acc[:, 0],
                                           ALU.mult, ALU.add).then_inc(up_free, 1)

            def experts(unit, b, more):
                dot_products(unit, b, 0)
                if more:
                    top_keys(unit + 1)
                weighted_rows(unit, 0)
                dot_products(unit, b, 1)
                if more:
                    top_experts(unit + 1)
                weighted_rows(unit, 1)
                if more:
                    gate_values(unit + 1)

            dve.sem_inc(down_free, RING)
            dve.sem_inc(up_free, RING)
            dve.wait_ge(scores_ready, 1)
            top_keys(0)
            top_experts(0)
            gate_values(0)
            for b in range(NB):
                dve.drain()
                link(V.memset(acc[:, 0], 0.0))
                dve.wait_ge(h2_ready, b + 1)
                if b == 1:
                    dve.wait_ge(scores_ready, 2)
                with dve.Fori(0, PH - 1, 1) as h:
                    experts(h + b * PH, b, True)
                experts(b * PH + PH - 1, b, b < NB - 1)
                dve.drain().then_inc(y2_ready, 1)
                dve.sem_inc(h2_used, 1)
                dve.wait_ge(y2_rms, b + 1)
                link(V.reciprocal(fin[:, 2:3], fin[:, 1:2]))
                link(V.scalar_tensor_tensor(acc[:, 1], acc[:, 0], fin[:, 2:3], gain2, ALU.mult, ALU.mult))
                V.tensor_tensor(x_sb[:, b], x_sb[:, b], acc[:, 1], ALU.add).then_inc(out_ready, 1)
                dve.wait_ge(out_ready, b + 1)

        @block.tensor
        def _(pe):
            T = nc.tensor
            chunks = [0]
            n_actT = [0]

            def fill(uses, free, key):
                bank, turn = uses[key]
                if turn:
                    pe.wait_ge(free[bank], turn)
                return bank

            def chunk():
                n = chunks[0]
                pe.wait_ge(chunk_in[n % WRING], 16 * (n // WRING + 1))
                return wring[:, n % WRING]

            def chunk_through():
                chunks[0] += 1

            def transpose4(key, source):
                bank = fill(TR, tr_free, key)
                for j in range(4):
                    last = T.transpose(tr[:, bank, j * P:(j + 1) * P], source(j), ident[:])
                last.then_inc(tr_full[bank], 1)

            def actT_in():
                n_actT[0] += 1
                pe.wait_ge(actT_dve, n_actT[0])
                pe.wait_ge(actT_act, n_actT[0])

            def last_chunk_used(bank, turn):
                pe.wait_ge(mm_full[bank], turn + 1)
                pe.sem_inc(chunk_used, 1)

            pe.wait_ge(consts_in, 16 * N_CONSTS)
            for stage, b in steps():
                if stage == "ADA_COL":
                    if b == SH1:
                        pe.wait_ge(c_ready, 1)
                    bank = fill(MM, mm_free, ("ada", b))
                    for m in range(KD):
                        w = chunk()
                        for k in range(KD):
                            last = T.matmul(mm[:, bank, m:m + 1], w[:, k], c_act[:, k:k + 1],
                                            start=(k == 0), stop=(k == KD - 1))
                        if m < KD - 1:
                            last.then_inc(chunk_used, 1)
                        else:
                            last.then_inc(mm_full[bank], 1)
                            last_chunk_used(bank, MM["ada", b][1])
                        chunk_through()
                elif stage == "ADA_ROW":
                    pe.wait_ge(c_rows_ready, 1 if b == GT1 else 2)
                    left = c_rows if b == GT1 else c_rows2
                    for half in range(2):
                        bank = fill(MM, mm_free, ("ada", b, half))
                        for m in range(4):
                            w = chunk()
                            for k in range(KD):
                                last = T.matmul(mm[:, bank, m * P:(m + 1) * P], left[:, k], w[:, k],
                                                start=(k == 0), stop=(k == KD - 1))
                            if m < 3:
                                last.then_inc(chunk_used, 1)
                            else:
                                last.then_inc(mm_full[bank], 1)
                                last_chunk_used(bank, MM["ada", b, half][1])
                            chunk_through()
                elif stage == "T":
                    pe.wait_ge(xn_ready, b + 1)
                    for half in range(2):
                        transpose4(("x", b, half), lambda j: xn[:, (4 * half + j) * P:(4 * half + j + 1) * P])
                elif stage == "P":
                    actT_in()
                    for c, (first, n) in enumerate(PROJ):
                        if b == 0:
                            pe.wait_ge(win_in[c], 16)
                        bank = fill(MM, mm_free, ("proj", b, c))
                        for k in range(KD):
                            last = T.matmul(mm[:, bank, 0:n], actT[:, k], win_sb[:, k, first:first + n],
                                            start=(k == 0), stop=(k == KD - 1))
                        last.then_inc(mm_full[bank], 1)
                elif stage == "S1":
                    pe.wait_ge(rope_ready, b + 1)
                    transpose4(("q", b), lambda j: q_rot[:, j * P:(j + 1) * P])
                    bank = fill(TR, tr_free, ("k", b))
                    for g in range(KVH):
                        last = T.transpose(tr[:, bank, g * P:(g + 1) * P],
                                           k_dup[:, g].rearrange("p r d -> p (r d)"), ident[:])
                    last.then_inc(tr_full[bank], 1)
                elif stage == "S2":
                    pe.wait_ge(qT_ready, b + 1)
                    pe.wait_ge(kT_ready, b + 1)
                    first = max(b - 1, 0)
                    off = 0 if b else P
                    for g in range(KVH):
                        if 2 * b + g:
                            pe.wait_ge(sc_free, 2 * b + g)
                        for h in range(GROUP):
                            head = g * GROUP + h
                            rows_ = slice(HD * (head % 2), HD * (head % 2) + HD)
                            last = T.matmul(sc[:, h % 2, (h // 2) * 2 * P + off:(h // 2 + 1) * 2 * P],
                                            qT[rows_, head // 2], kT[rows_, g, first * P:(b + 1) * P],
                                            start=True, stop=True)
                        last.then_inc(sc_full, 1)
                elif stage == "G":
                    pe.wait_ge(vn_ready, b + 1)
                    if b == 0:
                        pe.wait_ge(wsT_ready, 1)
                    else:
                        pe.wait_ge(sgu_free, b)
                    for h in range(SGU_H):
                        last = T.matmul(sgu_ps[:, h * HD:(h + 1) * HD], wsT[:, h], vn[:, h * HD:(h + 1) * HD],
                                        start=True, stop=True)
                    last.then_inc(sgu_full, 1)
                elif stage == "W":
                    pe.wait_ge(mix_ready, b + 1)
                    for half in range(2):
                        transpose4(("mix", b, half), lambda j: yn[:, (4 * half + j) * P:(4 * half + j + 1) * P])
                    actT_in()
                    pe.wait_ge(wout_in, 16)
                    for half in range(2):
                        bank = fill(MM, mm_free, ("y", b, half))
                        for k in range(KD):
                            last = T.matmul(mm[:, bank, :], actT[:, k], wout_sb[:, k, half * 512:(half + 1) * 512],
                                            start=(k == 0), stop=(k == KD - 1))
                        last.then_inc(mm_full[bank], 1)
                elif stage == "O":
                    for g in range(KVH):
                        pe.wait_ge(exp_ready, 2 * b + g + 1)
                        for j in range(2):
                            transpose4(("prob", b, g, j),
                                       lambda h: probs[g][:, (2 * h + j) * P:(2 * h + j + 1) * P])
                        pe.wait_ge(pT_act, 2 * b + g + 1)
                        pe.wait_ge(pT_dve, 2 * b + g + 1)
                        if g == 0 and b:
                            pe.wait_ge(att_free, b)
                        for h in range(GROUP):
                            head = g * GROUP + h
                            for j in range(2):
                                last = T.matmul(att_ps[:, head * HD:(head + 1) * HD], pT[:, j, h],
                                                v_all[:, max(b - 1 + j, 0), g * HD:(g + 1) * HD],
                                                start=(j == 0), stop=(j == 1))
                    last.then_inc(att_full, 1)
                elif stage == "F":
                    pe.wait_ge(xn2_ready, b + 1)
                    for half in range(2):
                        transpose4(("ffn", b, half), lambda j: xn2[:, (4 * half + j) * P:(4 * half + j + 1) * P])
                if (stage, b) == ("F", NB - 1):
                    bank, turn = TR["ffn", NB - 1, 1]
                    pe.wait_ge(tr_full[bank], turn + 1)
                    pe.sem_inc(mixer_pe, 1)

            def query(half):
                if half == 0:
                    pe.wait_ge(h2T_dve, NB)
                    pe.wait_ge(h2T_act, NB)
                    pe.wait_ge(keys_in, 16)
                for group in range(4):
                    for j in range(4):
                        hp = 4 * group + j
                        bank = fill(MM, mm_free, ("query", half, hp))
                        w = chunk()
                        for k in range(KD):
                            last = T.matmul(mm[:, bank, 0:2 * P], w[:, k], h2T[:, k, half * 2 * P:(half + 1) * 2 * P],
                                            start=(k == 0), stop=(k == KD - 1))
                        last.then_inc(mm_full[bank], 1)
                        last_chunk_used(bank, MM["query", half, hp][1])
                        chunk_through()
                    pe.wait_ge(qhT_ready, half * 4 + group + 1)
                    for tb in range(2):
                        n = (half * 4 + group) * 2 + tb
                        if n >= 2:
                            pe.wait_ge(qs_free, n - 1)
                        for j in range(4):
                            last = T.matmul(sc[:, tb, j * P:(j + 1) * P], qhT[:, group % 2, j, tb * P:(tb + 1) * P],
                                            keys_sb[:, 4 * group + j], start=True, stop=True)
                        last.then_inc(qs_full, 1)

            def h2_rows(b):
                for part in range(2):
                    transpose4(("h2", b, part), lambda j: h2T[:, 4 * part + j, b * P:(b + 1) * P])

            query(0)
            h2_rows(0)
            h2_rows(1)
            query(1)
            h2_rows(2)
            h2_rows(3)


def kernel(x, c, w_ada, b_ada, g_pre_mix, g_post_mix, g_pre_ffn, g_post_ffn, w_in, w_s, b_s, sgu_ln_g,
           sgu_ln_b, sinks, g_att_out, g_sgu_out, w_out, w_query, sub_keys, expert_down, expert_up):
    import concourse.bacc as bacc
    from concourse.bass_utils import run_bass_kernel_spmd

    f = lambda a: np.ascontiguousarray(np.asarray(a))

    def columns(v):
        return f(v).reshape(-1, P).T

    def chunks(w):
        w = f(w)
        return np.ascontiguousarray(w.reshape(KD, P, -1, P).transpose(2, 1, 0, 3))

    half = HD // 2
    inv = np.float32(10000.0) ** (-np.arange(half, dtype=np.float32) / np.float32(half))
    ang = np.arange(SEQ, dtype=np.float32)[:, None] * inv[None, :]
    cos, sin = np.cos(ang), np.sin(ang)
    by_block = lambda t: np.ascontiguousarray(t.reshape(NB, P, HD).transpose(1, 0, 2), dtype=np.float32)
    q, s = np.arange(P)[:, None], np.arange(P)[None, :]
    masks = np.concatenate([
        (q <= s).astype(np.float32),
        np.where(s > q, 0.0, MASKED).astype(np.float32),
        np.where(s <= q, 0.0, MASKED).astype(np.float32),
    ], axis=1)

    mod_rows = f(b_ada)[0].reshape(6, D)
    arrays = {
        "x": f(x)[0],
        "cols": np.ascontiguousarray(np.concatenate([
            columns(f(c)[0]), columns(f(b_ada)[0]), columns(f(g_pre_mix)[0]), columns(f(g_pre_ffn)[0]),
            columns(f(g_att_out)[0]), columns(f(g_sgu_out)[0])], axis=1)),
        "rows": np.concatenate([mod_rows[GT1], f(g_post_mix)[0], mod_rows[GT2], f(g_post_ffn)[0],
                                f(sgu_ln_g)[0].reshape(-1), f(sgu_ln_b)[0].reshape(-1)]),
        "w_ada": chunks(f(w_ada)[0]),
        "w_in": f(w_in)[0],
        "w_s": np.ascontiguousarray(f(w_s)[0].transpose(2, 0, 1)),
        "b_s": np.ascontiguousarray(f(b_s)[0].T),
        "sinks": np.ascontiguousarray(f(sinks)[0].reshape(KVH, 2, 2).transpose(0, 2, 1).reshape(-1)),
        "w_out": f(w_out)[0],
        "w_query": chunks(f(w_query)[0]),
        "keys": np.ascontiguousarray(f(sub_keys)[0].reshape(HP, NKEY, P).transpose(2, 0, 1)),
        "down": f(expert_down)[0],
        "up": f(expert_up)[0],
        "cos_tab": by_block(np.concatenate([cos, cos], axis=1)),
        "sin_tab": by_block(np.concatenate([-sin, sin], axis=1)),
        "masks": masks,
        "ident_in": np.eye(P, dtype=np.float32),
        "iota_in": np.ascontiguousarray(np.broadcast_to(np.arange(TOPK, dtype=np.float32), (P, TOPK))),
    }
    nc = bacc.Bacc("TRN2", target_bir_lowering=False, num_devices=1)
    aps = [nc.dram_tensor(f"in_{n}", a.shape, mybir.dt.from_np(a.dtype), kind="ExternalInput").ap()
           for n, a in arrays.items()]
    out = nc.dram_tensor("out_0", (SEQ, D), F32, kind="ExternalOutput").ap()
    hybrid_block(nc, *aps, out)
    r = run_bass_kernel_spmd(nc, [{f"in_{n}": a for n, a in arrays.items()}], core_ids=[0])
    return r.results[0]["out_0"].reshape(1, SEQ, D)
```

```python
from contextlib import ExitStack

import numpy as np

import concourse.bass as bass
from concourse import mybir
from concourse.alu_op_type import AluOpType as ALU

F32 = mybir.dt.float32
BF16 = mybir.dt.bfloat16
U32 = mybir.dt.uint32
ACT = mybir.ActivationFunctionType
AX_X = mybir.AxisListType.X

P = 128
D, SEQ = 1024, 512
NB = SEQ // P
KD = D // P
HD = 64
QH, KVH = 8, 2
GROUP = QH // KVH
SGU_H = 8
ATT_W, KV_W, SGU_W = QH * HD, KVH * HD, SGU_H * HD
IN_COLS = ATT_W + 2 * KV_W + 2 * SGU_W
PROJ = [(0, ATT_W), (ATT_W, 2 * KV_W), (ATT_W + 2 * KV_W, SGU_W), (ATT_W + 2 * KV_W + SGU_W, SGU_W)]
PH, TOPK, NKEY = 8, 16, 128
HP = PH * 2
DENSE_B = 2
DT = DENSE_B * P
GATHER_B = NB - DENSE_B
UNITS = GATHER_B * PH
TILES = NKEY
TILES_UNIT = TILES // UNITS
HALF_T = TILES // GATHER_B
BATCH = 8
BATCHES = DT // BATCH
TRING = 4
EPS = 1e-6
MASKED = -1e30
REMOVED = -3e38
RING = 4
PARTS = TOPK // RING
WRING = 6
ADA_CHUNKS = 6 * KD
SH1, SC1, GT1, SH2, SC2, GT2 = range(6)
COL_C, COL_BADA, COL_G1, COL_G2, COL_GOUT, N_COLS = 0, 8, 56, 64, 72, 80


def steps():
    out = [("N", 0), ("ADA_COL", SH1), ("ADA_COL", SC1)]
    for s in range(NB):
        out.append(("T", s))
        if s >= 1:
            out.append(("S1", s - 1))
        if s + 1 < NB:
            out.append(("N", s + 1))
        if s >= 1:
            out.append(("LN", s - 1))
        out.append(("P", s))
        if s == 0:
            out.append(("ADA_ROW", GT1))
        if s == 1:
            out += [("ADA_COL", SH2), ("ADA_COL", SC2)]
        if s >= 1:
            out += [("S2", s - 1), ("G", s - 1)]
        if s >= 2:
            out.append(("W", s - 2))
        if s >= 1:
            out.append(("O", s - 1))
        if s >= 2:
            out.append(("F", s - 2))
    a, z = NB - 2, NB - 1
    out += [("S1", z), ("Q", 0), ("LN", z), ("S2", z), ("G", z), ("TK", 0), ("W", a), ("O", z), ("Q", 1),
            ("F", a), ("TK", 1), ("W", z), ("Q", 2), ("F", z), ("Q", 3), ("TK", 2), ("TK", 3)]
    out += [("Q", 4 + g) for g in range(4)] + [("ADA_ROW", GT2)]
    return out


def bank_turns(names):
    return {name: (n % 2, n // 2) for n, name in enumerate(names)}


def matmul_uses():
    out = []
    for stage, b in steps():
        if stage == "ADA_COL":
            out.append(("ada", b))
        elif stage == "ADA_ROW":
            out += [("ada", b, half) for half in range(2)]
        elif stage == "P":
            out += [("proj", b, c) for c in range(len(PROJ))]
        elif stage == "W":
            out += [("y", b, half) for half in range(2)]
        elif stage == "Q":
            out += [("query", 4 * b + j) for j in range(4)] + [("score", b, tb) for tb in range(2)]
    return bank_turns(out)


def transpose_uses():
    out = []
    for stage, b in steps():
        if stage == "T":
            out += [("x", b, half) for half in range(2)]
        elif stage == "S1":
            out += [("q", b), ("k", b)]
        elif stage == "O":
            out += [("prob", b, g, j) for g in range(KVH) for j in range(2)]
        elif stage == "W":
            out += [("mix", b, half) for half in range(2)]
        elif stage == "F":
            out += [("ffn", b, half) for half in range(2)]
    out += [("h2", b, half) for b in range(DENSE_B, NB) for half in range(2)]
    out += [("onehot", 0), ("onehot", 1)]
    return bank_turns(out)


def hybrid_block(nc, x, cols, rows, w_ada, w_in, w_s, b_s, sinks, w_out, w_query, keys, down, up,
                 down_tiles, cos_tab, sin_tab, masks, ident_in, iota_in, out):
    MM, TR = matmul_uses(), transpose_uses()
    x1_dram = nc.dram_tensor("x1_kept", (NB, P, D), F32, kind="Internal").ap()
    with ExitStack() as ctx:
        def sb(name, shape, dt=F32):
            return ctx.enter_context(nc.sbuf_tensor(name, shape, dt))

        def psum(name, shape):
            return ctx.enter_context(nc.psum_tensor(name, shape, F32))

        def sem(name):
            return ctx.enter_context(nc.semaphore(name))

        W = sb("W", [P, KD * IN_COLS + KD * D])
        win_sb = W[:, 0:KD * IN_COLS].rearrange("p (k n) -> p k n", k=KD)
        wout_sb = W[:, KD * IN_COLS:KD * (IN_COLS + D)].rearrange("p (k n) -> p k n", k=KD)
        w_at = [0]

        def from_w(n):
            w_at[0] += n
            return W[:, w_at[0] - n:w_at[0]]

        cand = from_w(TOPK * TOPK)
        best_d = from_w(DT).rearrange("p (u k) -> p u k", k=TOPK)
        key_s2 = from_w(2 * P).rearrange("p (a n) -> p a n", a=2)
        key_s = from_w(2 * P).rearrange("p (a n) -> p a n", a=2)
        onehot = from_w(2 * TOPK * TOPK).rearrange("p (a j) -> p a j", j=TOPK)
        chosen = from_w(2 * DT)
        gates_d = from_w(DT)
        index = from_w(UNITS * TOPK).bitcast(U32)
        gates = from_w(UNITS * TOPK)
        assert w_at[0] <= 2816
        keys_sb = W[:, 2816:2816 + HP * P].rearrange("p (h n) -> p h n", h=HP)
        qhT = W[:, 4864:4864 + 2 * 4 * 2 * P].rearrange("p (r h n) -> p r h n", r=2, h=4)
        scores_d = W[:, 6912:6912 + DENSE_B * HP * P]
        hot_j = W[:, 2816:2816 + 2 * BATCH * P].rearrange("p (r t j) -> p r t j", r=2, t=BATCH)
        hot_i = W[:, 4864:4864 + 2 * BATCH * HALF_T].rearrange("p (r t i) -> p r t i", r=2, t=BATCH)
        x1_dense = W[:, 2816:2816 + DENSE_B * D].rearrange("p (b n) -> p b n", b=DENSE_B)
        gate_mat = W[:, 6144:6144 + DT * HALF_T].rearrange("p (t i) -> p t i", t=DT)

        wring = sb("wring", [P, WRING, KD, P])
        x_sb = sb("x_sb", [P, NB, D])
        h2T = sb("h2T", [P, 2, KD, 2 * P])
        c_rows = h2T[:, 0, :, 0:P]
        rope_cs = h2T[:, 1].rearrange("p k n -> p (k n)")[:, 0:2 * NB * HD].rearrange(
            "p (a b d) -> p a b d", a=2, b=NB)
        h2 = x_sb[:, 0:2]
        acc = x_sb[:, 2:4]
        tile_down = [wring[:, r] for r in range(TRING)]
        tile_up = [wring[:, TRING].rearrange("p k n -> p (k n)"), wring[:, TRING + 1].rearrange("p k n -> p (k n)"),
                   h2T[:, 1, 0:4].rearrange("p k n -> p (k n)"), h2T[:, 1, 4:8].rearrange("p k n -> p (k n)")]

        WORK = 15488
        work = sb("work", [P, WORK])
        at = [0]

        def take(n):
            at[0] += n
            assert at[0] <= WORK, at[0]
            return work[:, at[0] - n:at[0]]

        xn = take(D)
        actT = take(D).rearrange("p (k n) -> p k n", k=KD)
        yn = take(D)
        rope_tmp = take(2 * ATT_W).rearrange("p (a n) -> p a n", a=2)
        probs = [take(GROUP * 2 * P), rope_tmp.rearrange("p a n -> p (a n)")]
        q_rot = take(ATT_W)
        k_dup = take(2 * KV_W).rearrange("p (g r d) -> p g r d", g=KVH, r=2)
        v_all = take(NB * KV_W).rearrange("p (b n) -> p b n", b=NB)
        kT = take(KVH * NB * P).rearrange("p (g n) -> p g n", g=KVH)
        u_sb = take(2 * SGU_W).rearrange("p (r n) -> p r n", r=2)
        vg = take(SGU_W)
        ln_both = take(2 * SGU_W)
        ln_d, vn = ln_both[:, 0:SGU_W], ln_both[:, SGU_W:2 * SGU_W]
        xn2 = ln_both
        qT = take(ATT_W).rearrange("p (a n) -> p a n", a=GROUP)
        pT = take(2 * GROUP * P).rearrange("p (j h n) -> p j h n", j=2, h=GROUP)
        wsT = take(SGU_H * P).rearrange("p (h n) -> p h n", h=SGU_H)
        gain1 = take(D)
        ln_rows = take(2 * SGU_W).rearrange("p (a n) -> p a n", a=2)
        causal = take(P)
        mask_sb = take(2 * P)
        junk = take(D // 2).bitcast(BF16)

        at[0] = 0
        scores = take(UNITS * 2 * P)
        down_ring = take(RING * D).rearrange("p (r n) -> p r n", r=RING)
        up_ring = take(RING * D).rearrange("p (r n) -> p r n", r=RING)
        dot_junk = take(D).bitcast(BF16).rearrange("p (r n) -> p r n", r=2)
        gain2 = take(D)
        square_junk = dot_junk[:, 0]
        weights = take(TRING * DT).rearrange("p (r t) -> p r t", r=TRING)
        dots, gelus, coef = (take(PARTS * RING).rearrange("p (a r) -> p a r", a=PARTS) for _ in range(3))
        zeros = weights[:, TRING - 1, 0:P]
        c_rows2 = weights.rearrange("p r t -> p (r t)").rearrange("p (k n) -> p k n", k=KD)

        ident = sb("ident", [P, P])
        col = sb("col", [P, N_COLS])
        mod = sb("mod", [P, 4 * KD])
        bs_sb = sb("bs_sb", [P, SGU_H])
        sink_sb = sb("sink_sb", [P, QH])
        c_act = sb("c_act", [P, KD])
        halves = sb("halves", [P, 4])
        eps_sb = sb("eps_sb", [P, 1])
        st = sb("st", [P, 16])
        stat = sb("stat", [P, 4, SGU_H])
        soft = sb("soft", [P, KVH, 6, GROUP])
        iota = sb("iota", [P, P])
        top_v = sb("top_v", [P, 2, TOPK])
        top_i = sb("top_i", [P, 2, TOPK], U32)
        top_f = sb("top_f", [P, 2, TOPK])
        best_v = sb("best_v", [P, TOPK])
        best_j = sb("best_j", [P, TOPK], U32)
        pos_u = sb("pos_u", [P, 2, TOPK], U32)
        pos_f = sb("pos_f", [P, 2, TOPK])
        sel = sb("sel", [P, 2, TOPK])
        expert_f = sb("expert_f", [P, TOPK])
        gate_e = sb("gate_e", [P, TOPK])
        gate_s = sb("gate_s", [P, 4])
        staged = sb("staged", [P, 2, TOPK], U32)
        soft_d = sb("soft_d", [P, 2, DENSE_B * PH])
        fin = sb("fin", [P, 4])

        mm = psum("mm", [P, 2, 512])
        tr = psum("tr", [P, 2, 512])
        sc = psum("sc", [P, 2, 512])
        att_ps = psum("att_ps", [P, 512])
        sgu_ps = psum("sgu_ps", [P, 512])
        y_bank = [[sc[:, 0], sc[:, 1]], [att_ps[:], sgu_ps[:]]]

        consts_in = sem("consts_in")
        x_in = sem("x_in")
        win_in = [sem(f"win_in{c}") for c in range(len(PROJ))]
        wout_in = sem("wout_in")
        chunk_in = [sem(f"chunk_in{r}") for r in range(WRING)]
        chunk_used = sem("chunk_used")
        gain2_in = sem("gain2_in")
        keys_in = sem("keys_in")
        mm_full = [sem(f"mm_full{i}") for i in range(2)]
        mm_free = [sem(f"mm_free{i}") for i in range(2)]
        tr_full = [sem(f"tr_full{i}") for i in range(2)]
        tr_free = [sem(f"tr_free{i}") for i in range(2)]
        c_rows_ready = sem("c_rows_ready")
        c_ready = sem("c_ready")
        mod_ready = sem("mod_ready")
        x_squared = sem("x_squared")
        x_ms = sem("x_ms")
        x_rs = sem("x_rs")
        xn_ready = sem("xn_ready")
        actT_dve = sem("actT_dve")
        actT_act = sem("actT_act")
        rope_ready = sem("rope_ready")
        vg_ready = sem("vg_ready")
        vg_used = sem("vg_used")
        var_ready = sem("var_ready")
        var_rs = sem("var_rs")
        vn_ready = sem("vn_ready")
        wsT_ready = sem("wsT_ready")
        qT_ready = sem("qT_ready")
        kT_ready = sem("kT_ready")
        sc_full = sem("sc_full")
        sc_free = sem("sc_free")
        bias_ready = sem("bias_ready")
        exp_ready = sem("exp_ready")
        pT_act = sem("pT_act")
        pT_dve = sem("pT_dve")
        att_full = sem("att_full")
        sgu_full = sem("sgu_full")
        att_free = sem("att_free")
        sgu_free = sem("sgu_free")
        att_ready = sem("att_ready")
        u_ready = sem("u_ready")
        sgu_ready = sem("sgu_ready")
        mix_squared = sem("mix_squared")
        mix_ms = sem("mix_ms")
        mix_rs = sem("mix_rs")
        mix_ready = sem("mix_ready")
        y_squared = sem("y_squared")
        y_ms = sem("y_ms")
        y_rs = sem("y_rs")
        x1_ready = sem("x1_ready")
        x1_squared = sem("x1_squared")
        x1_ms = sem("x1_ms")
        x1_rs = sem("x1_rs")
        xn2_ready = sem("xn2_ready")
        h2T_dve = sem("h2T_dve")
        h2T_act = sem("h2T_act")
        mixer_pe = sem("mixer_pe")
        mixer_dve = sem("mixer_dve")
        mixer_act = sem("mixer_act")
        qhT_ready = sem("qhT_ready")
        x1_saved = sem("x1_saved")
        x1_back = sem("x1_back")
        x1_dense_in = sem("x1_dense_in")
        best_d_ready = sem("best_d_ready")
        gate_exp_d = sem("gate_exp_d")
        chosen_ready = sem("chosen_ready")
        hot_ready = sem("hot_ready")
        gate_full = sem("gate_full")
        gate_stored = sem("gate_stored")
        act_full = sem("act_full")
        tile_gelu = sem("tile_gelu")
        weights_ready = sem("weights_ready")
        tile_done = sem("tile_done")
        tile_down_in = [sem(f"tile_down_in{r}") for r in range(TRING)]
        tile_up_in = [sem(f"tile_up_in{r}") for r in range(TRING)]
        h2T_used = sem("h2T_used")
        dense_squared = sem("dense_squared")
        dense_rms = sem("dense_rms")
        dense_out = sem("dense_out")
        scores_ready = sem("scores_ready")
        h2_ready = sem("h2_ready")
        h2_used = sem("h2_used")
        down_in = [sem(f"down_in{r}") for r in range(RING)]
        up_in = [sem(f"up_in{r}") for r in range(RING)]
        down_free = sem("down_free")
        up_free = sem("up_free")
        index_ready = sem("index_ready")
        staged_ready = sem("staged_ready")
        issue_ok = sem("issue_ok")
        best_ready = sem("best_ready")
        gate_exp = sem("gate_exp")
        gelu_ready = sem("gelu_ready")
        y2_ready = sem("y2_ready")
        y2_rms = sem("y2_rms")
        out_ready = sem("out_ready")
        out_done = sem("out_done")
        dve_chain = sem("dve_chain")
        act_chain = sem("act_chain")
        pool_chain = sem("pool_chain")

        def linker(eng, chain):
            n = [0]

            def link(ins):
                n[0] += 1
                ins.then_inc(chain, 1)
                eng.wait_ge(chain, n[0])

            return link

        N_CONSTS = 13
        block = ctx.enter_context(nc.Block())

        @block.sync
        def _(sp):
            def chunk(n, source):
                if n >= WRING:
                    sp.wait_ge(chunk_used, n - WRING + 1)
                sp.dma_start(wring[:, n % WRING], source).then_inc(chunk_in[n % WRING], 16)

            sp.dma_start(col[:], cols).then_inc(consts_in, 16)
            sp.dma_start(x_sb[:, 0], x[0:P, :]).then_inc(x_in, 16)
            sp.dma_start(ident[:], ident_in).then_inc(consts_in, 16)
            sp.dma_start(rope_cs[:, 0], cos_tab).then_inc(consts_in, 16)
            sp.dma_start(rope_cs[:, 1], sin_tab).then_inc(consts_in, 16)
            sp.dma_start(causal, masks[:, 0:P]).then_inc(consts_in, 16)
            sp.dma_start(mask_sb, masks[:, P:3 * P]).then_inc(consts_in, 16)
            sp.dma_start(iota[:], iota_in).then_inc(consts_in, 16)
            sp.dma_start(bs_sb[:], b_s).then_inc(consts_in, 16)
            sp.dma_start(sink_sb[:], sinks.partition_broadcast(P)).then_inc(consts_in, 16)
            sp.dma_start(wsT, w_s).then_inc(consts_in, 16)
            sp.dma_start(ln_rows, rows[4 * D:4 * D + 2 * SGU_W].partition_broadcast(P)
                         .rearrange("p (a n) -> p a n", a=2)).then_inc(consts_in, 16)
            sp.dma_start(gain1, rows[0:D].partition_broadcast(P)).then_inc(consts_in, 16)
            sp.dma_start(yn, rows[D:2 * D].partition_broadcast(P)).then_inc(consts_in, 16)
            for n in range(2 * KD):
                chunk(n, w_ada[n])
            for c, (first, n) in enumerate(PROJ):
                sp.dma_start(win_sb[:, :, first:first + n],
                             w_in.rearrange("(k p) n -> p k n", p=P)[:, :, first:first + n]
                             ).then_inc(win_in[c], 16)
            sp.wait_ge(x_in, 16)
            for b in range(1, NB):
                sp.dma_start(x_sb[:, b], x[b * P:(b + 1) * P, :]).then_inc(x_in, 16)
                sp.wait_ge(x_in, 16 * (b + 1))
            sp.dma_start(wout_sb, w_out.rearrange("(k p) n -> p k n", p=P)).then_inc(wout_in, 16)
            for n in range(2 * KD, 5 * KD):
                chunk(n, w_ada[n])
            bank, turn = MM["proj", NB - 1, len(PROJ) - 1]
            sp.wait_ge(mm_full[bank], turn + 1)
            sp.dma_start(keys_sb, keys).then_inc(keys_in, 16)
            for hp in range(HP):
                chunk(5 * KD + hp, w_query[hp])
            for hp in range(HP):
                chunk(5 * KD + HP + hp, w_query[hp])
            sp.wait_ge(mixer_pe, 1)
            sp.wait_ge(mixer_dve, 1)
            sp.wait_ge(mixer_act, 1)
            sp.wait_ge(x1_saved, 16 * NB)
            sp.dma_start(gain2, rows[2 * D:3 * D].partition_broadcast(P)).then_inc(gain2_in, 16)
            sp.dma_start(acc[:, 0], rows[3 * D:4 * D].partition_broadcast(P)).then_inc(gain2_in, 16)
            for n in range(KD):
                chunk(5 * KD + 2 * HP + n, w_ada[GT2 * KD + n])
            sp.dma_start(acc[:, 1], x1_dram[DENSE_B]).then_inc(x1_back, 16)
            sp.wait_ge(chunk_used, ADA_CHUNKS + 2 * HP)
            sp.wait_ge(h2T_used, 1)
            with sp.Fori(0, TILES // TRING, 1) as i:
                for r in range(TRING):
                    n = i * TRING + r
                    sp.wait_ge(act_full, n + 1)
                    sp.dma_start(tile_down[r], down_tiles[bass.ds(n, 1)].rearrange("o p k n -> (o p) k n")
                                 ).then_inc(tile_down_in[r], 16)
                    sp.wait_ge(tile_done, n + 1)
                    sp.dma_start(tile_up[r], up[bass.ds(n * P, P), :]).then_inc(tile_up_in[r], 16)
            sp.wait_ge(gate_full, 2 + GATHER_B * BATCHES)
            for b in range(DENSE_B):
                sp.dma_start(x1_dense[:, b], x1_dram[b]).then_inc(x1_dense_in, 16)
            sp.wait_ge(dense_out, DENSE_B)
            for b in range(DENSE_B):
                sp.dma_start(out[b * P:(b + 1) * P, :], x1_dense[:, b]).then_inc(out_done, 16)
            sp.wait_ge(out_done, 16 * NB)

        @block.gpsimd
        def _(pool):
            link = linker(pool, pool_chain)
            link(nc.gpsimd.memset(halves[:], -0.5))

            def rsqrt(ready, done, n, at_, width=1):
                pool.wait_ge(ready, n)
                nc.gpsimd.tensor_tensor(at_, at_, halves[:, 0:1].to_broadcast([P, width]),
                                        ALU.pow).then_inc(done, 1)

            for stage, b in steps():
                if stage == "N":
                    rsqrt(x_ms, x_rs, b + 1, st[:, 0:1])
                elif stage == "LN":
                    rsqrt(var_ready, var_rs, b + 1, stat[:, 3], SGU_H)
                elif stage == "O":
                    rsqrt(mix_ms, mix_rs, b + 1, st[:, 2:4], 2)
                elif stage == "W":
                    rsqrt(y_ms, y_rs, b + 1, st[:, 6:7])
                elif stage == "F":
                    rsqrt(x1_ms, x1_rs, b + 1, st[:, 8:9])
            pool.wait_ge(mixer_pe, 1)
            pool.wait_ge(mixer_act, 1)
            pool.wait_ge(mixer_dve, 1)

            def gather(table, ring, free, arrived, r, side, first):
                pool.wait_ge(free, first + r + 1)
                pool.sem_inc(issue_ok, 1)
                nc.gpsimd.indirect_dma_start(
                    ring[:, r % RING], None, table,
                    bass.IndirectOffsetOnAxis(ap=staged[:, side, r:r + 1], axis=0),
                ).then_inc(arrived[r % RING], 16)

            with pool.Fori(0, UNITS // 2, 1) as i:
                for side in range(2):
                    unit = i * 2 + side
                    pool.wait_ge(index_ready, unit + 1)
                    pool.wait_ge(up_free, unit * TOPK + 1)
                    nc.gpsimd.tensor_copy(staged[:, side], index[:, bass.ds(unit * TOPK, TOPK)]
                                          ).then_inc(staged_ready, 1)
                    pool.wait_ge(staged_ready, unit + 1)
                    pool.sem_inc(issue_ok, 1)
                    for part in range(PARTS):
                        for r in range(part * RING, (part + 1) * RING):
                            gather(down, down_ring, down_free, down_in, r, side, unit * TOPK)
                        for r in range(part * RING, (part + 1) * RING):
                            gather(up, up_ring, up_free, up_in, r, side, unit * TOPK)

        @block.scalar
        def _(act):
            link = linker(act, act_chain)
            act.wait_ge(consts_in, 16 * N_CONSTS)
            nc.scalar.activation(c_act[:], col[:, COL_C:COL_C + KD], ACT.Silu).then_inc(c_ready, 1)

            def scale_shift(key, out_of, gain_of, shift_of, done):
                bank, turn = TR[key]
                act.wait_ge(tr_full[bank], turn + 1)
                for j in range(4):
                    k = 4 * key[-1] + j
                    shift = shift_of(k) if shift_of else 0.0
                    last = nc.scalar.activation(out_of(k), tr[:, bank, j * P:(j + 1) * P],
                                                ACT.Identity if shift_of else ACT.Copy,
                                                bias=shift, scale=gain_of(k))
                link(last)
                act.sem_inc(tr_free[bank], 1)
                act.sem_inc(done, 1)

            def query(group):
                half, g = group // 4, group % 4
                if group == 4:
                    act.wait_ge(mixer_pe, 1)
                    act.wait_ge(mixer_dve, 1)
                for j in range(4):
                    bank, turn = MM["query", 4 * group + j]
                    act.wait_ge(mm_full[bank], turn + 1)
                    link(nc.scalar.activation(qhT[:, group % 2, j], mm[:, bank, 0:2 * P], ACT.Copy))
                    act.sem_inc(mm_free[bank], 1)
                act.sem_inc(qhT_ready, 1)
                target = scores if half else scores_d
                for tb in range(2):
                    bank, turn = MM["score", group, tb]
                    act.wait_ge(mm_full[bank], turn + 1)
                    first = (tb * HP + 4 * g) * P
                    link(nc.scalar.activation(target[:, first:first + 4 * P], mm[:, bank, :], ACT.Copy))
                    act.sem_inc(mm_free[bank], 1)
                act.sem_inc(scores_ready, 1)

            for stage, b in steps():
                if stage == "N":
                    act.wait_ge(x_in, 16 * (b + 1))
                    if b:
                        bank, turn = TR["x", b - 1, 1]
                        act.wait_ge(tr_full[bank], turn + 1)
                        act.wait_ge(x_ms, b)
                    nc.scalar.activation(junk, x_sb[:, b], ACT.Square, accum_out=st[:, 1:2]).then_inc(x_squared, 1)
                    act.wait_ge(x_rs, b + 1)
                    nc.scalar.activation(xn, x_sb[:, b], ACT.Copy, scale=st[:, 0:1]).then_inc(xn_ready, 1)
                elif stage == "T":
                    act.wait_ge(mod_ready, 2)
                    scale_shift(("x", b, 1), lambda k: actT[:, k],
                                lambda k: mod[:, KD + k:KD + k + 1], lambda k: mod[:, k:k + 1], actT_act)
                elif stage == "S1":
                    bank, turn = TR["k", b]
                    act.wait_ge(tr_full[bank], turn + 1)
                    link(nc.scalar.activation(kT[:, :, b * P:(b + 1) * P],
                                              tr[:, bank, 0:2 * P].rearrange("p (g n) -> p g n", g=2), ACT.Copy))
                    act.sem_inc(tr_free[bank], 1)
                    act.sem_inc(kT_ready, 1)
                elif stage == "P":
                    bank, turn = MM["proj", b, 2]
                    act.wait_ge(mm_full[bank], turn + 1)
                    if b >= 2:
                        act.wait_ge(mix_ready, b - 1)
                    link(nc.scalar.activation(u_sb[:, b % 2], mm[:, bank, :], ACT.Gelu))
                    act.sem_inc(mm_free[bank], 1)
                    act.sem_inc(u_ready, 1)
                    bank, turn = MM["proj", b, 3]
                    act.wait_ge(mm_full[bank], turn + 1)
                    if b:
                        act.wait_ge(vg_used, b)
                    link(nc.scalar.activation(vg, mm[:, bank, :], ACT.Gelu))
                    act.sem_inc(mm_free[bank], 1)
                    act.sem_inc(vg_ready, 1)
                elif stage == "S2":
                    for g in range(KVH):
                        act.wait_ge(bias_ready, 2 * b + g + 1)
                        for h in range(GROUP):
                            s = probs[g][:, h * 2 * P:(h + 1) * 2 * P]
                            nc.scalar.activation(s, s, ACT.Exp, bias=soft[:, g, 1, h:h + 1],
                                                 accum_out=soft[:, g, 2, h:h + 1])
                        nc.scalar.activation(soft[:, g, 4], soft[:, g, 3], ACT.Exp).then_inc(exp_ready, 1)
                elif stage == "W":
                    scale_shift(("mix", b, 1), lambda k: actT[:, k],
                                lambda k: col[:, COL_GOUT + k:COL_GOUT + k + 1], None, actT_act)
                    for half in range(2):
                        bank, turn = MM["y", b, half]
                        act.wait_ge(mm_full[bank], turn + 1)
                        last = nc.scalar.activation(junk[:, half * 512:(half + 1) * 512], mm[:, bank, :],
                                                    ACT.Square, accum_out=st[:, 4 + half:5 + half])
                    last.then_inc(y_squared, 1)
                elif stage == "O":
                    for g in range(KVH):
                        bank, turn = TR["prob", b, g, 0]
                        act.wait_ge(tr_full[bank], turn + 1)
                        link(nc.scalar.activation(pT[:, 0], tr[:, bank, :].rearrange("p (h n) -> p h n", h=GROUP),
                                                  ACT.Copy))
                        act.sem_inc(tr_free[bank], 1)
                        act.sem_inc(pT_act, 1)
                    act.wait_ge(sgu_ready, b + 1)
                    link(nc.scalar.activation(junk[:, 512:1024], u_sb[:, b % 2], ACT.Square, accum_out=st[:, 11:12]))
                    act.wait_ge(att_ready, b + 1)
                    link(nc.scalar.activation(junk[:, 0:512], yn[:, 0:512], ACT.Square, accum_out=st[:, 10:11]))
                    act.sem_inc(mix_squared, 1)
                    act.wait_ge(mix_rs, b + 1)
                    nc.scalar.activation(yn[:, 0:512], yn[:, 0:512], ACT.Copy, scale=st[:, 2:3])
                    nc.scalar.activation(yn[:, 512:1024], u_sb[:, b % 2], ACT.Copy,
                                         scale=st[:, 3:4]).then_inc(mix_ready, 1)
                elif stage == "F":
                    act.wait_ge(x1_ready, b + 1)
                    nc.scalar.activation(junk, x_sb[:, b], ACT.Square, accum_out=st[:, 9:10]).then_inc(x1_squared, 1)
                    act.wait_ge(x1_rs, b + 1)
                    nc.scalar.activation(xn2, x_sb[:, b], ACT.Copy, scale=st[:, 8:9]).then_inc(xn2_ready, 1)
                    act.wait_ge(mod_ready, 4)
                    scale_shift(("ffn", b, 1), lambda k: h2T[:, b // 2, k, (b % 2) * P:(b % 2 + 1) * P],
                                lambda k: mod[:, 3 * KD + k:3 * KD + k + 1],
                                lambda k: mod[:, 2 * KD + k:2 * KD + k + 1], h2T_act)
                    act.dma_start(x1_dram[b], x_sb[:, b]).then_inc(x1_saved, 16)
                elif stage == "Q":
                    query(b)
                if (stage, b) == ("F", NB - 1):
                    act.sem_inc(mixer_act, 1)

            def h2_rows(b):
                for part in range(2):
                    bank, turn = TR["h2", b, part]
                    act.wait_ge(tr_full[bank], turn + 1)
                    link(nc.scalar.activation(h2[:, b % 2, part * 512:(part + 1) * 512], tr[:, bank, :], ACT.Copy))
                    act.sem_inc(tr_free[bank], 1)
                act.sem_inc(h2_ready, 1)

            act.wait_ge(x1_saved, 16 * NB)
            for b in range(DENSE_B, NB):
                h2_rows(b)
            act.wait_ge(best_d_ready, 1)
            nc.scalar.activation(best_d, best_d, ACT.Exp).then_inc(gate_exp_d, 1)

            def gate_softmax(unit):
                act.wait_ge(best_ready, unit + 1)
                nc.scalar.activation(gate_e[:], best_v[:], ACT.Exp, bias=gate_s[:, 0:1],
                                     accum_out=gate_s[:, 1:2]).then_inc(gate_exp, 1)

            def store_gates(half):
                if half:
                    act.wait_ge(weights_ready, half * HALF_T)
                with act.Fori(0, BATCHES // 2, 1) as i:
                    for side in range(2):
                        n = i * 2 + (side + half * BATCHES)
                        act.wait_ge(gate_full, n + 3)
                        nc.scalar.activation(
                            gate_mat[:, bass.ds(i * (2 * BATCH) + side * BATCH, BATCH)],
                            tr[:, side].rearrange("p (t i) -> p t i", t=BATCH), ACT.Copy).then_inc(gate_stored, 1)

            def tile_activations(unit, t):
                act.wait_ge(act_full, unit * TILES_UNIT + t + 1 + TRING)
                act.wait_ge(tile_done, unit * TILES_UNIT + t + 1)
                nc.scalar.activation(weights[:, t % TRING], mm[:, t % 2, 0:DT], ACT.Gelu).then_inc(tile_gelu, 1)

            def experts(unit, more):
                for part in range(PARTS):
                    tile_activations(unit, 2 * part)
                    act.wait_ge(down_free, unit * TOPK + (part + 2) * RING)
                    nc.scalar.activation(gelus[:, part], dots[:, part], ACT.Gelu).then_inc(gelu_ready, 1)
                    tile_activations(unit, 2 * part + 1)
                if more:
                    gate_softmax(unit + 1)

            gate_softmax(0)
            for b in range(GATHER_B):
                store_gates(b)
                with act.Fori(0, PH - 1, 1) as h:
                    experts(h + b * PH, True)
                experts(b * PH + PH - 1, b < GATHER_B - 1)
                act.wait_ge(y2_ready, b + 1)
                link(nc.scalar.activation(square_junk, acc[:, 0],
                                          ACT.Square, accum_out=fin[:, 0:1]))
                nc.scalar.activation(fin[:, 1:2], fin[:, 0:1], ACT.Sqrt, bias=eps_sb[:],
                                     scale=1.0 / D).then_inc(y2_rms, 1)
                act.wait_ge(out_ready, b + 1)
                act.dma_start(out[(DENSE_B + b) * P:(DENSE_B + b + 1) * P, :], acc[:, 1]).then_inc(out_done, 16)
                if b < GATHER_B - 1:
                    act.wait_ge(out_done, 16 * (b + 1))
                    act.dma_start(acc[:, 1], x1_dram[DENSE_B + b + 1]).then_inc(x1_back, 16)
            act.wait_ge(tile_done, TRING + TILES)
            for b in range(DENSE_B):
                for half in range(2):
                    last = nc.scalar.activation(dot_junk[:, b, half * 512:(half + 1) * 512], y_bank[b][half],
                                                ACT.Square, accum_out=soft_d[:, 0, 2 * b + half:2 * b + half + 1])
            last.then_inc(dense_squared, 1)
            act.wait_ge(dense_squared, 2)
            nc.scalar.activation(soft_d[:, 0, 6:8], soft_d[:, 0, 4:6], ACT.Sqrt, bias=eps_sb[:],
                                 scale=1.0 / D).then_inc(dense_rms, 1)

        @block.vector
        def _(dve):
            link = linker(dve, dve_chain)
            V = nc.vector
            link(V.memset(eps_sb[:], EPS))
            dve.wait_ge(consts_in, 16 * N_CONSTS)
            dve.wait_ge(c_ready, 1)
            V.tensor_copy(c_rows, c_act[:].unsqueeze(2).broadcast_to([P, KD, P])).then_inc(c_rows_ready, 1)
            link(V.tensor_tensor(wsT, wsT, causal.unsqueeze(1).broadcast_to([P, SGU_H, P]), ALU.mult))
            dve.sem_inc(wsT_ready, 1)

            def mean_square(squared, ready, n, source, target, width, count):
                dve.wait_ge(squared, n)
                V.tensor_scalar(target, source, 1.0 / count, EPS, ALU.mult, ALU.add).then_inc(ready, 1)

            def scale_shift(key, out_of, gain_of, shift_of, done):
                bank, turn = TR[key]
                dve.wait_ge(tr_full[bank], turn + 1)
                for j in range(4):
                    k = 4 * key[-1] + j
                    shift = shift_of(k) if shift_of else 0.0
                    last = V.tensor_scalar(out_of(k), tr[:, bank, j * P:(j + 1) * P], gain_of(k), shift,
                                           ALU.mult, ALU.add)
                link(last)
                dve.sem_inc(tr_free[bank], 1)
                dve.sem_inc(done, 1)

            def ada_col(v):
                bank, turn = MM["ada", v]
                dve.wait_ge(mm_full[bank], turn + 1)
                slot = {SH1: 0, SC1: 1, SH2: 2, SC2: 3}[v]
                m = mod[:, slot * KD:(slot + 1) * KD]
                link(V.tensor_tensor(m, mm[:, bank, 0:KD], col[:, COL_BADA + v * KD:COL_BADA + (v + 1) * KD], ALU.add))
                if v in (SC1, SC2):
                    g = COL_G1 if v == SC1 else COL_G2
                    link(V.scalar_tensor_tensor(m, m, 1.0, col[:, g:g + KD], ALU.add, ALU.mult))
                dve.sem_inc(mm_free[bank], 1)
                dve.sem_inc(mod_ready, 1)

            def ada_row(v, gain, factor):
                for half in range(2):
                    bank, turn = MM["ada", v, half]
                    cols_ = slice(half * 512, (half + 1) * 512)
                    dve.wait_ge(mm_full[bank], turn + 1)
                    link(V.tensor_tensor(gain[:, cols_], mm[:, bank, :], gain[:, cols_], ALU.add))
                    dve.sem_inc(mm_free[bank], 1)
                    link(V.tensor_tensor(gain[:, cols_], gain[:, cols_], factor[:, cols_], ALU.mult))

            def rope(src, out_lo_hi, heads, b):
                cos = rope_cs[:, 0, b].unsqueeze(1).broadcast_to([P, heads, HD])
                half = HD // 2
                a = rope_tmp[:, 0, 0:heads * HD].rearrange("p (h d) -> p h d", h=heads)
                c = rope_tmp[:, 1, 0:heads * HD].rearrange("p (h d) -> p h d", h=heads)
                V.tensor_tensor(a, src, cos, ALU.mult)
                for lo, hi in ((0, half), (half, 0)):
                    s = rope_cs[:, 1, b, lo:lo + half].unsqueeze(1).broadcast_to([P, heads, half])
                    last = V.tensor_tensor(c[:, :, lo:lo + half], src[:, :, hi:hi + half], s, ALU.mult)
                link(last)
                for o in out_lo_hi:
                    last = V.tensor_tensor(o, a, c, ALU.add)
                link(last)

            def top_keys(source):
                V.tensor_copy(key_s.rearrange("p a n -> p (a n)"), source)
                dve.drain()
                for p in range(2):
                    V.max(top_v[:, p, 0:8], key_s[:, p])
                dve.drain()
                for p in range(2):
                    V.max_index(top_i[:, p, 0:8], top_v[:, p, 0:8], key_s[:, p])
                    V.match_replace(key_s2[:, p], top_v[:, p, 0:8], key_s[:, p], REMOVED)
                dve.drain()
                for p in range(2):
                    V.max(top_v[:, p, 8:16], key_s2[:, p])
                dve.drain()
                for p in range(2):
                    V.max_index(top_i[:, p, 8:16], top_v[:, p, 8:16], key_s2[:, p])
                V.tensor_tensor(cand.rearrange("p (a c) -> p a c", a=TOPK),
                                top_v[:, 0].unsqueeze(2).broadcast_to([P, TOPK, TOPK]),
                                top_v[:, 1].unsqueeze(1).broadcast_to([P, TOPK, TOPK]), ALU.add)
                dve.drain()

            def top_sums(best, signal):
                V.tensor_copy(top_f[:], top_i[:])
                V.max(best[:, 0:8], cand)
                dve.drain()
                V.max_index(best_j[:, 0:8], best[:, 0:8], cand)
                V.match_replace(cand, best[:, 0:8], cand, REMOVED)
                V.tensor_scalar(gate_s[:, 0:1], best[:, 0:1], -1.0, None, ALU.mult)
                dve.drain()
                V.max(best[:, 8:16], cand)
                if signal:
                    dve.drain().then_inc(best_ready, 1)
                else:
                    dve.drain()
                V.max_index(best_j[:, 8:16], best[:, 8:16], cand)
                dve.drain()

            def chosen_keys(target):
                V.tensor_scalar(pos_u[:, 0], best_j[:], 4, None, ALU.logical_shift_right)
                V.tensor_scalar(pos_u[:, 1], best_j[:], TOPK - 1, None, ALU.bitwise_and)
                dve.drain()
                V.tensor_copy(pos_f[:], pos_u[:])
                dve.drain()
                V.tensor_tensor(onehot, iota[:, 0:TOPK].unsqueeze(1).broadcast_to([P, 2 * TOPK, TOPK]),
                                pos_f[:].rearrange("p a k -> p (a k)").unsqueeze(2).broadcast_to([P, 2 * TOPK, TOPK]),
                                ALU.is_equal)
                dve.drain()
                hot4 = onehot.rearrange("p (a k) j -> p a k j", a=2)
                V.tensor_tensor(hot4, hot4, top_f[:].unsqueeze(2).broadcast_to([P, 2, TOPK, TOPK]), ALU.mult)
                dve.drain()
                V.tensor_reduce(target, hot4, AX_X, ALU.add)
                dve.drain()

            def expert_numbers(unit):
                V.scalar_tensor_tensor(expert_f[:], sel[:, 0], float(NKEY), sel[:, 1], ALU.mult, ALU.add)
                dve.drain()
                V.tensor_copy(index[:, bass.ds(unit * TOPK, TOPK)], expert_f[:]).then_inc(index_ready, 1)

            def gate_values(unit):
                dve.wait_ge(gate_exp, unit + 1)
                V.reciprocal(gate_s[:, 2:3], gate_s[:, 1:2])
                dve.drain()
                V.tensor_scalar(gates[:, bass.ds(unit * TOPK, TOPK)], gate_e[:], gate_s[:, 2:3], None, ALU.mult)
                dve.drain()

            chosen4 = chosen.rearrange("p (a m) -> p a m", a=2)

            def top_dense(group):
                dve.wait_ge(scores_ready, group + 1)
                for head in (2 * group, 2 * group + 1):
                    for b in range(DENSE_B):
                        n = b * PH + head
                        top_keys(scores_d[:, n * 2 * P:(n + 1) * 2 * P])
                        top_sums(best_d[:, n], False)
                        chosen_keys(chosen4[:, :, n * TOPK:(n + 1) * TOPK])

            def dense_gates():
                u = DENSE_B * PH
                link(V.tensor_copy(soft_d[:, 0], best_d[:, :, 0]))
                V.tensor_tensor(best_d, best_d, soft_d[:, 0].unsqueeze(2).broadcast_to([P, u, TOPK]),
                                ALU.subtract).then_inc(best_d_ready, 1)
                dve.wait_ge(gate_exp_d, 1)
                link(V.tensor_reduce(soft_d[:, 0], best_d, AX_X, ALU.add))
                link(V.reciprocal(soft_d[:, 1], soft_d[:, 0]))
                V.tensor_tensor(gates_d.rearrange("p (u k) -> p u k", u=u), best_d,
                                soft_d[:, 1].unsqueeze(2).broadcast_to([P, u, TOPK]), ALU.mult
                                ).then_inc(chosen_ready, 1)

            for stage, b in steps():
                if stage == "N":
                    mean_square(x_squared, x_ms, b + 1, st[:, 1:2], st[:, 0:1], 1, D)
                elif stage == "ADA_COL":
                    ada_col(b)
                elif stage == "ADA_ROW" and b == GT1:
                    ada_row(b, gain1, yn)
                elif stage == "ADA_ROW":
                    dense_gates()
                    dve.wait_ge(gain2_in, 32)
                    ada_row(b, gain2, acc[:, 0])
                elif stage == "T":
                    scale_shift(("x", b, 0), lambda k: actT[:, k], lambda k: mod[:, KD + k:KD + k + 1],
                                lambda k: mod[:, k:k + 1], actT_dve)
                elif stage == "P":
                    bank, turn = MM["proj", b, 0]
                    dve.wait_ge(mm_full[bank], turn + 1)
                    rope(mm[:, bank, :].rearrange("p (h d) -> p h d", h=QH),
                         [q_rot.rearrange("p (h d) -> p h d", h=QH)], QH, b)
                    dve.sem_inc(mm_free[bank], 1)
                    bank, turn = MM["proj", b, 1]
                    dve.wait_ge(mm_full[bank], turn + 1)
                    V.tensor_copy(v_all[:, b], mm[:, bank, KV_W:2 * KV_W])
                    rope(mm[:, bank, 0:KV_W].rearrange("p (h d) -> p h d", h=KVH),
                         [k_dup[:, :, r] for r in range(2)], KVH, b)
                    dve.sem_inc(mm_free[bank], 1)
                    dve.sem_inc(rope_ready, 1)
                elif stage == "LN":
                    dve.wait_ge(vg_ready, b + 1)
                    v3 = vg.rearrange("p (h d) -> p h d", h=SGU_H)
                    d3 = ln_d.rearrange("p (h d) -> p h d", h=SGU_H)
                    n3 = vn.rearrange("p (h d) -> p h d", h=SGU_H)
                    link(V.tensor_reduce(stat[:, 0], v3, AX_X, ALU.add))
                    link(V.tensor_scalar(stat[:, 1], stat[:, 0], 1.0 / HD, None, ALU.mult))
                    link(V.tensor_tensor(d3, v3, stat[:, 1].unsqueeze(2).broadcast_to([P, SGU_H, HD]), ALU.subtract))
                    dve.sem_inc(vg_used, 1)
                    link(V.tensor_tensor(n3, d3, d3, ALU.mult))
                    link(V.tensor_reduce(stat[:, 2], n3, AX_X, ALU.add))
                    V.tensor_scalar(stat[:, 3], stat[:, 2], 1.0 / HD, EPS, ALU.mult, ALU.add).then_inc(var_ready, 1)
                    dve.wait_ge(var_rs, b + 1)
                    link(V.tensor_tensor(n3, d3, stat[:, 3].unsqueeze(2).broadcast_to([P, SGU_H, HD]), ALU.mult))
                    link(V.tensor_tensor(vn, vn, ln_rows[:, 0], ALU.mult))
                    V.tensor_tensor(vn, vn, ln_rows[:, 1], ALU.add).then_inc(vn_ready, 1)
                elif stage == "S1":
                    bank, turn = TR["q", b]
                    dve.wait_ge(tr_full[bank], turn + 1)
                    link(V.tensor_copy(qT.rearrange("p a n -> p (a n)"), tr[:, bank, :]))
                    dve.sem_inc(tr_free[bank], 1)
                    dve.sem_inc(qT_ready, 1)
                elif stage == "S2":
                    for g in range(KVH):
                        dve.wait_ge(sc_full, 2 * b + g + 1)
                        s3 = probs[g].rearrange("p (h n) -> p h n", h=GROUP)
                        first = 0 if b else P
                        if b == 0:
                            V.memset(s3[:, :, 0:P], MASKED)
                        link(V.scalar_tensor_tensor(
                            s3[:, :, first:], sc[:].rearrange("p a (c n) -> p (a c) n", c=2)[:, :, first:],
                            HD ** -0.5, mask_sb[:, first:].unsqueeze(1).broadcast_to([P, GROUP, 2 * P - first]),
                            ALU.mult, ALU.add))
                        dve.sem_inc(sc_free, 1)
                        t = soft[:, g]
                        sk = sink_sb[:, g * GROUP:(g + 1) * GROUP]
                        link(V.tensor_reduce(t[:, 0], s3, AX_X, ALU.max))
                        link(V.tensor_tensor(t[:, 0], t[:, 0], sk, ALU.max))
                        V.tensor_scalar(t[:, 1], t[:, 0], -1.0, None, ALU.mult)
                        link(V.tensor_tensor(t[:, 3], sk, t[:, 0], ALU.subtract))
                        dve.sem_inc(bias_ready, 1)
                elif stage == "G":
                    dve.wait_ge(sgu_full, b + 1)
                    dve.wait_ge(u_ready, b + 1)
                    o3 = ln_d.rearrange("p (h d) -> p h d", h=SGU_H)
                    link(V.tensor_tensor(o3, sgu_ps[:].rearrange("p (h d) -> p h d", h=SGU_H),
                                         bs_sb[:].unsqueeze(2).broadcast_to([P, SGU_H, HD]), ALU.add))
                    dve.sem_inc(sgu_free, 1)
                    V.tensor_tensor(u_sb[:, b % 2], ln_d, u_sb[:, b % 2], ALU.mult).then_inc(sgu_ready, 1)
                    dve.wait_ge(sgu_ready, b + 1)
                elif stage == "W":
                    scale_shift(("mix", b, 0), lambda k: actT[:, k],
                                lambda k: col[:, COL_GOUT + k:COL_GOUT + k + 1], None, actT_dve)
                    dve.wait_ge(y_squared, b + 1)
                    link(V.tensor_tensor(st[:, 7:8], st[:, 4:5], st[:, 5:6], ALU.add))
                    V.tensor_scalar(st[:, 6:7], st[:, 7:8], 1.0 / D, EPS, ALU.mult, ALU.add).then_inc(y_ms, 1)
                    dve.wait_ge(y_rs, b + 1)
                    for half in range(2):
                        bank, turn = MM["y", b, half]
                        c_ = slice(half * 512, (half + 1) * 512)
                        dve.wait_ge(mm_full[bank], turn + 1)
                        link(V.scalar_tensor_tensor(xn2[:, c_], mm[:, bank, :], st[:, 6:7], gain1[:, c_],
                                                    ALU.mult, ALU.mult))
                        dve.sem_inc(mm_free[bank], 1)
                    V.tensor_tensor(x_sb[:, b], x_sb[:, b], xn2, ALU.add).then_inc(x1_ready, 1)
                elif stage == "O":
                    for g in range(KVH):
                        bank, turn = TR["prob", b, g, 1]
                        dve.wait_ge(tr_full[bank], turn + 1)
                        link(V.tensor_copy(pT[:, 1].rearrange("p h n -> p (h n)"), tr[:, bank, :]))
                        dve.sem_inc(tr_free[bank], 1)
                        dve.sem_inc(pT_dve, 1)
                        t = soft[:, g]
                        dve.wait_ge(exp_ready, 2 * b + g + 1)
                        link(V.tensor_tensor(t[:, 5], t[:, 2], t[:, 4], ALU.add))
                        link(V.reciprocal(t[:, 5], t[:, 5]))
                    dve.wait_ge(att_full, b + 1)
                    for g in range(KVH):
                        a_ = slice(g * GROUP * HD, (g + 1) * GROUP * HD)
                        last = V.tensor_tensor(
                            yn[:, a_].rearrange("p (c o d) -> p o c d", o=2, c=2),
                            att_ps[:, a_].rearrange("p (o c d) -> p o c d", o=2, c=2),
                            soft[:, g, 5].rearrange("p (o c) -> p o c", o=2).unsqueeze(3).broadcast_to([P, 2, 2, HD]),
                            ALU.mult)
                    link(last)
                    dve.sem_inc(att_free, 1)
                    dve.sem_inc(att_ready, 1)
                    mean_square(mix_squared, mix_ms, b + 1, st[:, 10:12], st[:, 2:4], 2, SGU_W)
                elif stage == "F":
                    mean_square(x1_squared, x1_ms, b + 1, st[:, 9:10], st[:, 8:9], 1, D)
                    scale_shift(("ffn", b, 0), lambda k: h2T[:, b // 2, k, (b % 2) * P:(b % 2 + 1) * P],
                                lambda k: mod[:, 3 * KD + k:3 * KD + k + 1],
                                lambda k: mod[:, 2 * KD + k:2 * KD + k + 1], h2T_dve)
                elif stage == "TK":
                    top_dense(b)
                if (stage, b) == ("F", NB - 1):
                    dve.sem_inc(mixer_dve, 1)
                    dve.wait_ge(mixer_pe, 1)
                    dve.wait_ge(mixer_act, 1)
                    V.tensor_copy(c_rows2, c_act[:].unsqueeze(2).broadcast_to([P, KD, P])).then_inc(c_rows_ready, 1)


            def transposed_gates():
                for n, (target, width) in enumerate(((chosen, 4 * P), (gates_d, 2 * P))):
                    bank, turn = TR["onehot", n]
                    dve.wait_ge(tr_full[bank], turn + 1)
                    link(V.tensor_copy(target, tr[:, bank, 0:width]))
                    dve.sem_inc(tr_free[bank], 1)

            def one_hot_rows(half):
                with dve.Fori(0, BATCHES // 2, 1) as i:
                    for side in range(2):
                        n = i * 2 + (side + half * BATCHES)
                        t0 = i * (2 * BATCH) + side * BATCH
                        dve.wait_ge(gate_full, n + 1)
                        V.tensor_tensor(hot_i[:, side],
                                        iota[:, half * HALF_T:(half + 1) * HALF_T].unsqueeze(1)
                                        .broadcast_to([P, BATCH, HALF_T]),
                                        chosen[:, bass.ds(t0, BATCH)].unsqueeze(2).broadcast_to([P, BATCH, HALF_T]),
                                        ALU.is_equal)
                        for t in range(BATCH):
                            V.tensor_scalar(hot_j[:, side, t], iota[:], chosen[:, bass.ds(t0 + (DT + t), 1)],
                                            gates_d[:, bass.ds(t0 + t, 1)], ALU.is_equal, ALU.mult)
                        dve.drain().then_inc(hot_ready, 1)

            def dot_products(unit, b, part):
                for r in range(RING):
                    dve.wait_ge(down_in[r], unit * (16 * PARTS) + 16 * (part + 1))
                    dve.wait_ge(down_free, unit * TOPK + (part + 1) * RING + r - 1)
                    V.tensor_tensor_reduce(out=dot_junk[:, r % 2], in0=down_ring[:, r], in1=h2[:, b],
                                           scale=1.0, scalar=0.0, op0=ALU.mult, op1=ALU.add,
                                           accum_out=dots[:, part, r:r + 1]).then_inc(down_free, 1)

            def weighted_rows(unit, part):
                dve.wait_ge(gelu_ready, unit * PARTS + part + 1)
                V.tensor_tensor(coef[:, part], gelus[:, part],
                                gates[:, bass.ds(unit * TOPK + part * RING, RING)], ALU.mult)
                dve.drain()
                for r in range(RING):
                    dve.wait_ge(up_in[r], unit * (16 * PARTS) + 16 * (part + 1))
                    dve.wait_ge(up_free, unit * TOPK + (part + 1) * RING + r)
                    V.scalar_tensor_tensor(acc[:, 0], up_ring[:, r], coef[:, part, r:r + 1], acc[:, 0],
                                           ALU.mult, ALU.add).then_inc(up_free, 1)

            def tile_weights(unit, h, t):
                dve.wait_ge(tile_gelu, unit * TILES_UNIT + t + 1)
                V.tensor_tensor(weights[:, t % TRING], weights[:, t % TRING],
                                gate_mat[:, :, bass.ds(h * TILES_UNIT + t, 1)].rearrange("p t o -> p (t o)"),
                                ALU.mult).then_inc(weights_ready, 1)

            def experts(b, h, more):
                unit = h + b * PH
                for part in range(PARTS):
                    dot_products(unit, b, part)
                    tile_weights(unit, h, 2 * part)
                    if more and part == 0:
                        top_keys(scores[:, bass.ds((unit + 1) * (2 * P), 2 * P)])
                    if more and part == 1:
                        top_sums(best_v, True)
                    if more and part == 2:
                        chosen_keys(sel[:])
                        expert_numbers(unit + 1)
                    weighted_rows(unit, part)
                    tile_weights(unit, h, 2 * part + 1)
                if more:
                    gate_values(unit + 1)

            dve.sem_inc(down_free, RING)
            dve.sem_inc(up_free, RING)
            dve.wait_ge(scores_ready, 8)
            top_keys(scores[:, 0:2 * P])
            top_sums(best_v, True)
            chosen_keys(sel[:])
            expert_numbers(0)
            gate_values(0)
            transposed_gates()
            link(V.memset(zeros, 0.0))
            for b in range(GATHER_B):
                one_hot_rows(b)
                link(V.memset(acc[:, 0], 0.0))
                dve.wait_ge(h2_ready, b + 1)
                dve.wait_ge(gate_stored, 2 + (b + 1) * BATCHES)
                with dve.Fori(0, PH - 1, 1) as h:
                    experts(b, h, True)
                experts(b, PH - 1, b < GATHER_B - 1)
                dve.drain().then_inc(y2_ready, 1)
                dve.wait_ge(y2_rms, b + 1)
                link(V.reciprocal(fin[:, 2:3], fin[:, 1:2]))
                link(V.scalar_tensor_tensor(acc[:, 0], acc[:, 0], fin[:, 2:3], gain2, ALU.mult, ALU.mult))
                dve.wait_ge(x1_back, 16 * (b + 1))
                V.tensor_tensor(acc[:, 1], acc[:, 1], acc[:, 0], ALU.add).then_inc(out_ready, 1)
                dve.wait_ge(out_ready, b + 1)
            dve.wait_ge(dense_squared, 1)
            s4 = soft_d[:, 0, 0:4].rearrange("p (b h) -> p b h", b=DENSE_B)
            V.tensor_tensor(soft_d[:, 0, 4:6], s4[:, :, 0], s4[:, :, 1], ALU.add).then_inc(dense_squared, 1)
            dve.wait_ge(dense_rms, 1)
            link(V.reciprocal(soft_d[:, 0, 8:10], soft_d[:, 0, 6:8]))
            dve.wait_ge(x1_dense_in, 16 * DENSE_B)
            for b in range(DENSE_B):
                for half in range(2):
                    c_ = slice(half * 512, (half + 1) * 512)
                    last = V.scalar_tensor_tensor(down_ring[:, b, c_], y_bank[b][half],
                                                  soft_d[:, 0, 8 + b:9 + b], gain2[:, c_], ALU.mult, ALU.mult)
                link(last)
                V.tensor_tensor(x1_dense[:, b], x1_dense[:, b], down_ring[:, b], ALU.add).then_inc(dense_out, 1)

        @block.tensor
        def _(pe):
            T = nc.tensor
            chunks = [0]
            n_actT = [0]

            def fill(uses, free, key):
                bank, turn = uses[key]
                if turn:
                    pe.wait_ge(free[bank], turn)
                return bank

            def chunk():
                n = chunks[0]
                pe.wait_ge(chunk_in[n % WRING], 16 * (n // WRING + 1))
                return wring[:, n % WRING]

            def chunk_through():
                chunks[0] += 1

            def transpose4(key, source):
                bank = fill(TR, tr_free, key)
                for j in range(4):
                    last = T.transpose(tr[:, bank, j * P:(j + 1) * P], source(j), ident[:])
                last.then_inc(tr_full[bank], 1)

            def actT_in():
                n_actT[0] += 1
                pe.wait_ge(actT_dve, n_actT[0])
                pe.wait_ge(actT_act, n_actT[0])

            def last_chunk_used(bank, turn):
                pe.wait_ge(mm_full[bank], turn + 1)
                pe.sem_inc(chunk_used, 1)

            def query(group):
                half, g = group // 4, group % 4
                if g == 0:
                    pe.wait_ge(h2T_dve, DENSE_B if half == 0 else NB)
                    pe.wait_ge(h2T_act, DENSE_B if half == 0 else NB)
                    pe.wait_ge(keys_in, 16)
                for j in range(4):
                    key = ("query", 4 * group + j)
                    bank = fill(MM, mm_free, key)
                    w = chunk()
                    for k in range(KD):
                        last = T.matmul(mm[:, bank, 0:2 * P], w[:, k], h2T[:, half, k], start=(k == 0), stop=(k == KD - 1))
                    last.then_inc(mm_full[bank], 1)
                    last_chunk_used(bank, MM[key][1])
                    chunk_through()
                pe.wait_ge(qhT_ready, group + 1)
                for tb in range(2):
                    bank = fill(MM, mm_free, ("score", group, tb))
                    for j in range(4):
                        last = T.matmul(mm[:, bank, j * P:(j + 1) * P], qhT[:, group % 2, j, tb * P:(tb + 1) * P],
                                        keys_sb[:, 4 * g + j], start=True, stop=True)
                    last.then_inc(mm_full[bank], 1)

            pe.wait_ge(consts_in, 16 * N_CONSTS)
            for stage, b in steps():
                if stage == "ADA_COL":
                    if b == SH1:
                        pe.wait_ge(c_ready, 1)
                    bank = fill(MM, mm_free, ("ada", b))
                    for m in range(KD):
                        w = chunk()
                        for k in range(KD):
                            last = T.matmul(mm[:, bank, m:m + 1], w[:, k], c_act[:, k:k + 1],
                                            start=(k == 0), stop=(k == KD - 1))
                        if m < KD - 1:
                            last.then_inc(chunk_used, 1)
                        else:
                            last.then_inc(mm_full[bank], 1)
                            last_chunk_used(bank, MM["ada", b][1])
                        chunk_through()
                elif stage == "ADA_ROW":
                    pe.wait_ge(c_rows_ready, 1 if b == GT1 else 2)
                    left = c_rows if b == GT1 else c_rows2
                    for half in range(2):
                        bank = fill(MM, mm_free, ("ada", b, half))
                        for m in range(4):
                            w = chunk()
                            for k in range(KD):
                                last = T.matmul(mm[:, bank, m * P:(m + 1) * P], left[:, k], w[:, k],
                                                start=(k == 0), stop=(k == KD - 1))
                            if m < 3:
                                last.then_inc(chunk_used, 1)
                            else:
                                last.then_inc(mm_full[bank], 1)
                                last_chunk_used(bank, MM["ada", b, half][1])
                            chunk_through()
                elif stage == "T":
                    pe.wait_ge(xn_ready, b + 1)
                    for half in range(2):
                        transpose4(("x", b, half), lambda j: xn[:, (4 * half + j) * P:(4 * half + j + 1) * P])
                elif stage == "P":
                    actT_in()
                    for c, (first, n) in enumerate(PROJ):
                        if b == 0:
                            pe.wait_ge(win_in[c], 16)
                        bank = fill(MM, mm_free, ("proj", b, c))
                        for k in range(KD):
                            last = T.matmul(mm[:, bank, 0:n], actT[:, k], win_sb[:, k, first:first + n],
                                            start=(k == 0), stop=(k == KD - 1))
                        last.then_inc(mm_full[bank], 1)
                elif stage == "S1":
                    pe.wait_ge(rope_ready, b + 1)
                    transpose4(("q", b), lambda j: q_rot[:, j * P:(j + 1) * P])
                    bank = fill(TR, tr_free, ("k", b))
                    for g in range(KVH):
                        last = T.transpose(tr[:, bank, g * P:(g + 1) * P],
                                           k_dup[:, g].rearrange("p r d -> p (r d)"), ident[:])
                    last.then_inc(tr_full[bank], 1)
                elif stage == "S2":
                    pe.wait_ge(qT_ready, b + 1)
                    pe.wait_ge(kT_ready, b + 1)
                    first = max(b - 1, 0)
                    off = 0 if b else P
                    for g in range(KVH):
                        if 2 * b + g:
                            pe.wait_ge(sc_free, 2 * b + g)
                        for h in range(GROUP):
                            head = g * GROUP + h
                            rows_ = slice(HD * (head % 2), HD * (head % 2) + HD)
                            last = T.matmul(sc[:, h % 2, (h // 2) * 2 * P + off:(h // 2 + 1) * 2 * P],
                                            qT[rows_, head // 2], kT[rows_, g, first * P:(b + 1) * P],
                                            start=True, stop=True)
                        last.then_inc(sc_full, 1)
                elif stage == "G":
                    pe.wait_ge(vn_ready, b + 1)
                    if b == 0:
                        pe.wait_ge(wsT_ready, 1)
                    else:
                        pe.wait_ge(sgu_free, b)
                    for h in range(SGU_H):
                        last = T.matmul(sgu_ps[:, h * HD:(h + 1) * HD], wsT[:, h], vn[:, h * HD:(h + 1) * HD],
                                        start=True, stop=True)
                    last.then_inc(sgu_full, 1)
                elif stage == "W":
                    pe.wait_ge(mix_ready, b + 1)
                    for half in range(2):
                        transpose4(("mix", b, half), lambda j: yn[:, (4 * half + j) * P:(4 * half + j + 1) * P])
                    actT_in()
                    pe.wait_ge(wout_in, 16)
                    for half in range(2):
                        bank = fill(MM, mm_free, ("y", b, half))
                        for k in range(KD):
                            last = T.matmul(mm[:, bank, :], actT[:, k], wout_sb[:, k, half * 512:(half + 1) * 512],
                                            start=(k == 0), stop=(k == KD - 1))
                        last.then_inc(mm_full[bank], 1)
                elif stage == "O":
                    for g in range(KVH):
                        pe.wait_ge(exp_ready, 2 * b + g + 1)
                        for j in range(2):
                            transpose4(("prob", b, g, j),
                                       lambda h: probs[g][:, (2 * h + j) * P:(2 * h + j + 1) * P])
                        pe.wait_ge(pT_act, 2 * b + g + 1)
                        pe.wait_ge(pT_dve, 2 * b + g + 1)
                        if g == 0 and b:
                            pe.wait_ge(att_free, b)
                        for h in range(GROUP):
                            head = g * GROUP + h
                            for j in range(2):
                                last = T.matmul(att_ps[:, head * HD:(head + 1) * HD], pT[:, j, h],
                                                v_all[:, max(b - 1 + j, 0), g * HD:(g + 1) * HD],
                                                start=(j == 0), stop=(j == 1))
                    last.then_inc(att_full, 1)
                elif stage == "F":
                    pe.wait_ge(xn2_ready, b + 1)
                    for half in range(2):
                        transpose4(("ffn", b, half), lambda j: xn2[:, (4 * half + j) * P:(4 * half + j + 1) * P])
                elif stage == "Q":
                    query(b)
                if (stage, b) == ("F", NB - 1):
                    bank, turn = TR["ffn", NB - 1, 1]
                    pe.wait_ge(tr_full[bank], turn + 1)
                    pe.sem_inc(mixer_pe, 1)

            def gate_matrix(half):
                with pe.Fori(0, BATCHES // 2, 1) as i:
                    for side in range(2):
                        n = i * 2 + (side + half * BATCHES)
                        pe.wait_ge(hot_ready, n + 1)
                        pe.wait_ge(gate_stored, n + 1)
                        for t in range(BATCH):
                            last = T.matmul(tr[:, side, t * HALF_T:(t + 1) * HALF_T], hot_j[:, side, t],
                                            hot_i[:, side, t], start=True, stop=True)
                        last.then_inc(gate_full, 1)

            def tile_products(slot, arrived, bank):
                pe.wait_ge(tile_down_in[slot], arrived)
                for k in range(KD):
                    last = T.matmul(mm[:, bank, 0:DT], tile_down[slot][:, k], h2T[:, 0, k],
                                    start=(k == 0), stop=(k == KD - 1))
                last.then_inc(act_full, 1)

            def tile_sums(unit, t):
                slot = t % TRING
                pe.wait_ge(weights_ready, unit * TILES_UNIT + t + 1)
                pe.wait_ge(tile_up_in[slot], unit * (16 * TILES_UNIT // TRING) + 16 * (t // TRING + 1))
                for b in range(DENSE_B):
                    for half in range(2):
                        last = T.matmul(y_bank[b][half], weights[:, slot, b * P:(b + 1) * P],
                                        tile_up[slot][:, half * 512:(half + 1) * 512], start=False, stop=False,
                                        skip_group_check=True)
                last.then_inc(tile_done, 1)

            def experts(unit, ahead):
                for t in range(TILES_UNIT):
                    if t < ahead:
                        pe.wait_ge(tile_gelu, unit * TILES_UNIT + t + 1)
                        nxt = t + 2
                        tile_products(nxt % TRING,
                                      unit * (16 * TILES_UNIT // TRING) + 16 * (nxt // TRING + 1), t % 2)
                    tile_sums(unit, t)

            for b in range(DENSE_B, NB):
                for part in range(2):
                    transpose4(("h2", b, part), lambda j: h2T[:, 1, 4 * part + j, (b % 2) * P:(b % 2 + 1) * P])
            bank, turn = TR["h2", NB - 1, 1]
            pe.wait_ge(tr_full[bank], turn + 1)
            pe.sem_inc(h2T_used, 1)
            pe.sem_inc(act_full, TRING)
            pe.sem_inc(tile_done, TRING)
            pe.wait_ge(chosen_ready, 1)
            transpose4(("onehot", 0), lambda j: chosen[:, j * P:(j + 1) * P])
            bank = fill(TR, tr_free, ("onehot", 1))
            for j in range(2):
                last = T.transpose(tr[:, bank, j * P:(j + 1) * P], gates_d[:, j * P:(j + 1) * P], ident[:])
            last.then_inc(tr_full[bank], 1)
            for n in range(2):
                bank, turn = TR["onehot", n]
                pe.wait_ge(tr_free[bank], turn + 1)
            for bank in range(2):
                pe.wait_ge(mm_free[bank], len([1 for b_, _ in MM.values() if b_ == bank]))
            pe.wait_ge(sc_free, KVH * NB)
            pe.wait_ge(att_free, NB)
            pe.wait_ge(sgu_free, NB)
            pe.sem_inc(gate_full, 2)
            pe.sem_inc(gate_stored, 2)
            gate_matrix(0)
            for b in range(DENSE_B):
                for half in range(2):
                    T.matmul(y_bank[b][half], zeros, h2T[:, 0, 0:2].rearrange("p k n -> p (k n)"),
                             start=True, stop=False, skip_group_check=True)
            for n in range(2):
                tile_products(n, 16, n)
            for b in range(GATHER_B):
                if b:
                    gate_matrix(b)
                with pe.Fori(0, PH - 1, 1) as h:
                    experts(h + b * PH, TILES_UNIT)
                experts(b * PH + PH - 1, TILES_UNIT if b < GATHER_B - 1 else TILES_UNIT - 2)


def kernel(x, c, w_ada, b_ada, g_pre_mix, g_post_mix, g_pre_ffn, g_post_ffn, w_in, w_s, b_s, sgu_ln_g,
           sgu_ln_b, sinks, g_att_out, g_sgu_out, w_out, w_query, sub_keys, expert_down, expert_up):
    import concourse.bacc as bacc
    from concourse.bass_utils import run_bass_kernel_spmd

    f = lambda a: np.ascontiguousarray(np.asarray(a))

    def columns(v):
        return f(v).reshape(-1, P).T

    def chunks(w):
        w = f(w)
        return np.ascontiguousarray(w.reshape(KD, P, -1, P).transpose(2, 1, 0, 3))

    half = HD // 2
    inv = np.float32(10000.0) ** (-np.arange(half, dtype=np.float32) / np.float32(half))
    ang = np.arange(SEQ, dtype=np.float32)[:, None] * inv[None, :]
    cos, sin = np.cos(ang), np.sin(ang)
    by_block = lambda t: np.ascontiguousarray(t.reshape(NB, P, HD).transpose(1, 0, 2), dtype=np.float32)
    q, s = np.arange(P)[:, None], np.arange(P)[None, :]
    masks = np.concatenate([
        (q <= s).astype(np.float32),
        np.where(s > q, 0.0, MASKED).astype(np.float32),
        np.where(s <= q, 0.0, MASKED).astype(np.float32),
    ], axis=1)

    mod_rows = f(b_ada)[0].reshape(6, D)
    arrays = {
        "x": f(x)[0],
        "cols": np.ascontiguousarray(np.concatenate([
            columns(f(c)[0]), columns(f(b_ada)[0]), columns(f(g_pre_mix)[0]), columns(f(g_pre_ffn)[0]),
            columns(f(g_att_out)[0]), columns(f(g_sgu_out)[0])], axis=1)),
        "rows": np.concatenate([mod_rows[GT1], f(g_post_mix)[0], mod_rows[GT2], f(g_post_ffn)[0],
                                f(sgu_ln_g)[0].reshape(-1), f(sgu_ln_b)[0].reshape(-1)]),
        "w_ada": chunks(f(w_ada)[0]),
        "w_in": f(w_in)[0],
        "w_s": np.ascontiguousarray(f(w_s)[0].transpose(2, 0, 1)),
        "b_s": np.ascontiguousarray(f(b_s)[0].T),
        "sinks": np.ascontiguousarray(f(sinks)[0].reshape(KVH, 2, 2).transpose(0, 2, 1).reshape(-1)),
        "w_out": f(w_out)[0],
        "w_query": chunks(f(w_query)[0]),
        "keys": np.ascontiguousarray(f(sub_keys)[0].reshape(HP, NKEY, P).transpose(2, 0, 1)),
        "down": f(expert_down)[0],
        "up": f(expert_up)[0],
        "down_tiles": np.ascontiguousarray(f(expert_down)[0].reshape(TILES, P, KD, P).transpose(0, 3, 2, 1)),
        "cos_tab": by_block(np.concatenate([cos, cos], axis=1)),
        "sin_tab": by_block(np.concatenate([-sin, sin], axis=1)),
        "masks": masks,
        "ident_in": np.eye(P, dtype=np.float32),
        "iota_in": np.ascontiguousarray(np.broadcast_to(np.arange(P, dtype=np.float32), (P, P))),
    }
    nc = bacc.Bacc("TRN2", target_bir_lowering=False, num_devices=1)
    aps = [nc.dram_tensor(f"in_{n}", a.shape, mybir.dt.from_np(a.dtype), kind="ExternalInput").ap()
           for n, a in arrays.items()]
    out = nc.dram_tensor("out_0", (SEQ, D), F32, kind="ExternalOutput").ap()
    hybrid_block(nc, *aps, out)
    r = run_bass_kernel_spmd(nc, [{f"in_{n}": a for n, a in arrays.items()}], core_ids=[0])
    return r.results[0]["out_0"].reshape(1, SEQ, D)
```

```python
from contextlib import ExitStack

import numpy as np

import concourse.bass as bass
from concourse import mybir
from concourse.alu_op_type import AluOpType as ALU

F32 = mybir.dt.float32
BF16 = mybir.dt.bfloat16
U32 = mybir.dt.uint32
ACT = mybir.ActivationFunctionType
AX_X = mybir.AxisListType.X

P = 128
D, SEQ = 1024, 512
NB = SEQ // P
KD = D // P
HD = 64
QH, KVH = 8, 2
GROUP = QH // KVH
SGU_H = 8
ATT_W, KV_W, SGU_W = QH * HD, KVH * HD, SGU_H * HD
IN_COLS = ATT_W + 2 * KV_W + 2 * SGU_W
PROJ = [(0, ATT_W), (ATT_W, 2 * KV_W), (ATT_W + 2 * KV_W, SGU_W), (ATT_W + 2 * KV_W + SGU_W, SGU_W)]
PH, TOPK, NKEY = 8, 16, 128
HP = PH * 2
DENSE_B = 2
DT = DENSE_B * P
GATHER_B = NB - DENSE_B
UNITS = GATHER_B * PH
TILES = NKEY
TILES_UNIT = TILES // UNITS
QUARTERS = 4
QUNITS = UNITS // QUARTERS
QT = TILES // QUARTERS
GT2_PIECES = 4
BATCH = 8
SHARE = 5
BATCHES = DT // BATCH
assert BATCHES == QUNITS * TILES_UNIT
TRING = 4
EPS = 1e-6
MASKED = -1e30
REMOVED = -3e38
RING = 4
PARTS = TOPK // RING
WRING = 6
ADA_CHUNKS = 6 * KD
SH1, SC1, GT1, SH2, SC2, GT2 = range(6)
COL_C, COL_BADA, COL_G1, COL_G2, COL_GOUT, N_COLS = 0, 8, 56, 64, 72, 80

TK_IN_W = {NB - 2: (0, 1), NB - 1: (4, 5)}


def steps():
    out = [("N", 0), ("ADA_COL", SH1), ("ADA_COL", SC1)]
    for s in range(NB):
        out.append(("T", s))
        if s >= 3:
            out.append(("F1", s - 3))
        if s >= 1:
            out.append(("S1", s - 1))
        if s >= 3:
            out.append(("F2", s - 3))
        if s + 1 < NB:
            out.append(("N", s + 1))
        if s >= 1:
            out.append(("LN", s - 1))
        out.append(("P", s))
        if s == 0:
            out.append(("ADA_ROW", GT1))
        if s == 1:
            out += [("ADA_COL", SH2), ("ADA_COL", SC2)]
        if s >= 1:
            out += [("S2", s - 1), ("G", s - 1)]
        if s >= 2:
            out.append(("W", s - 2))
        if s >= 1:
            out.append(("O", s - 1))
        if s >= 2:
            out.append(("W2", s - 2))
    a, z = NB - 2, NB - 1
    out += [("F1", a - 1), ("S1", z), ("F2", a - 1), ("Q", 0), ("LN", z), ("S2", z), ("G", z), ("W", a), ("O", z),
            ("W2", a), ("F1", a), ("TK", 2), ("Q", 1), ("TK", 3), ("F2", a), ("W", z), ("W2", z), ("F1", z),
            ("Q", 2), ("TK", 6), ("F2", z), ("Q", 3)] + [("TK", n) for n in range(7, DENSE_B * PH)]
    out += [("Q", 4 + g) for g in range(4)] + [("TURN", 0), ("ADA_ROW", GT2)]
    return out


def bank_turns(names):
    return {name: (n % 2, n // 2) for n, name in enumerate(names)}


def matmul_uses():
    out = []
    for stage, b in steps():
        if stage in ("ADA_COL", "ADA_ROW"):
            out += [("ada", b, half) for half in range(2)]
        elif stage == "P":
            out += [("proj", b, c) for c in range(len(PROJ))]
        elif stage == "W":
            out += [("y", b, half) for half in range(2)]
        elif stage == "Q":
            out += [("query", 4 * b + j) for j in range(4)] + [("score", b, tb) for tb in range(2)]
    return bank_turns(out)


def chunk_signals(mm_uses):
    out, counted = [], 0
    for stage, b in steps():
        if stage in ("ADA_COL", "ADA_ROW"):
            for half in range(2):
                for m in range(4):
                    if m < 3:
                        counted += 1
                        out.append((None, counted))
                    else:
                        out.append(mm_uses["ada", b, half])
        elif stage == "Q":
            out += [mm_uses["query", 4 * b + j] for j in range(4)]
    return out


def transpose_uses():
    out = []
    for stage, b in steps():
        if stage == "T":
            out += [("x", b, half) for half in range(2)]
        elif stage == "S1":
            out += [("q", b), ("k", b)]
        elif stage == "O":
            out += [("prob", b, g, j) for g in range(KVH) for j in range(2)]
        elif stage == "W":
            out += [("mix", b, half) for half in range(2)]
        elif stage == "F2":
            out += [("ffn", b, half) for half in range(2)]
    out += [("h2", b, half) for b in range(DENSE_B, NB) for half in range(2)]
    out += [("onehot", 0), ("onehot", 1)]
    return bank_turns(out)


def hybrid_block(nc, x, cols, rows, w_ada, w_in, w_s, b_s, sinks, w_out, w_query, keys, down, up,
                 down_tiles, cos_tab, sin_tab, masks, ident_in, iota_in, out):
    MM, TR = matmul_uses(), transpose_uses()
    x1_dram = nc.dram_tensor("x1_kept", (NB, P, D), F32, kind="Internal").ap()
    with ExitStack() as ctx:
        def sb(name, shape, dt=F32):
            return ctx.enter_context(nc.sbuf_tensor(name, shape, dt))

        def psum(name, shape):
            return ctx.enter_context(nc.psum_tensor(name, shape, F32))

        def sem(name):
            return ctx.enter_context(nc.semaphore(name))

        W = sb("W", [P, KD * IN_COLS + KD * D])
        win_sb = W[:, 0:KD * IN_COLS].rearrange("p (k n) -> p k n", k=KD)
        wout_sb = W[:, KD * IN_COLS:KD * (IN_COLS + D)].rearrange("p (k n) -> p k n", k=KD)
        w_at = [0]

        def from_w(n):
            w_at[0] += n
            return W[:, w_at[0] - n:w_at[0]]

        cand = from_w(TOPK * TOPK)
        best_d = from_w(DT).rearrange("p (u k) -> p u k", k=TOPK)
        key_s2 = from_w(2 * P).rearrange("p (a n) -> p a n", a=2)
        key_s = from_w(2 * P).rearrange("p (a n) -> p a n", a=2)
        onehot = from_w(2 * TOPK * TOPK).rearrange("p (a j) -> p a j", j=TOPK)
        chosen = from_w(2 * DT)
        gates_d = from_w(DT)
        index = from_w(UNITS * TOPK).bitcast(U32)
        gates = from_w(UNITS * TOPK)
        assert w_at[0] <= 2816
        keys_sb = W[:, 2816:2816 + HP * P].rearrange("p (h n) -> p h n", h=HP)
        qhT = W[:, 4864:4864 + 2 * 4 * 2 * P].rearrange("p (r h n) -> p r h n", r=2, h=4)
        scores_d = W[:, 6912:6912 + DENSE_B * HP * P]
        at_w = [2816]

        def at_keys(n):
            at_w[0] += n
            assert at_w[0] <= 6144
            return W[:, at_w[0] - n:at_w[0]]

        hot_j = at_keys(BATCH * P).bitcast(BF16).rearrange("p (r t j) -> p r t j", r=2, t=BATCH)
        hot_i = at_keys(3 * BATCH * QT).bitcast(BF16).rearrange("p (r a t i) -> p r a t i", r=2, a=3, t=BATCH)
        first_hot = at_keys(BATCH * QT // 2).bitcast(BF16).rearrange("p (t i) -> p t i", t=BATCH)
        gate_rest = at_keys(DT)
        gate_parts = at_keys(3 * DT // 2).bitcast(BF16).rearrange("p (a t) -> p a t", a=3)
        far = at_keys(BATCH * P // 2).bitcast(BF16)
        key_now = at_keys(2 * BATCH).rearrange("p (r t) -> p r t", r=2)
        one = at_keys(1)
        x1_dense = W[:, 2816:2816 + DENSE_B * D].rearrange("p (b n) -> p b n", b=DENSE_B)
        gate_mat = W[:, 6144:6144 + DT * 2 * QT].rearrange("p (t i) -> p t i", t=DT)

        wring = sb("wring", [P, WRING, KD, P])
        x_sb = sb("x_sb", [P, NB, D])
        h2T = sb("h2T", [P, 2, KD, 2 * P])
        c_rows = h2T[:, 0, :, 0:P]
        rope_cs = h2T[:, 1].rearrange("p k n -> p (k n)")[:, 0:2 * NB * HD].rearrange(
            "p (a b d) -> p a b d", a=2, b=NB)
        h2 = x_sb[:, 0:2]
        acc = x_sb[:, 2:4]
        tile_down = [wring[:, r] for r in range(TRING)]
        tile_up = [wring[:, TRING].rearrange("p k n -> p (k n)"), wring[:, TRING + 1].rearrange("p k n -> p (k n)"),
                   h2T[:, 1, 0:4].rearrange("p k n -> p (k n)"), h2T[:, 1, 4:8].rearrange("p k n -> p (k n)")]

        WORK = 15488
        work = sb("work", [P, WORK])
        at = [0]

        def take(n):
            at[0] += n
            assert at[0] <= WORK, at[0]
            return work[:, at[0] - n:at[0]]

        xn = take(D)
        actT = take(D).rearrange("p (k n) -> p k n", k=KD)
        yn = take(D)
        rope_tmp = take(2 * ATT_W).rearrange("p (a n) -> p a n", a=2)
        probs = [take(GROUP * 2 * P), rope_tmp.rearrange("p a n -> p (a n)")]
        q_rot = take(ATT_W)
        k_dup = take(2 * KV_W).rearrange("p (g r d) -> p g r d", g=KVH, r=2)
        v_all = take(NB * KV_W).rearrange("p (b n) -> p b n", b=NB)
        kT = take(KVH * NB * P).rearrange("p (g n) -> p g n", g=KVH)
        u_sb = take(2 * SGU_W).rearrange("p (r n) -> p r n", r=2)
        vg = take(SGU_W)
        ln_both = take(2 * SGU_W)
        ln_d, vn = ln_both[:, 0:SGU_W], ln_both[:, SGU_W:2 * SGU_W]
        xn2 = ln_both
        qT = take(ATT_W).rearrange("p (a n) -> p a n", a=GROUP)
        pT = take(2 * GROUP * P).rearrange("p (j h n) -> p j h n", j=2, h=GROUP)
        diag = pT.rearrange("p j h n -> p (j h n)")[:, 0:4 * P]
        wsT = take(SGU_H * P).rearrange("p (h n) -> p h n", h=SGU_H)
        gain1 = take(D)
        ln_rows = take(2 * SGU_W).rearrange("p (a n) -> p a n", a=2)
        causal = take(P)
        mask_sb = take(2 * P)
        junk = take(D // 2).bitcast(BF16)

        at[0] = 0
        scores = take(UNITS * 2 * P)
        down_ring = take(RING * D).rearrange("p (r n) -> p r n", r=RING)
        up_ring = take(RING * D).rearrange("p (r n) -> p r n", r=RING)
        dot_junk = take(D).bitcast(BF16).rearrange("p (r n) -> p r n", r=2)
        gain2 = take(D)
        square_junk = dot_junk[:, 0]
        weights = take(TRING * DT).rearrange("p (r t) -> p r t", r=TRING)
        dots, gelus, coef = (take(PARTS * RING).rearrange("p (a r) -> p a r", a=PARTS) for _ in range(3))
        zeros = weights[:, TRING - 1, 0:P]
        c_rows2 = weights.rearrange("p r t -> p (r t)").rearrange("p (k n) -> p k n", k=KD)

        ident = sb("ident", [P, P])
        col = sb("col", [P, N_COLS])
        mod = sb("mod", [P, 4 * KD])
        bs_sb = sb("bs_sb", [P, SGU_H])
        sink_sb = sb("sink_sb", [P, QH])
        c_act = sb("c_act", [P, KD])
        halves = sb("halves", [P, 4])
        eps_sb = sb("eps_sb", [P, 1])
        st = sb("st", [P, 16])
        stat = sb("stat", [P, 4, SGU_H])
        soft = sb("soft", [P, KVH, 6, GROUP])
        iota = sb("iota", [P, P])
        top_v = sb("top_v", [P, 2, TOPK])
        top_i = sb("top_i", [P, 2, TOPK], U32)
        top_f = sb("top_f", [P, 2, TOPK])
        best_v = sb("best_v", [P, TOPK])
        best_j = sb("best_j", [P, TOPK], U32)
        pos_u = sb("pos_u", [P, 2, TOPK], U32)
        pos_f = sb("pos_f", [P, 2, TOPK])
        sel = sb("sel", [P, 2, TOPK])
        expert_f = sb("expert_f", [P, TOPK])
        gate_e = sb("gate_e", [P, TOPK])
        gate_s = sb("gate_s", [P, 4])
        staged = sb("staged", [P, 2, TOPK], U32)
        soft_d = sb("soft_d", [P, 2, DENSE_B * PH])
        fin = sb("fin", [P, 4])

        mm = psum("mm", [P, 2, 512])
        tr = psum("tr", [P, 2, 512])
        sc = psum("sc", [P, 2, 512])
        att_ps = psum("att_ps", [P, 512])
        sgu_ps = psum("sgu_ps", [P, 512])
        y_bank = [[sc[:, 0], sc[:, 1]], [att_ps[:], sgu_ps[:]]]

        consts_in = sem("consts_in")
        x_in = sem("x_in")
        win_in = [sem(f"win_in{c}") for c in range(len(PROJ))]
        wout_in = sem("wout_in")
        chunk_in = [sem(f"chunk_in{r}") for r in range(WRING)]
        chunk_used = sem("chunk_used")
        gain2_in = sem("gain2_in")
        keys_in = sem("keys_in")
        mm_full = [sem(f"mm_full{i}") for i in range(2)]
        mm_free = [sem(f"mm_free{i}") for i in range(2)]
        tr_full = [sem(f"tr_full{i}") for i in range(2)]
        tr_free = [sem(f"tr_free{i}") for i in range(2)]
        c_rows_ready = sem("c_rows_ready")
        c_ready = sem("c_ready")
        mod_ready = sem("mod_ready")
        x_squared = sem("x_squared")
        x_ms = sem("x_ms")
        x_rs = sem("x_rs")
        xn_ready = sem("xn_ready")
        actT_dve = sem("actT_dve")
        actT_act = sem("actT_act")
        rope_ready = sem("rope_ready")
        vg_ready = sem("vg_ready")
        vg_used = sem("vg_used")
        var_ready = sem("var_ready")
        var_rs = sem("var_rs")
        vn_ready = sem("vn_ready")
        wsT_ready = sem("wsT_ready")
        qT_ready = sem("qT_ready")
        kT_ready = sem("kT_ready")
        sc_full = sem("sc_full")
        sc_free = sem("sc_free")
        bias_ready = sem("bias_ready")
        exp_ready = sem("exp_ready")
        pT_act = sem("pT_act")
        pT_dve = sem("pT_dve")
        att_full = sem("att_full")
        sgu_full = sem("sgu_full")
        att_free = sem("att_free")
        sgu_free = sem("sgu_free")
        att_ready = sem("att_ready")
        u_ready = sem("u_ready")
        sgu_ready = sem("sgu_ready")
        mix_squared = sem("mix_squared")
        mix_ms = sem("mix_ms")
        mix_rs = sem("mix_rs")
        mix_ready = sem("mix_ready")
        y_squared = sem("y_squared")
        y_ms = sem("y_ms")
        y_rs = sem("y_rs")
        x1_ready = sem("x1_ready")
        x1_squared = sem("x1_squared")
        x1_ms = sem("x1_ms")
        x1_rs = sem("x1_rs")
        xn2_ready = sem("xn2_ready")
        h2T_dve = sem("h2T_dve")
        h2T_act = sem("h2T_act")
        mixer_pe = sem("mixer_pe")
        mixer_dve = sem("mixer_dve")
        mixer_act = sem("mixer_act")
        qhT_ready = sem("qhT_ready")
        x1_saved = sem("x1_saved")
        x1_back = sem("x1_back")
        x1_dense_in = sem("x1_dense_in")
        best_d_ready = sem("best_d_ready")
        gate_exp_d = sem("gate_exp_d")
        chosen_ready = sem("chosen_ready")
        key_now_ready = sem("key_now_ready")
        zeros_ready = sem("zeros_ready")
        far_ready = sem("far_ready")
        hot_i_ready = sem("hot_i_ready")
        hot_j_ready = sem("hot_j_ready")
        gate_full = sem("gate_full")
        gate_stored = sem("gate_stored")
        act_full = sem("act_full")
        tile_gelu = sem("tile_gelu")
        weights_ready = sem("weights_ready")
        tile_done = sem("tile_done")
        tile_down_in = [sem(f"tile_down_in{r}") for r in range(TRING)]
        tile_up_in = [sem(f"tile_up_in{r}") for r in range(TRING)]
        h2T_used = sem("h2T_used")
        dense_squared = sem("dense_squared")
        dense_rms = sem("dense_rms")
        dense_out = sem("dense_out")
        scores_ready = sem("scores_ready")
        h2_ready = sem("h2_ready")
        down_in = [sem(f"down_in{r}") for r in range(RING)]
        up_in = [sem(f"up_in{r}") for r in range(RING)]
        down_free = sem("down_free")
        up_free = sem("up_free")
        index_ready = sem("index_ready")
        staged_ready = sem("staged_ready")
        issue_ok = sem("issue_ok")
        best_ready = sem("best_ready")
        gate_exp = sem("gate_exp")
        gelu_ready = sem("gelu_ready")
        y2_ready = sem("y2_ready")
        y2_rms = sem("y2_rms")
        out_ready = sem("out_ready")
        out_done = sem("out_done")
        dve_chain = sem("dve_chain")
        act_chain = sem("act_chain")
        pool_chain = sem("pool_chain")

        def linker(eng, chain):
            n = [0]

            def link(ins):
                n[0] += 1
                ins.then_inc(chain, 1)
                eng.wait_ge(chain, n[0])

            return link

        N_CONSTS = 13
        block = ctx.enter_context(nc.Block())

        @block.sync
        def _(sp):
            USED = chunk_signals(MM)

            def chunk_free(n):
                bank, turn = USED[n]
                if bank is None:
                    sp.wait_ge(chunk_used, turn)
                else:
                    sp.wait_ge(mm_full[bank], turn + 1)

            def chunk(n, source):
                if n >= WRING:
                    chunk_free(n - WRING)
                sp.dma_start(wring[:, n % WRING], source).then_inc(chunk_in[n % WRING], 16)

            sp.dma_start(col[:], cols).then_inc(consts_in, 16)
            sp.dma_start(x_sb[:, 0], x[0:P, :]).then_inc(x_in, 16)
            sp.dma_start(ident[:], ident_in).then_inc(consts_in, 16)
            sp.dma_start(rope_cs[:, 0], cos_tab).then_inc(consts_in, 16)
            sp.dma_start(rope_cs[:, 1], sin_tab).then_inc(consts_in, 16)
            sp.dma_start(causal, masks[:, 0:P]).then_inc(consts_in, 16)
            sp.dma_start(mask_sb, masks[:, P:3 * P]).then_inc(consts_in, 16)
            sp.dma_start(iota[:], iota_in).then_inc(consts_in, 16)
            sp.dma_start(bs_sb[:], b_s).then_inc(consts_in, 16)
            sp.dma_start(sink_sb[:], sinks.partition_broadcast(P)).then_inc(consts_in, 16)
            sp.dma_start(wsT, w_s).then_inc(consts_in, 16)
            sp.dma_start(ln_rows, rows[4 * D:4 * D + 2 * SGU_W].partition_broadcast(P)
                         .rearrange("p (a n) -> p a n", a=2)).then_inc(consts_in, 16)
            sp.dma_start(gain1, rows[0:D].partition_broadcast(P)).then_inc(consts_in, 16)
            sp.dma_start(yn, rows[D:2 * D].partition_broadcast(P)).then_inc(consts_in, 16)
            for n in range(2 * KD):
                chunk(n, w_ada[n])
            for c, (first, n) in enumerate(PROJ):
                sp.dma_start(win_sb[:, :, first:first + n],
                             w_in.rearrange("(k p) n -> p k n", p=P)[:, :, first:first + n]
                             ).then_inc(win_in[c], 16)
            sp.wait_ge(x_in, 16)
            for b in range(1, NB):
                sp.dma_start(x_sb[:, b], x[b * P:(b + 1) * P, :]).then_inc(x_in, 16)
                sp.wait_ge(x_in, 16 * (b + 1))
            sp.dma_start(wout_sb, w_out.rearrange("(k p) n -> p k n", p=P)).then_inc(wout_in, 16)
            for n in range(2 * KD, 5 * KD):
                chunk(n, w_ada[n])
            bank, turn = MM["proj", NB - 1, len(PROJ) - 1]
            sp.wait_ge(mm_full[bank], turn + 1)
            sp.dma_start(keys_sb, keys).then_inc(keys_in, 16)
            for hp in range(HP):
                chunk(5 * KD + hp, w_query[hp])
            for hp in range(HP):
                chunk(5 * KD + HP + hp, w_query[hp])
            sp.wait_ge(mixer_pe, 1)
            sp.wait_ge(mixer_dve, 1)
            sp.wait_ge(mixer_act, 1)
            sp.wait_ge(x1_saved, 16 * NB)
            sp.dma_start(gain2, rows[2 * D:3 * D].partition_broadcast(P)).then_inc(gain2_in, 16)
            sp.dma_start(acc[:, 0], rows[3 * D:4 * D].partition_broadcast(P)).then_inc(gain2_in, 16)
            for n in range(KD):
                chunk(5 * KD + 2 * HP + n, w_ada[GT2 * KD + n])
            sp.dma_start(acc[:, 1], x1_dram[DENSE_B]).then_inc(x1_back, 16)
            for n in range(len(USED) - WRING, len(USED)):
                chunk_free(n)
            sp.wait_ge(h2T_used, 1)
            with sp.Fori(0, TILES // TRING, 1) as i:
                for r in range(TRING):
                    n = i * TRING + r
                    sp.wait_ge(act_full, n + 1)
                    sp.dma_start(tile_down[r], down_tiles[bass.ds(n, 1)].rearrange("o p k n -> (o p) k n")
                                 ).then_inc(tile_down_in[r], 16)
                    sp.wait_ge(tile_done, n + 1)
                    sp.dma_start(tile_up[r], up[bass.ds(n * P, P), :]).then_inc(tile_up_in[r], 16)
            sp.wait_ge(gate_full, 2 + QUARTERS * BATCHES)
            for b in range(DENSE_B):
                sp.dma_start(x1_dense[:, b], x1_dram[b]).then_inc(x1_dense_in, 16)
            sp.wait_ge(dense_out, DENSE_B)
            for b in range(DENSE_B):
                sp.dma_start(out[b * P:(b + 1) * P, :], x1_dense[:, b]).then_inc(out_done, 16)
            sp.wait_ge(out_done, 16 * NB)

        @block.gpsimd
        def _(pool):
            link = linker(pool, pool_chain)
            link(nc.gpsimd.memset(halves[:], -0.5))

            def rsqrt(ready, done, n, at_, width=1):
                pool.wait_ge(ready, n)
                nc.gpsimd.tensor_tensor(at_, at_, halves[:, 0:1].to_broadcast([P, width]),
                                        ALU.pow).then_inc(done, 1)

            for stage, b in steps():
                if stage == "N":
                    rsqrt(x_ms, x_rs, b + 1, st[:, 0:1])
                elif stage == "LN":
                    rsqrt(var_ready, var_rs, b + 1, stat[:, 3], SGU_H)
                elif stage == "O":
                    rsqrt(mix_ms, mix_rs, b + 1, st[:, 2:4], 2)
                elif stage == "W2":
                    rsqrt(y_ms, y_rs, b + 1, st[:, 6:7])
                elif stage == "F1":
                    rsqrt(x1_ms, x1_rs, b + 1, st[:, 8:9])
            pool.wait_ge(mixer_pe, 1)
            pool.wait_ge(mixer_act, 1)
            pool.wait_ge(mixer_dve, 1)

            def gather(table, ring, free, arrived, r, side, first):
                pool.wait_ge(free, first + r + 1)
                pool.sem_inc(issue_ok, 1)
                nc.gpsimd.indirect_dma_start(
                    ring[:, r % RING], None, table,
                    bass.IndirectOffsetOnAxis(ap=staged[:, side, r:r + 1], axis=0),
                ).then_inc(arrived[r % RING], 16)

            with pool.Fori(0, UNITS // 2, 1) as i:
                for side in range(2):
                    unit = i * 2 + side
                    pool.wait_ge(index_ready, unit + 1)
                    pool.wait_ge(up_free, unit * TOPK + 1)
                    nc.gpsimd.tensor_copy(staged[:, side], index[:, bass.ds(unit * TOPK, TOPK)]
                                          ).then_inc(staged_ready, 1)
                    pool.wait_ge(staged_ready, unit + 1)
                    pool.sem_inc(issue_ok, 1)
                    for part in range(PARTS):
                        for r in range(part * RING, (part + 1) * RING):
                            gather(down, down_ring, down_free, down_in, r, side, unit * TOPK)
                        for r in range(part * RING, (part + 1) * RING):
                            gather(up, up_ring, up_free, up_in, r, side, unit * TOPK)

        @block.scalar
        def _(act):
            link = linker(act, act_chain)
            act.wait_ge(consts_in, 16 * N_CONSTS)
            nc.scalar.activation(c_act[:], col[:, COL_C:COL_C + KD], ACT.Silu).then_inc(c_ready, 1)

            def scale_shift(key, out_of, gain_of, shift_of, done):
                bank, turn = TR[key]
                act.wait_ge(tr_full[bank], turn + 1)
                for j in range(4):
                    k = 4 * key[-1] + j
                    shift = shift_of(k) if shift_of else 0.0
                    last = nc.scalar.activation(out_of(k), tr[:, bank, j * P:(j + 1) * P],
                                                ACT.Identity if shift_of else ACT.Copy,
                                                bias=shift, scale=gain_of(k))
                link(last)
                act.sem_inc(tr_free[bank], 1)
                act.sem_inc(done, 1)

            def query(group):
                half, g = group // 4, group % 4
                if group == 4:
                    act.wait_ge(mixer_pe, 1)
                    act.wait_ge(mixer_dve, 1)
                for j in range(4):
                    bank, turn = MM["query", 4 * group + j]
                    act.wait_ge(mm_full[bank], turn + 1)
                    link(nc.scalar.activation(qhT[:, group % 2, j], mm[:, bank, 0:2 * P], ACT.Copy))
                    act.sem_inc(mm_free[bank], 1)
                act.sem_inc(qhT_ready, 1)
                target = scores if half else scores_d
                for tb in range(2):
                    bank, turn = MM["score", group, tb]
                    act.wait_ge(mm_full[bank], turn + 1)
                    first = (tb * HP + 4 * g) * P
                    link(nc.scalar.activation(target[:, first:first + 4 * P], mm[:, bank, :], ACT.Copy))
                    act.sem_inc(mm_free[bank], 1)
                act.sem_inc(scores_ready, 1)

            def h2_rows(b):
                for part in range(2):
                    bank, turn = TR["h2", b, part]
                    act.wait_ge(tr_full[bank], turn + 1)
                    link(nc.scalar.activation(h2[:, b % 2, part * 512:(part + 1) * 512], tr[:, bank, :], ACT.Copy))
                    act.sem_inc(tr_free[bank], 1)
                act.sem_inc(h2_ready, 1)

            def gate_softmax(unit):
                act.wait_ge(best_ready, unit + 1)
                nc.scalar.activation(gate_e[:], best_v[:], ACT.Exp, bias=gate_s[:, 0:1],
                                     accum_out=gate_s[:, 1:2]).then_inc(gate_exp, 1)

            for stage, b in steps():
                if stage == "N":
                    act.wait_ge(x_in, 16 * (b + 1))
                    if b:
                        bank, turn = TR["x", b - 1, 1]
                        act.wait_ge(tr_full[bank], turn + 1)
                        act.wait_ge(x_ms, b)
                    nc.scalar.activation(junk, x_sb[:, b], ACT.Square, accum_out=st[:, 1:2]).then_inc(x_squared, 1)
                    act.wait_ge(x_rs, b + 1)
                    nc.scalar.activation(xn, x_sb[:, b], ACT.Copy, scale=st[:, 0:1]).then_inc(xn_ready, 1)
                elif stage == "T":
                    act.wait_ge(mod_ready, 2)
                    scale_shift(("x", b, 1), lambda k: actT[:, k],
                                lambda k: mod[:, KD + k:KD + k + 1], lambda k: mod[:, k:k + 1], actT_act)
                elif stage == "S1":
                    bank, turn = TR["k", b]
                    act.wait_ge(tr_full[bank], turn + 1)
                    link(nc.scalar.activation(kT[:, :, b * P:(b + 1) * P],
                                              tr[:, bank, 0:2 * P].rearrange("p (g n) -> p g n", g=2), ACT.Copy))
                    act.sem_inc(tr_free[bank], 1)
                    act.sem_inc(kT_ready, 1)
                elif stage == "P":
                    bank, turn = MM["proj", b, 2]
                    act.wait_ge(mm_full[bank], turn + 1)
                    if b >= 2:
                        act.wait_ge(mix_ready, b - 1)
                    link(nc.scalar.activation(u_sb[:, b % 2], mm[:, bank, :], ACT.Gelu))
                    act.sem_inc(mm_free[bank], 1)
                    act.sem_inc(u_ready, 1)
                    bank, turn = MM["proj", b, 3]
                    act.wait_ge(mm_full[bank], turn + 1)
                    if b:
                        act.wait_ge(vg_used, b)
                    link(nc.scalar.activation(vg, mm[:, bank, :], ACT.Gelu))
                    act.sem_inc(mm_free[bank], 1)
                    act.sem_inc(vg_ready, 1)
                elif stage == "S2":
                    for g in range(KVH):
                        act.wait_ge(bias_ready, 2 * b + g + 1)
                        for h in range(GROUP):
                            s = probs[g][:, h * 2 * P:(h + 1) * 2 * P]
                            nc.scalar.activation(s, s, ACT.Exp, bias=soft[:, g, 1, h:h + 1],
                                                 accum_out=soft[:, g, 2, h:h + 1])
                        nc.scalar.activation(soft[:, g, 4], soft[:, g, 3], ACT.Exp).then_inc(exp_ready, 1)
                elif stage == "W":
                    scale_shift(("mix", b, 1), lambda k: actT[:, k],
                                lambda k: col[:, COL_GOUT + k:COL_GOUT + k + 1], None, actT_act)
                    for half in range(2):
                        bank, turn = MM["y", b, half]
                        act.wait_ge(mm_full[bank], turn + 1)
                        last = nc.scalar.activation(junk[:, half * 512:(half + 1) * 512], mm[:, bank, :],
                                                    ACT.Square, accum_out=st[:, 4 + half:5 + half])
                    last.then_inc(y_squared, 1)
                elif stage == "O":
                    for g in range(KVH):
                        bank, turn = TR["prob", b, g, 0]
                        act.wait_ge(tr_full[bank], turn + 1)
                        link(nc.scalar.activation(pT[:, 0], tr[:, bank, :].rearrange("p (h n) -> p h n", h=GROUP),
                                                  ACT.Copy))
                        act.sem_inc(tr_free[bank], 1)
                        act.sem_inc(pT_act, 1)
                    act.wait_ge(sgu_ready, b + 1)
                    link(nc.scalar.activation(junk[:, 512:1024], u_sb[:, b % 2], ACT.Square, accum_out=st[:, 11:12]))
                    act.wait_ge(att_ready, b + 1)
                    link(nc.scalar.activation(junk[:, 0:512], yn[:, 0:512], ACT.Square, accum_out=st[:, 10:11]))
                    act.sem_inc(mix_squared, 1)
                    act.wait_ge(mix_rs, b + 1)
                    nc.scalar.activation(yn[:, 0:512], yn[:, 0:512], ACT.Copy, scale=st[:, 2:3])
                    nc.scalar.activation(yn[:, 512:1024], u_sb[:, b % 2], ACT.Copy,
                                         scale=st[:, 3:4]).then_inc(mix_ready, 1)
                elif stage == "F1":
                    act.wait_ge(x1_ready, b + 1)
                    nc.scalar.activation(junk, x_sb[:, b], ACT.Square, accum_out=st[:, 9:10]).then_inc(x1_squared, 1)
                    act.wait_ge(x1_rs, b + 1)
                    nc.scalar.activation(xn2, x_sb[:, b], ACT.Copy, scale=st[:, 8:9]).then_inc(xn2_ready, 1)
                elif stage == "F2":
                    act.wait_ge(mod_ready, 4)
                    scale_shift(("ffn", b, 1), lambda k: h2T[:, b // 2, k, (b % 2) * P:(b % 2 + 1) * P],
                                lambda k: mod[:, 3 * KD + k:3 * KD + k + 1],
                                lambda k: mod[:, 2 * KD + k:2 * KD + k + 1], h2T_act)
                    act.dma_start(x1_dram[b], x_sb[:, b]).then_inc(x1_saved, 16)
                elif stage == "Q":
                    query(b)
                elif stage == "TURN":
                    act.wait_ge(best_d_ready, 1)
                    nc.scalar.activation(best_d, best_d, ACT.Exp).then_inc(gate_exp_d, 1)
                    act.wait_ge(x1_saved, 16 * NB)
                    for b_ in range(DENSE_B, NB):
                        h2_rows(b_)
                    gate_softmax(0)
                if (stage, b) == ("F2", NB - 1):
                    act.sem_inc(mixer_act, 1)

            def second_key_rows(n, side, tokens):
                act.wait_ge(key_now_ready, n + 1)
                act.wait_ge(hot_j_ready, n + 1)
                for t in range(tokens):
                    last = nc.scalar.activation(far[:, t * P:(t + 1) * P], iota[:], ACT.Square,
                                                bias=key_now[:, side, t:t + 1], scale=-1.0)
                last.then_inc(far_ready, 1)
                act.wait_ge(far_ready, n + 1)
                nc.scalar.activation(hot_j[:, side, 0:tokens].rearrange("p t j -> p (t j)"), far[:, 0:tokens * P],
                                     ACT.Relu, bias=one, scale=-1.0).then_inc(hot_j_ready, 1)

            def store_gates(n, side, quarter, t0):
                act.wait_ge(gate_full, n + 3)
                nc.scalar.activation(
                    gate_mat[:, bass.ds(t0, BATCH), quarter % 2 * QT:(quarter % 2 + 1) * QT],
                    tr[:, side, 0:BATCH * QT].rearrange("p (t i) -> p t i", t=BATCH), ACT.Copy
                ).then_inc(gate_stored, 1)

            def tile_activations(unit, t):
                act.wait_ge(act_full, unit * TILES_UNIT + t + 1 + TRING)
                act.wait_ge(tile_done, unit * TILES_UNIT + t + 1)
                nc.scalar.activation(weights[:, t % TRING], mm[:, t % 2, 0:DT], ACT.Gelu).then_inc(tile_gelu, 1)

            def gate_step(q, i, t):
                if q == QUARTERS - 1:
                    return
                n = i * TILES_UNIT + (t + (q + 1) * BATCHES)
                second_key_rows(n, t % 2, BATCH)
                if t:
                    store_gates(n - 1, (t - 1) % 2, q + 1, i * (TILES_UNIT * BATCH) + (t - 1) * BATCH)
                if t == TILES_UNIT - 1:
                    store_gates(n, t % 2, q + 1, i * (TILES_UNIT * BATCH) + t * BATCH)

            def experts(q, i, more):
                unit = i + q * QUNITS
                for part in range(PARTS):
                    tile_activations(unit, 2 * part)
                    gate_step(q, i, 2 * part)
                    tile_activations(unit, 2 * part + 1)
                    act.wait_ge(down_free, unit * TOPK + (part + 2) * RING)
                    nc.scalar.activation(gelus[:, part], dots[:, part], ACT.Gelu).then_inc(gelu_ready, 1)
                    gate_step(q, i, 2 * part + 1)
                if more:
                    gate_softmax(unit + 1)

            act.sem_inc(hot_j_ready, 1)
            second_key_rows(0, 0, SHARE)
            with act.Fori(0, BATCHES // 2 - 1, 1) as i:
                for side in range(2):
                    second_key_rows(i * 2 + (side + 1), 1 - side, SHARE)
                    store_gates(i * 2 + side, side, 0, i * (2 * BATCH) + side * BATCH)
            second_key_rows(BATCHES - 1, 1, SHARE)
            for n in (BATCHES - 2, BATCHES - 1):
                store_gates(n, n % 2, 0, n * BATCH)
            for b in range(GATHER_B):
                for q in (2 * b, 2 * b + 1):
                    if q:
                        act.wait_ge(weights_ready, q * QT)
                    with act.Fori(0, QUNITS - q % 2, 1) as i:
                        experts(q, i, True)
                    if b and q == 2 * b:
                        act.wait_ge(out_done, 16 * b)
                        act.dma_start(acc[:, 1], x1_dram[DENSE_B + b]).then_inc(x1_back, 16)
                experts(q, QUNITS - 1, b < GATHER_B - 1)
                act.wait_ge(y2_ready, b + 1)
                link(nc.scalar.activation(square_junk, acc[:, 0],
                                          ACT.Square, accum_out=fin[:, 0:1]))
                nc.scalar.activation(fin[:, 1:2], fin[:, 0:1], ACT.Sqrt, bias=eps_sb[:],
                                     scale=1.0 / D).then_inc(y2_rms, 1)
                act.wait_ge(out_ready, b + 1)
                act.dma_start(out[(DENSE_B + b) * P:(DENSE_B + b + 1) * P, :], acc[:, 1]).then_inc(out_done, 16)
            act.wait_ge(tile_done, TRING + TILES)
            for b in range(DENSE_B):
                for half in range(2):
                    last = nc.scalar.activation(dot_junk[:, b, half * 512:(half + 1) * 512], y_bank[b][half],
                                                ACT.Square, accum_out=soft_d[:, 0, 2 * b + half:2 * b + half + 1])
            last.then_inc(dense_squared, 1)
            act.wait_ge(dense_squared, 2)
            nc.scalar.activation(soft_d[:, 0, 6:8], soft_d[:, 0, 4:6], ACT.Sqrt, bias=eps_sb[:],
                                 scale=1.0 / D).then_inc(dense_rms, 1)

        @block.vector
        def _(dve):
            link = linker(dve, dve_chain)
            V = nc.vector
            link(V.memset(eps_sb[:], EPS))
            dve.wait_ge(consts_in, 16 * N_CONSTS)
            dve.wait_ge(c_ready, 1)
            V.tensor_copy(c_rows, c_act[:].unsqueeze(2).broadcast_to([P, KD, P])).then_inc(c_rows_ready, 1)
            link(V.tensor_tensor(wsT, wsT, causal.unsqueeze(1).broadcast_to([P, SGU_H, P]), ALU.mult))
            dve.sem_inc(wsT_ready, 1)

            def mean_square(squared, ready, n, source, target, width, count):
                dve.wait_ge(squared, n)
                V.tensor_scalar(target, source, 1.0 / count, EPS, ALU.mult, ALU.add).then_inc(ready, 1)

            def scale_shift(key, out_of, gain_of, shift_of, done):
                bank, turn = TR[key]
                dve.wait_ge(tr_full[bank], turn + 1)
                for j in range(4):
                    k = 4 * key[-1] + j
                    shift = shift_of(k) if shift_of else 0.0
                    last = V.tensor_scalar(out_of(k), tr[:, bank, j * P:(j + 1) * P], gain_of(k), shift,
                                           ALU.mult, ALU.add)
                link(last)
                dve.sem_inc(tr_free[bank], 1)
                dve.sem_inc(done, 1)

            def ada_col(v):
                slot = {SH1: 0, SC1: 1, SH2: 2, SC2: 3}[v]
                m = mod[:, slot * KD:(slot + 1) * KD]
                square = diag.rearrange("p (m n) -> p m n", m=4)
                for half in range(2):
                    bank, turn = MM["ada", v, half]
                    dve.wait_ge(mm_full[bank], turn + 1)
                    link(V.tensor_tensor(square, mm[:, bank, :].rearrange("p (m n) -> p m n", m=4),
                                         ident[:].unsqueeze(1).broadcast_to([P, 4, P]), ALU.mult))
                    dve.sem_inc(mm_free[bank], 1)
                    link(V.tensor_reduce(m[:, half * 4:(half + 1) * 4], square, AX_X, ALU.add))
                link(V.tensor_tensor(m, m, col[:, COL_BADA + v * KD:COL_BADA + (v + 1) * KD], ALU.add))
                if v in (SC1, SC2):
                    g = COL_G1 if v == SC1 else COL_G2
                    link(V.scalar_tensor_tensor(m, m, 1.0, col[:, g:g + KD], ALU.add, ALU.mult))
                dve.sem_inc(mod_ready, 1)

            def ada_row(v, gain, factor):
                for half in range(2):
                    bank, turn = MM["ada", v, half]
                    cols_ = slice(half * 512, (half + 1) * 512)
                    dve.wait_ge(mm_full[bank], turn + 1)
                    link(V.tensor_tensor(gain[:, cols_], mm[:, bank, :], gain[:, cols_], ALU.add))
                    dve.sem_inc(mm_free[bank], 1)
                    link(V.tensor_tensor(gain[:, cols_], gain[:, cols_], factor[:, cols_], ALU.mult))

            def rope(src, out_lo_hi, heads, b):
                cos = rope_cs[:, 0, b].unsqueeze(1).broadcast_to([P, heads, HD])
                half = HD // 2
                a = rope_tmp[:, 0, 0:heads * HD].rearrange("p (h d) -> p h d", h=heads)
                c = rope_tmp[:, 1, 0:heads * HD].rearrange("p (h d) -> p h d", h=heads)
                V.tensor_tensor(a, src, cos, ALU.mult)
                for lo, hi in ((0, half), (half, 0)):
                    s = rope_cs[:, 1, b, lo:lo + half].unsqueeze(1).broadcast_to([P, heads, half])
                    last = V.tensor_tensor(c[:, :, lo:lo + half], src[:, :, hi:hi + half], s, ALU.mult)
                link(last)
                for o in out_lo_hi:
                    last = V.tensor_tensor(o, a, c, ALU.add)
                link(last)

            def top_keys(source):
                for p in range(2):
                    V.max(top_v[:, p, 0:8], source[p])
                dve.drain()
                for p in range(2):
                    V.max_index(top_i[:, p, 0:8], top_v[:, p, 0:8], source[p])
                    V.match_replace(key_s2[:, p], top_v[:, p, 0:8], source[p], REMOVED)
                dve.drain()
                for p in range(2):
                    V.max(top_v[:, p, 8:16], key_s2[:, p])
                dve.drain()
                for p in range(2):
                    V.max_index(top_i[:, p, 8:16], top_v[:, p, 8:16], key_s2[:, p])
                V.tensor_tensor(cand.rearrange("p (a c) -> p a c", a=TOPK),
                                top_v[:, 0].unsqueeze(2).broadcast_to([P, TOPK, TOPK]),
                                top_v[:, 1].unsqueeze(1).broadcast_to([P, TOPK, TOPK]), ALU.add)
                dve.drain()

            def top_sums(best, signal):
                V.tensor_copy(top_f[:], top_i[:])
                V.max(best[:, 0:8], cand)
                dve.drain()
                V.max_index(best_j[:, 0:8], best[:, 0:8], cand)
                V.match_replace(cand, best[:, 0:8], cand, REMOVED)
                V.tensor_scalar(gate_s[:, 0:1], best[:, 0:1], -1.0, None, ALU.mult)
                dve.drain()
                V.max(best[:, 8:16], cand)
                if signal:
                    dve.drain().then_inc(best_ready, 1)
                else:
                    dve.drain()
                V.max_index(best_j[:, 8:16], best[:, 8:16], cand)
                dve.drain()

            def chosen_keys(target):
                V.tensor_scalar(pos_u[:, 0], best_j[:], 4, None, ALU.logical_shift_right)
                V.tensor_scalar(pos_u[:, 1], best_j[:], TOPK - 1, None, ALU.bitwise_and)
                dve.drain()
                V.tensor_copy(pos_f[:], pos_u[:])
                dve.drain()
                V.tensor_tensor(onehot, iota[:, 0:TOPK].unsqueeze(1).broadcast_to([P, 2 * TOPK, TOPK]),
                                pos_f[:].rearrange("p a k -> p (a k)").unsqueeze(2).broadcast_to([P, 2 * TOPK, TOPK]),
                                ALU.is_equal)
                dve.drain()
                hot4 = onehot.rearrange("p (a k) j -> p a k j", a=2)
                V.tensor_tensor(hot4, hot4, top_f[:].unsqueeze(2).broadcast_to([P, 2, TOPK, TOPK]), ALU.mult)
                dve.drain()
                V.tensor_reduce(target, hot4, AX_X, ALU.add)
                dve.drain()

            def expert_numbers(unit):
                V.scalar_tensor_tensor(expert_f[:], sel[:, 0], float(NKEY), sel[:, 1], ALU.mult, ALU.add)
                dve.drain()
                V.tensor_copy(index[:, bass.ds(unit * TOPK, TOPK)], expert_f[:]).then_inc(index_ready, 1)

            def gate_values(unit):
                dve.wait_ge(gate_exp, unit + 1)
                V.reciprocal(gate_s[:, 2:3], gate_s[:, 1:2])
                dve.drain()
                V.tensor_scalar(gates[:, bass.ds(unit * TOPK, TOPK)], gate_e[:], gate_s[:, 2:3], None, ALU.mult)
                dve.drain()

            chosen4 = chosen.rearrange("p (a m) -> p a m", a=2)

            def top_dense(unit):
                dve.wait_ge(scores_ready, unit // 4 + 1)
                n = unit % DENSE_B * PH + unit // DENSE_B
                first = n * 2 * P
                top_keys([scores_d[:, first + p * P:first + (p + 1) * P] for p in range(2)])
                top_sums(best_d[:, n], False)
                chosen_keys(chosen4[:, :, n * TOPK:(n + 1) * TOPK])

            def dense_gates():
                u = DENSE_B * PH
                link(V.tensor_copy(soft_d[:, 0], best_d[:, :, 0]))
                V.tensor_tensor(best_d, best_d, soft_d[:, 0].unsqueeze(2).broadcast_to([P, u, TOPK]),
                                ALU.subtract).then_inc(best_d_ready, 1)
                dve.wait_ge(gate_exp_d, 1)
                link(V.tensor_reduce(soft_d[:, 0], best_d, AX_X, ALU.add))
                link(V.reciprocal(soft_d[:, 1], soft_d[:, 0]))
                V.tensor_tensor(gates_d.rearrange("p (u k) -> p u k", u=u), best_d,
                                soft_d[:, 1].unsqueeze(2).broadcast_to([P, u, TOPK]), ALU.mult
                                ).then_inc(chosen_ready, 1)

            def transposed_gates():
                for n, (target, width) in enumerate(((chosen, 4 * P), (gates_d, 2 * P))):
                    bank, turn = TR["onehot", n]
                    dve.wait_ge(tr_full[bank], turn + 1)
                    link(V.tensor_copy(target, tr[:, bank, 0:width]))
                    dve.sem_inc(tr_free[bank], 1)

            def split_gates():
                V.tensor_copy(gate_rest, gates_d)
                dve.drain()
                for part in range(3):
                    V.tensor_copy(gate_parts[:, part], gate_rest)
                    dve.drain()
                    if part < 2:
                        V.tensor_tensor(gate_rest, gate_rest, gate_parts[:, part], ALU.subtract)
                        dve.drain()

            for stage, b in steps():
                if stage == "N":
                    mean_square(x_squared, x_ms, b + 1, st[:, 1:2], st[:, 0:1], 1, D)
                elif stage == "ADA_COL":
                    ada_col(b)
                elif stage == "ADA_ROW" and b == GT1:
                    ada_row(b, gain1, yn)
                elif stage == "TURN":
                    dense_gates()
                    dve.sem_inc(down_free, RING)
                    dve.sem_inc(up_free, RING)
                    dve.wait_ge(scores_ready, 8)
                    top_keys([scores[:, p * P:(p + 1) * P] for p in range(2)])
                    top_sums(best_v, True)
                    chosen_keys(sel[:])
                    expert_numbers(0)
                    gate_values(0)
                    transposed_gates()
                    link(V.memset(one, 1.0))
                    split_gates()
                elif stage == "T":
                    scale_shift(("x", b, 0), lambda k: actT[:, k], lambda k: mod[:, KD + k:KD + k + 1],
                                lambda k: mod[:, k:k + 1], actT_dve)
                elif stage == "P":
                    bank, turn = MM["proj", b, 0]
                    dve.wait_ge(mm_full[bank], turn + 1)
                    rope(mm[:, bank, :].rearrange("p (h d) -> p h d", h=QH),
                         [q_rot.rearrange("p (h d) -> p h d", h=QH)], QH, b)
                    dve.sem_inc(mm_free[bank], 1)
                    bank, turn = MM["proj", b, 1]
                    dve.wait_ge(mm_full[bank], turn + 1)
                    V.tensor_copy(v_all[:, b], mm[:, bank, KV_W:2 * KV_W])
                    rope(mm[:, bank, 0:KV_W].rearrange("p (h d) -> p h d", h=KVH),
                         [k_dup[:, :, r] for r in range(2)], KVH, b)
                    dve.sem_inc(mm_free[bank], 1)
                    dve.sem_inc(rope_ready, 1)
                elif stage == "LN":
                    dve.wait_ge(vg_ready, b + 1)
                    if b >= 2:
                        dve.wait_ge(h2T_act, b - 1)
                    v3 = vg.rearrange("p (h d) -> p h d", h=SGU_H)
                    d3 = ln_d.rearrange("p (h d) -> p h d", h=SGU_H)
                    n3 = vn.rearrange("p (h d) -> p h d", h=SGU_H)
                    link(V.tensor_reduce(stat[:, 0], v3, AX_X, ALU.add))
                    link(V.tensor_scalar(stat[:, 1], stat[:, 0], 1.0 / HD, None, ALU.mult))
                    link(V.tensor_tensor(d3, v3, stat[:, 1].unsqueeze(2).broadcast_to([P, SGU_H, HD]), ALU.subtract))
                    dve.sem_inc(vg_used, 1)
                    link(V.tensor_tensor(n3, d3, d3, ALU.mult))
                    link(V.tensor_reduce(stat[:, 2], n3, AX_X, ALU.add))
                    V.tensor_scalar(stat[:, 3], stat[:, 2], 1.0 / HD, EPS, ALU.mult, ALU.add).then_inc(var_ready, 1)
                    dve.wait_ge(var_rs, b + 1)
                    link(V.tensor_tensor(n3, d3, stat[:, 3].unsqueeze(2).broadcast_to([P, SGU_H, HD]), ALU.mult))
                    link(V.tensor_tensor(vn, vn, ln_rows[:, 0], ALU.mult))
                    V.tensor_tensor(vn, vn, ln_rows[:, 1], ALU.add).then_inc(vn_ready, 1)
                elif stage == "S1":
                    bank, turn = TR["q", b]
                    dve.wait_ge(tr_full[bank], turn + 1)
                    link(V.tensor_copy(qT.rearrange("p a n -> p (a n)"), tr[:, bank, :]))
                    dve.sem_inc(tr_free[bank], 1)
                    dve.sem_inc(qT_ready, 1)
                elif stage == "S2":
                    for g in range(KVH):
                        dve.wait_ge(sc_full, 2 * b + g + 1)
                        s3 = probs[g].rearrange("p (h n) -> p h n", h=GROUP)
                        first = 0 if b else P
                        if b == 0:
                            V.memset(s3[:, :, 0:P], MASKED)
                        link(V.scalar_tensor_tensor(
                            s3[:, :, first:], sc[:].rearrange("p a (c n) -> p (a c) n", c=2)[:, :, first:],
                            HD ** -0.5, mask_sb[:, first:].unsqueeze(1).broadcast_to([P, GROUP, 2 * P - first]),
                            ALU.mult, ALU.add))
                        dve.sem_inc(sc_free, 1)
                        t = soft[:, g]
                        sk = sink_sb[:, g * GROUP:(g + 1) * GROUP]
                        link(V.tensor_reduce(t[:, 0], s3, AX_X, ALU.max))
                        link(V.tensor_tensor(t[:, 0], t[:, 0], sk, ALU.max))
                        V.tensor_scalar(t[:, 1], t[:, 0], -1.0, None, ALU.mult)
                        link(V.tensor_tensor(t[:, 3], sk, t[:, 0], ALU.subtract))
                        dve.sem_inc(bias_ready, 1)
                elif stage == "G":
                    dve.wait_ge(sgu_full, b + 1)
                    dve.wait_ge(u_ready, b + 1)
                    o3 = ln_d.rearrange("p (h d) -> p h d", h=SGU_H)
                    link(V.tensor_tensor(o3, sgu_ps[:].rearrange("p (h d) -> p h d", h=SGU_H),
                                         bs_sb[:].unsqueeze(2).broadcast_to([P, SGU_H, HD]), ALU.add))
                    dve.sem_inc(sgu_free, 1)
                    V.tensor_tensor(u_sb[:, b % 2], ln_d, u_sb[:, b % 2], ALU.mult).then_inc(sgu_ready, 1)
                    dve.wait_ge(sgu_ready, b + 1)
                elif stage == "W":
                    scale_shift(("mix", b, 0), lambda k: actT[:, k],
                                lambda k: col[:, COL_GOUT + k:COL_GOUT + k + 1], None, actT_dve)
                    for n in TK_IN_W.get(b, ()):
                        top_dense(n)
                elif stage == "W2":
                    dve.wait_ge(y_squared, b + 1)
                    link(V.tensor_tensor(st[:, 7:8], st[:, 4:5], st[:, 5:6], ALU.add))
                    V.tensor_scalar(st[:, 6:7], st[:, 7:8], 1.0 / D, EPS, ALU.mult, ALU.add).then_inc(y_ms, 1)
                    dve.wait_ge(y_rs, b + 1)
                    for half in range(2):
                        bank, turn = MM["y", b, half]
                        c_ = slice(half * 512, (half + 1) * 512)
                        dve.wait_ge(mm_full[bank], turn + 1)
                        link(V.scalar_tensor_tensor(xn2[:, c_], mm[:, bank, :], st[:, 6:7], gain1[:, c_],
                                                    ALU.mult, ALU.mult))
                        dve.sem_inc(mm_free[bank], 1)
                    V.tensor_tensor(x_sb[:, b], x_sb[:, b], xn2, ALU.add).then_inc(x1_ready, 1)
                elif stage == "O":
                    for g in range(KVH):
                        bank, turn = TR["prob", b, g, 1]
                        dve.wait_ge(tr_full[bank], turn + 1)
                        link(V.tensor_copy(pT[:, 1].rearrange("p h n -> p (h n)"), tr[:, bank, :]))
                        dve.sem_inc(tr_free[bank], 1)
                        dve.sem_inc(pT_dve, 1)
                        t = soft[:, g]
                        dve.wait_ge(exp_ready, 2 * b + g + 1)
                        link(V.tensor_tensor(t[:, 5], t[:, 2], t[:, 4], ALU.add))
                        link(V.reciprocal(t[:, 5], t[:, 5]))
                    dve.wait_ge(att_full, b + 1)
                    for g in range(KVH):
                        a_ = slice(g * GROUP * HD, (g + 1) * GROUP * HD)
                        last = V.tensor_tensor(
                            yn[:, a_].rearrange("p (c o d) -> p o c d", o=2, c=2),
                            att_ps[:, a_].rearrange("p (o c d) -> p o c d", o=2, c=2),
                            soft[:, g, 5].rearrange("p (o c) -> p o c", o=2).unsqueeze(3).broadcast_to([P, 2, 2, HD]),
                            ALU.mult)
                    link(last)
                    dve.sem_inc(att_free, 1)
                    dve.sem_inc(att_ready, 1)
                    mean_square(mix_squared, mix_ms, b + 1, st[:, 10:12], st[:, 2:4], 2, SGU_W)
                elif stage == "F1":
                    mean_square(x1_squared, x1_ms, b + 1, st[:, 9:10], st[:, 8:9], 1, D)
                elif stage == "F2":
                    scale_shift(("ffn", b, 0), lambda k: h2T[:, b // 2, k, (b % 2) * P:(b % 2 + 1) * P],
                                lambda k: mod[:, 3 * KD + k:3 * KD + k + 1],
                                lambda k: mod[:, 2 * KD + k:2 * KD + k + 1], h2T_dve)
                elif stage == "TK":
                    top_dense(b)
                if (stage, b) == ("F2", NB - 1):
                    dve.sem_inc(mixer_dve, 1)
                    dve.wait_ge(mixer_pe, 1)
                    dve.wait_ge(mixer_act, 1)
                    V.tensor_copy(c_rows2, c_act[:].unsqueeze(2).broadcast_to([P, KD, P])).then_inc(c_rows_ready, 1)


            def first_key_rows(n, side, quarter, t0, share):
                dve.wait_ge(gate_full, n + 1)
                V.tensor_copy(key_now[:, side], chosen[:, bass.ds(t0 + DT, BATCH)]).then_inc(key_now_ready, 1)
                V.tensor_tensor(first_hot, iota[:, quarter * QT:(quarter + 1) * QT].unsqueeze(1)
                                .broadcast_to([P, BATCH, QT]),
                                chosen[:, bass.ds(t0, BATCH)].unsqueeze(2).broadcast_to([P, BATCH, QT]),
                                ALU.is_equal)
                dve.drain()
                V.tensor_tensor(hot_i[:, side], first_hot.unsqueeze(1).broadcast_to([P, 3, BATCH, QT]),
                                gate_parts[:, :, bass.ds(t0, BATCH)].unsqueeze(3)
                                .broadcast_to([P, 3, BATCH, QT]), ALU.mult)
                if share < BATCH:
                    V.tensor_tensor(hot_j[:, side, share:], iota[:].unsqueeze(1).broadcast_to([P, BATCH - share, P]),
                                    key_now[:, side, share:].unsqueeze(2).broadcast_to([P, BATCH - share, P]),
                                    ALU.is_equal)
                dve.drain().then_inc(hot_i_ready, 1)

            def gate_step(q, i, t):
                if q < QUARTERS - 1:
                    first_key_rows(i * TILES_UNIT + (t + (q + 1) * BATCHES), t % 2, q + 1,
                                   i * (TILES_UNIT * BATCH) + t * BATCH, BATCH)

            def dot_products(unit, b, part):
                for r in range(RING):
                    dve.wait_ge(down_in[r], unit * (16 * PARTS) + 16 * (part + 1))
                    dve.wait_ge(down_free, unit * TOPK + (part + 1) * RING + r - 1)
                    V.tensor_tensor_reduce(out=dot_junk[:, r % 2], in0=down_ring[:, r], in1=h2[:, b],
                                           scale=1.0, scalar=0.0, op0=ALU.mult, op1=ALU.add,
                                           accum_out=dots[:, part, r:r + 1]).then_inc(down_free, 1)

            def weighted_rows(unit, part):
                dve.wait_ge(gelu_ready, unit * PARTS + part + 1)
                V.tensor_tensor(coef[:, part], gelus[:, part],
                                gates[:, bass.ds(unit * TOPK + part * RING, RING)], ALU.mult)
                dve.drain()
                for r in range(RING):
                    dve.wait_ge(up_in[r], unit * (16 * PARTS) + 16 * (part + 1))
                    dve.wait_ge(up_free, unit * TOPK + (part + 1) * RING + r)
                    V.scalar_tensor_tensor(acc[:, 0], up_ring[:, r], coef[:, part, r:r + 1], acc[:, 0],
                                           ALU.mult, ALU.add).then_inc(up_free, 1)

            def tile_weights(q, i, t):
                dve.wait_ge(tile_gelu, i * TILES_UNIT + (q * QT + t + 1))
                V.tensor_tensor(weights[:, t % TRING], weights[:, t % TRING],
                                gate_mat[:, :, bass.ds(i * TILES_UNIT + (q % 2 * QT + t), 1)].rearrange("p t o -> p (t o)"),
                                ALU.mult).then_inc(weights_ready, 1)

            def experts(q, i, more):
                unit = i + q * QUNITS
                for part in range(PARTS):
                    gate_step(q, i, 2 * part)
                    tile_weights(q, i, 2 * part)
                    dot_products(unit, q // 2, part)
                    gate_step(q, i, 2 * part + 1)
                    if more and part == 1:
                        V.tensor_copy(key_s.rearrange("p a n -> p (a n)"),
                                      scores[:, bass.ds((unit + 1) * (2 * P), 2 * P)])
                        dve.drain()
                        top_keys([key_s[:, p] for p in range(2)])
                    if more and part == 2:
                        top_sums(best_v, True)
                    if more and part == 3:
                        chosen_keys(sel[:])
                        expert_numbers(unit + 1)
                    tile_weights(q, i, 2 * part + 1)
                    weighted_rows(unit, part)
                if more:
                    gate_values(unit + 1)

            with dve.Fori(0, BATCHES // 4, 1) as i:
                for m in range(4):
                    first_key_rows(i * 4 + m, m % 2, 0, i * (4 * BATCH) + m * BATCH, SHARE)
            dve.wait_ge(gain2_in, 32)
            ada_row(GT2, gain2, acc[:, 0])
            link(V.memset(zeros, 0.0))
            dve.sem_inc(zeros_ready, 1)
            for b in range(GATHER_B):
                link(V.memset(acc[:, 0], 0.0))
                dve.wait_ge(h2_ready, b + 1)
                for q in (2 * b, 2 * b + 1):
                    dve.wait_ge(gate_stored, 2 + (q + 1) * BATCHES)
                    with dve.Fori(0, QUNITS - q % 2, 1) as i:
                        experts(q, i, True)
                experts(q, QUNITS - 1, b < GATHER_B - 1)
                dve.drain().then_inc(y2_ready, 1)
                dve.wait_ge(y2_rms, b + 1)
                link(V.reciprocal(fin[:, 2:3], fin[:, 1:2]))
                link(V.scalar_tensor_tensor(acc[:, 0], acc[:, 0], fin[:, 2:3], gain2, ALU.mult, ALU.mult))
                dve.wait_ge(x1_back, 16 * (b + 1))
                V.tensor_tensor(acc[:, 1], acc[:, 1], acc[:, 0], ALU.add).then_inc(out_ready, 1)
                dve.wait_ge(out_ready, b + 1)
            dve.wait_ge(dense_squared, 1)
            s4 = soft_d[:, 0, 0:4].rearrange("p (b h) -> p b h", b=DENSE_B)
            V.tensor_tensor(soft_d[:, 0, 4:6], s4[:, :, 0], s4[:, :, 1], ALU.add).then_inc(dense_squared, 1)
            dve.wait_ge(dense_rms, 1)
            link(V.reciprocal(soft_d[:, 0, 8:10], soft_d[:, 0, 6:8]))
            dve.wait_ge(x1_dense_in, 16 * DENSE_B)
            for b in range(DENSE_B):
                for half in range(2):
                    c_ = slice(half * 512, (half + 1) * 512)
                    last = V.scalar_tensor_tensor(down_ring[:, b, c_], y_bank[b][half],
                                                  soft_d[:, 0, 8 + b:9 + b], gain2[:, c_], ALU.mult, ALU.mult)
                link(last)
                V.tensor_tensor(x1_dense[:, b], x1_dense[:, b], down_ring[:, b], ALU.add).then_inc(dense_out, 1)

        @block.tensor
        def _(pe):
            T = nc.tensor
            chunks = [0]
            n_actT = [0]

            def fill(uses, free, key):
                bank, turn = uses[key]
                if turn:
                    pe.wait_ge(free[bank], turn)
                return bank

            def chunk():
                n = chunks[0]
                chunks[0] += 1
                pe.wait_ge(chunk_in[n % WRING], 16 * (n // WRING + 1))
                return wring[:, n % WRING]

            def transpose4(key, source):
                bank = fill(TR, tr_free, key)
                for j in range(4):
                    last = T.transpose(tr[:, bank, j * P:(j + 1) * P], source(j), ident[:])
                last.then_inc(tr_full[bank], 1)

            def actT_in():
                n_actT[0] += 1
                pe.wait_ge(actT_dve, n_actT[0])
                pe.wait_ge(actT_act, n_actT[0])

            def query(group):
                half, g = group // 4, group % 4
                if g == 0:
                    pe.wait_ge(h2T_dve, DENSE_B if half == 0 else NB)
                    pe.wait_ge(h2T_act, DENSE_B if half == 0 else NB)
                    pe.wait_ge(keys_in, 16)
                for j in range(4):
                    key = ("query", 4 * group + j)
                    bank = fill(MM, mm_free, key)
                    w = chunk()
                    for k in range(KD):
                        last = T.matmul(mm[:, bank, 0:2 * P], w[:, k], h2T[:, half, k], start=(k == 0), stop=(k == KD - 1))
                    last.then_inc(mm_full[bank], 1)
                pe.wait_ge(qhT_ready, group + 1)
                for tb in range(2):
                    bank = fill(MM, mm_free, ("score", group, tb))
                    for j in range(4):
                        last = T.matmul(mm[:, bank, j * P:(j + 1) * P], qhT[:, group % 2, j, tb * P:(tb + 1) * P],
                                        keys_sb[:, 4 * g + j], start=True, stop=True)
                    last.then_inc(mm_full[bank], 1)

            def modulation(v, m, left):
                bank, turn = MM["ada", v, m // 4]
                if m % 4 == 0:
                    fill(MM, mm_free, ("ada", v, m // 4))
                w = chunk()
                for k in range(KD):
                    last = T.matmul(mm[:, bank, m % 4 * P:(m % 4 + 1) * P], left[:, k], w[:, k],
                                    start=(k == 0), stop=(k == KD - 1))
                last.then_inc(chunk_used if m % 4 < 3 else mm_full[bank], 1)

            def turn_to_experts():
                for b in range(DENSE_B, NB):
                    for part in range(2):
                        transpose4(("h2", b, part), lambda j: h2T[:, 1, 4 * part + j, (b % 2) * P:(b % 2 + 1) * P])
                bank, turn = TR["h2", NB - 1, 1]
                pe.wait_ge(tr_full[bank], turn + 1)
                pe.sem_inc(h2T_used, 1)
                pe.wait_ge(chosen_ready, 1)
                transpose4(("onehot", 0), lambda j: chosen[:, j * P:(j + 1) * P])
                bank = fill(TR, tr_free, ("onehot", 1))
                for j in range(2):
                    last = T.transpose(tr[:, bank, j * P:(j + 1) * P], gates_d[:, j * P:(j + 1) * P], ident[:])
                last.then_inc(tr_full[bank], 1)

            pe.wait_ge(consts_in, 16 * N_CONSTS)
            for stage, b in steps():
                if stage == "ADA_ROW" and b == GT2:
                    continue
                if stage in ("ADA_COL", "ADA_ROW"):
                    pe.wait_ge(c_rows_ready, 1)
                    for m in range(KD):
                        modulation(b, m, c_rows)
                elif stage == "T":
                    pe.wait_ge(xn_ready, b + 1)
                    for half in range(2):
                        transpose4(("x", b, half), lambda j: xn[:, (4 * half + j) * P:(4 * half + j + 1) * P])
                elif stage == "P":
                    actT_in()
                    for c, (first, n) in enumerate(PROJ):
                        if b == 0:
                            pe.wait_ge(win_in[c], 16)
                        bank = fill(MM, mm_free, ("proj", b, c))
                        for k in range(KD):
                            last = T.matmul(mm[:, bank, 0:n], actT[:, k], win_sb[:, k, first:first + n],
                                            start=(k == 0), stop=(k == KD - 1))
                        last.then_inc(mm_full[bank], 1)
                elif stage == "S1":
                    pe.wait_ge(rope_ready, b + 1)
                    transpose4(("q", b), lambda j: q_rot[:, j * P:(j + 1) * P])
                    bank = fill(TR, tr_free, ("k", b))
                    for g in range(KVH):
                        last = T.transpose(tr[:, bank, g * P:(g + 1) * P],
                                           k_dup[:, g].rearrange("p r d -> p (r d)"), ident[:])
                    last.then_inc(tr_full[bank], 1)
                elif stage == "S2":
                    pe.wait_ge(qT_ready, b + 1)
                    pe.wait_ge(kT_ready, b + 1)
                    first = max(b - 1, 0)
                    off = 0 if b else P
                    for g in range(KVH):
                        if 2 * b + g:
                            pe.wait_ge(sc_free, 2 * b + g)
                        for h in range(GROUP):
                            head = g * GROUP + h
                            rows_ = slice(HD * (head % 2), HD * (head % 2) + HD)
                            last = T.matmul(sc[:, h % 2, (h // 2) * 2 * P + off:(h // 2 + 1) * 2 * P],
                                            qT[rows_, head // 2], kT[rows_, g, first * P:(b + 1) * P],
                                            start=True, stop=True)
                        last.then_inc(sc_full, 1)
                elif stage == "G":
                    pe.wait_ge(vn_ready, b + 1)
                    if b == 0:
                        pe.wait_ge(wsT_ready, 1)
                    else:
                        pe.wait_ge(sgu_free, b)
                    for h in range(SGU_H):
                        last = T.matmul(sgu_ps[:, h * HD:(h + 1) * HD], wsT[:, h], vn[:, h * HD:(h + 1) * HD],
                                        start=True, stop=True)
                    last.then_inc(sgu_full, 1)
                elif stage == "W":
                    pe.wait_ge(mix_ready, b + 1)
                    for half in range(2):
                        transpose4(("mix", b, half), lambda j: yn[:, (4 * half + j) * P:(4 * half + j + 1) * P])
                    actT_in()
                    pe.wait_ge(wout_in, 16)
                    for half in range(2):
                        bank = fill(MM, mm_free, ("y", b, half))
                        for k in range(KD):
                            last = T.matmul(mm[:, bank, :], actT[:, k], wout_sb[:, k, half * 512:(half + 1) * 512],
                                            start=(k == 0), stop=(k == KD - 1))
                        last.then_inc(mm_full[bank], 1)
                elif stage == "O":
                    for g in range(KVH):
                        pe.wait_ge(exp_ready, 2 * b + g + 1)
                        for j in range(2):
                            transpose4(("prob", b, g, j),
                                       lambda h: probs[g][:, (2 * h + j) * P:(2 * h + j + 1) * P])
                        pe.wait_ge(pT_act, 2 * b + g + 1)
                        pe.wait_ge(pT_dve, 2 * b + g + 1)
                        if g == 0 and b:
                            pe.wait_ge(att_free, b)
                        for h in range(GROUP):
                            head = g * GROUP + h
                            for j in range(2):
                                last = T.matmul(att_ps[:, head * HD:(head + 1) * HD], pT[:, j, h],
                                                v_all[:, max(b - 1 + j, 0), g * HD:(g + 1) * HD],
                                                start=(j == 0), stop=(j == 1))
                    last.then_inc(att_full, 1)
                elif stage == "F2":
                    pe.wait_ge(xn2_ready, b + 1)
                    for half in range(2):
                        transpose4(("ffn", b, half), lambda j: xn2[:, (4 * half + j) * P:(4 * half + j + 1) * P])
                elif stage == "Q":
                    query(b)
                elif stage == "TURN":
                    turn_to_experts()
                if (stage, b) == ("F2", NB - 1):
                    bank, turn = TR["ffn", NB - 1, 1]
                    pe.wait_ge(tr_full[bank], turn + 1)
                    pe.sem_inc(mixer_pe, 1)

            def gate_products(n, side):
                pe.wait_ge(hot_i_ready, n + 1)
                pe.wait_ge(hot_j_ready, n + 2)
                pe.wait_ge(gate_stored, n + 1)
                for t in range(BATCH):
                    for part in range(3):
                        last = T.matmul(tr[:, side, t * QT:(t + 1) * QT], hot_j[:, side, t], hot_i[:, side, part, t],
                                        start=(part == 0), stop=(part == 2))
                last.then_inc(gate_full, 1)

            def tile_products(slot, arrived, bank):
                pe.wait_ge(tile_down_in[slot], arrived)
                for k in range(KD):
                    last = T.matmul(mm[:, bank, 0:DT], tile_down[slot][:, k], h2T[:, 0, k],
                                    start=(k == 0), stop=(k == KD - 1))
                last.then_inc(act_full, 1)

            def tile_sums(unit, t):
                slot = t % TRING
                pe.wait_ge(weights_ready, unit * TILES_UNIT + t + 1)
                pe.wait_ge(tile_up_in[slot], unit * (16 * TILES_UNIT // TRING) + 16 * (t // TRING + 1))
                for b in range(DENSE_B):
                    for half in range(2):
                        last = T.matmul(y_bank[b][half], weights[:, slot, b * P:(b + 1) * P],
                                        tile_up[slot][:, half * 512:(half + 1) * 512], start=False, stop=False,
                                        skip_group_check=True)
                last.then_inc(tile_done, 1)

            def experts(q, i, ahead):
                unit = i + q * QUNITS
                for t in range(TILES_UNIT):
                    if t < ahead:
                        pe.wait_ge(tile_gelu, unit * TILES_UNIT + t + 1)
                        nxt = t + 2
                        tile_products(nxt % TRING,
                                      unit * (16 * TILES_UNIT // TRING) + 16 * (nxt // TRING + 1), t % 2)
                    if q < QUARTERS - 1:
                        gate_products(i * TILES_UNIT + (t + (q + 1) * BATCHES), t % 2)
                    tile_sums(unit, t)

            pe.sem_inc(act_full, TRING)
            pe.sem_inc(tile_done, TRING)
            pe.wait_ge(sc_free, KVH * NB)
            pe.wait_ge(att_free, NB)
            pe.wait_ge(sgu_free, NB)
            pe.sem_inc(gate_full, 2)
            pe.sem_inc(gate_stored, 2)
            pe.wait_ge(c_rows_ready, 2)
            for piece in range(GT2_PIECES):
                for m in range(piece * KD // GT2_PIECES, (piece + 1) * KD // GT2_PIECES):
                    modulation(GT2, m, c_rows2)
                if piece == 0:
                    for n in range(2):
                        bank, turn = TR["onehot", n]
                        pe.wait_ge(tr_free[bank], turn + 1)
                with pe.Fori(0, BATCHES // 4 // GT2_PIECES, 1) as i:
                    for m in range(4):
                        gate_products(i * 4 + (m + piece * BATCHES // GT2_PIECES), m % 2)
            for bank in range(2):
                pe.wait_ge(mm_free[bank], len([1 for b_, _ in MM.values() if b_ == bank]))
            pe.wait_ge(zeros_ready, 1)
            for b in range(DENSE_B):
                for half in range(2):
                    T.matmul(y_bank[b][half], zeros, h2T[:, 0, 0:2].rearrange("p k n -> p (k n)"),
                             start=True, stop=False, skip_group_check=True)
            for n in range(2):
                tile_products(n, 16, n)
            for b in range(GATHER_B):
                for q in (2 * b, 2 * b + 1):
                    with pe.Fori(0, QUNITS - q % 2, 1) as i:
                        experts(q, i, TILES_UNIT)
                experts(q, QUNITS - 1, TILES_UNIT if b < GATHER_B - 1 else TILES_UNIT - 2)


def kernel(x, c, w_ada, b_ada, g_pre_mix, g_post_mix, g_pre_ffn, g_post_ffn, w_in, w_s, b_s, sgu_ln_g,
           sgu_ln_b, sinks, g_att_out, g_sgu_out, w_out, w_query, sub_keys, expert_down, expert_up):
    import concourse.bacc as bacc
    from concourse.bass_utils import run_bass_kernel_spmd

    f = lambda a: np.ascontiguousarray(np.asarray(a))

    def columns(v):
        return f(v).reshape(-1, P).T

    def chunks(w):
        w = f(w)
        return np.ascontiguousarray(w.reshape(KD, P, -1, P).transpose(2, 1, 0, 3))

    half = HD // 2
    inv = np.float32(10000.0) ** (-np.arange(half, dtype=np.float32) / np.float32(half))
    ang = np.arange(SEQ, dtype=np.float32)[:, None] * inv[None, :]
    cos, sin = np.cos(ang), np.sin(ang)
    by_block = lambda t: np.ascontiguousarray(t.reshape(NB, P, HD).transpose(1, 0, 2), dtype=np.float32)
    q, s = np.arange(P)[:, None], np.arange(P)[None, :]
    masks = np.concatenate([
        (q <= s).astype(np.float32),
        np.where(s > q, 0.0, MASKED).astype(np.float32),
        np.where(s <= q, 0.0, MASKED).astype(np.float32),
    ], axis=1)

    mod_rows = f(b_ada)[0].reshape(6, D)
    arrays = {
        "x": f(x)[0],
        "cols": np.ascontiguousarray(np.concatenate([
            columns(f(c)[0]), columns(f(b_ada)[0]), columns(f(g_pre_mix)[0]), columns(f(g_pre_ffn)[0]),
            columns(f(g_att_out)[0]), columns(f(g_sgu_out)[0])], axis=1)),
        "rows": np.concatenate([mod_rows[GT1], f(g_post_mix)[0], mod_rows[GT2], f(g_post_ffn)[0],
                                f(sgu_ln_g)[0].reshape(-1), f(sgu_ln_b)[0].reshape(-1)]),
        "w_ada": chunks(f(w_ada)[0]),
        "w_in": f(w_in)[0],
        "w_s": np.ascontiguousarray(f(w_s)[0].transpose(2, 0, 1)),
        "b_s": np.ascontiguousarray(f(b_s)[0].T),
        "sinks": np.ascontiguousarray(f(sinks)[0].reshape(KVH, 2, 2).transpose(0, 2, 1).reshape(-1)),
        "w_out": f(w_out)[0],
        "w_query": chunks(f(w_query)[0]),
        "keys": np.ascontiguousarray(f(sub_keys)[0].reshape(HP, NKEY, P).transpose(2, 0, 1)),
        "down": f(expert_down)[0],
        "up": f(expert_up)[0],
        "down_tiles": np.ascontiguousarray(f(expert_down)[0].reshape(TILES, P, KD, P).transpose(0, 3, 2, 1)),
        "cos_tab": by_block(np.concatenate([cos, cos], axis=1)),
        "sin_tab": by_block(np.concatenate([-sin, sin], axis=1)),
        "masks": masks,
        "ident_in": np.eye(P, dtype=np.float32),
        "iota_in": np.ascontiguousarray(np.broadcast_to(np.arange(P, dtype=np.float32), (P, P))),
    }
    nc = bacc.Bacc("TRN2", target_bir_lowering=False, num_devices=1)
    aps = [nc.dram_tensor(f"in_{n}", a.shape, mybir.dt.from_np(a.dtype), kind="ExternalInput").ap()
           for n, a in arrays.items()]
    out = nc.dram_tensor("out_0", (SEQ, D), F32, kind="ExternalOutput").ap()
    hybrid_block(nc, *aps, out)
    r = run_bass_kernel_spmd(nc, [{f"in_{n}": a for n, a in arrays.items()}], core_ids=[0])
    return r.results[0]["out_0"].reshape(1, SEQ, D)
```
